# Optimizing a Trainium2 kernel written in Bass

```python
import math
import jax, jax.numpy as jnp
from jax import lax
import numpy as np

D_MODEL = 1024
BATCH = 1
SEQ = 256
DEPTH = 2
DEC_BATCH = 8
DEC_SEQ = 8
PAST_LEN = 1024
PAGE_SIZE = 128

N_EVEN = (DEPTH + 1) // 2
N_ODD = DEPTH // 2

D_A = D_MODEL // 2
DH_A = 64
H_A = D_A // DH_A
R_DECAY = 64
R_ICLR = 64
R_GATE = 128
A_PROJ = 3 * D_A + R_DECAY + R_ICLR + R_GATE
GN_EPS = 64e-5
D_B = D_MODEL // 2
H_B = 4
C_B = D_B // H_B
CHUNK = 128
D_C = D_MODEL // 2
H_C = 8
DH_C = D_C // H_C
CONV_W = 4
LRU_C = 8.0
D_D = D_MODEL // 2
H_D = 8
DH_D = D_D // H_D
DILATED = ((128, 1), (512, 4), (2048, 16))
WINDOW_MAX = 2048
ATT_BLOCK = 128
N_BUCKETS = 32
BUCKET_MAX_DIST = WINDOW_MAX
NEG_BIG = -1e30
N_GROUPS = 4
EXP_PER_GROUP = 4
N_EXPERTS = N_GROUPS * EXP_PER_GROUP
TOP_K_INNER = 2
D_EXPERT = 512
NORM_EPS = 1e-6

kernel_name = 'hybrid_rwkv7_gmlp_rglru_dilated_hmoe_step'

def rmsnorm(x, g):
    xf = x.astype(jnp.float32)
    y = xf * lax.rsqrt(jnp.mean(xf * xf, -1, keepdims=True) + NORM_EPS)
    return (y * g.astype(jnp.float32)).astype(x.dtype)

def t5_bucket(dist):
    dist = np.asarray(dist)
    max_exact = N_BUCKETS // 2
    scaled = np.log(np.maximum(dist, 1) / max_exact) / math.log(BUCKET_MAX_DIST / max_exact)
    large = np.minimum(max_exact + (scaled * (N_BUCKETS - max_exact)).astype(np.int32), N_BUCKETS - 1)
    return np.where(dist < max_exact, dist, large).astype(np.int32)

def rwkv7_mix(p, p_prev, wkv0, shift_mu, decay_w0, decay_up, iclr_a0, iclr_up, gate_up,
              key_k, key_a, bonus_r_k, lnx_g, lnx_b):
    B, L, _ = p.shape
    f32 = jnp.float32
    shifted = jnp.concatenate([p_prev[:, None], p[:, :-1]], axis=1)
    xs = p + (shifted - p) * shift_mu
    r, k, v, wd, ad, gd = jnp.split(
        xs, [D_A, 2 * D_A, 3 * D_A, 3 * D_A + R_DECAY, 3 * D_A + R_DECAY + R_ICLR], axis=-1)
    w_log = -jax.nn.softplus(-(decay_w0 + jnp.tanh(wd) @ decay_up).astype(f32)) - 0.5
    decay = jnp.exp(-jnp.exp(w_log))
    a = jax.nn.sigmoid((iclr_a0 + ad @ iclr_up).astype(f32))
    g = (jax.nn.sigmoid(gd) @ gate_up).astype(f32)

    def heads(t):
        return t.reshape(B, L, H_A, DH_A)

    kk = heads(k.astype(f32) * key_k)
    kk = kk / jnp.maximum(jnp.sqrt(jnp.sum(kk * kk, -1, keepdims=True)), 1e-12)
    k = k.astype(f32) * (1.0 + (a - 1.0) * key_a)
    rh, kh, vh, wh, ah = heads(r.astype(f32)), heads(k), heads(v.astype(f32)), heads(decay), heads(a)

    def step(s, inp):
        r_t, w_t, k_t, v_t, kk_t, kka_t = inp
        sa = jnp.einsum('bhvk,bhk->bhv', s, -kk_t)
        s = s * w_t[:, :, None, :] + sa[..., None] * kka_t[:, :, None, :] + v_t[..., None] * k_t[:, :, None, :]
        return s, jnp.einsum('bhvk,bhk->bhv', s, r_t)

    seq = tuple(jnp.moveaxis(t, 1, 0) for t in (rh, wh, kh, vh, kk, kk * ah))
    s_fin, y = lax.scan(step, wkv0.astype(f32), seq)
    y = jnp.moveaxis(y, 0, 1)
    mu = jnp.mean(y, -1, keepdims=True)
    var = jnp.mean(jnp.square(y - mu), -1, keepdims=True)
    y = ((y - mu) * lax.rsqrt(var + GN_EPS)).reshape(B, L, D_A) * lnx_g + lnx_b
    bonus = jnp.sum(rh * kh * bonus_r_k, -1, keepdims=True) * vh
    y = (y + bonus.reshape(B, L, D_A)) * g
    return y.astype(p.dtype), p[:, -1], s_fin.astype(wkv0.dtype)

def chunk_gmlp(u, v, chunk, sgu_norm_g, sgu_norm_b, sgu_w, sgu_b):
    B, L, _ = u.shape
    vf = v.astype(jnp.float32)
    mu = jnp.mean(vf, -1, keepdims=True)
    var = jnp.mean(jnp.square(vf - mu), -1, keepdims=True)
    vn = (vf - mu) * lax.rsqrt(var + NORM_EPS) * sgu_norm_g + sgu_norm_b
    wm = sgu_w[:, :chunk, :chunk] * np.tril(np.ones((chunk, chunk), np.float32))
    vc = vn.reshape(B, L // chunk, chunk, H_B, C_B)
    s = jnp.einsum('hts,bnshc->bnthc', wm, vc) + jnp.transpose(sgu_b[:, :chunk])[None, None, :, :, None]
    out = u.astype(jnp.float32) * s.reshape(B, L, D_B)
    return out.astype(u.dtype), vn.astype(u.dtype)

def even_mixer(h, shift_prev, wkv0, chunk, w_in, w_out, shift_mu, decay_w0, decay_up, iclr_a0, iclr_up,
               gate_up, key_k, key_a, bonus_r_k, lnx_g, lnx_b, sgu_norm_g, sgu_norm_b, sgu_w, sgu_b):
    proj = h @ w_in
    pa, pu, pv = jnp.split(proj, [A_PROJ, A_PROJ + D_B], axis=-1)
    ya, last, wkv = rwkv7_mix(pa, shift_prev, wkv0, shift_mu, decay_w0, decay_up, iclr_a0, iclr_up, gate_up,
                              key_k, key_a, bonus_r_k, lnx_g, lnx_b)
    yb, vn = chunk_gmlp(jax.nn.gelu(pu), jax.nn.gelu(pv), chunk, sgu_norm_g, sgu_norm_b, sgu_w, sgu_b)
    y = jnp.concatenate([ya, yb], axis=-1) @ w_out
    return y, last, wkv, vn

def rglru(xb, conv_prev, h0, pos, conv_w, conv_b, rgate_w, rgate_b, igate_w, igate_b, lru_lambda):
    B, L, _ = xb.shape
    f32 = jnp.float32
    xe = jnp.concatenate([conv_prev, xb], axis=1)
    xc = conv_b + xe[:, 0:L] * conv_w[0]
    for i in range(1, CONV_W):
        xc = xc + xe[:, i:i + L] * conv_w[i]
    xh = xc.reshape(B, L, H_C, DH_C)
    r = jax.nn.sigmoid((jnp.einsum('blhi,hij->blhj', xh, rgate_w).reshape(B, L, D_C) + rgate_b).astype(f32))
    ig = jax.nn.sigmoid((jnp.einsum('blhi,hij->blhj', xh, igate_w).reshape(B, L, D_C) + igate_b).astype(f32))
    log_a = -LRU_C * r * jax.nn.softplus(-lru_lambda.astype(f32))
    a = jnp.exp(log_a)
    mult = jnp.sqrt(-jnp.expm1(2.0 * log_a))
    mult = jnp.where((pos == 0)[None, :, None], 1.0, mult)
    b = mult * ig * xc.astype(f32)
    b = b.at[:, 0].add(a[:, 0] * h0.astype(f32))

    def comb(e1, e2):
        a1, b1 = e1
        a2, b2 = e2
        return a1 * a2, a2 * b1 + b2

    _, hs = lax.associative_scan(comb, (a, b), axis=1)
    return hs, xe[:, -(CONV_W - 1):], hs[:, -1]

def dilated_attn_prompt(q, k, v, rel_bias):
    B, L, H, E = q.shape
    outs, lses = [], []
    for window, dil in DILATED:
        nk = window // dil
        ls = L // dil
        nblk = -(-ls // ATT_BLOCK)
        lp = nblk * ATT_BLOCK

        def split(t):
            t = t.reshape(B, ls, dil, H, E).transpose(0, 2, 1, 3, 4)
            t = jnp.pad(t, ((0, 0), (0, 0), (0, lp - ls), (0, 0), (0, 0)))
            return t.reshape(B, dil, nblk, ATT_BLOCK, H, E)

        def band(t):
            prev = jnp.pad(t[:, :, :-1], ((0, 0), (0, 0), (1, 0), (0, 0), (0, 0), (0, 0)))
            return jnp.concatenate([prev, t], axis=3)

        qb = split(q)
        kw, vw = band(split(k)), band(split(v))
        s = jnp.einsum('bcnqhe,bcnshe->bcnhqs', qb, kw, preferred_element_type=jnp.float32) * (E ** -0.5)
        qi = np.arange(ATT_BLOCK)[:, None]
        si = np.arange(2 * ATT_BLOCK)[None, :]
        delta = qi + ATT_BLOCK - si
        key_sub = np.arange(nblk)[:, None, None] * ATT_BLOCK + si[None] - ATT_BLOCK
        valid = (delta >= 0) & (delta <= nk) & (key_sub >= 0)
        bias = rel_bias[t5_bucket(np.clip(delta, 0, nk) * dil)]
        s = s + jnp.transpose(bias, (2, 0, 1)).astype(jnp.float32)
        s = jnp.where(valid[:, None], s, NEG_BIG)
        m = jnp.max(s, -1, keepdims=True)
        p = jnp.exp(s - m)
        den = jnp.sum(p, -1, keepdims=True)
        o = jnp.einsum('bcnhqs,bcnshe->bcnqhe', p / den, vw.astype(jnp.float32))
        lse = (m + jnp.log(den))[..., 0]
        o = o.reshape(B, dil, lp, H, E)[:, :, :ls].transpose(0, 2, 1, 3, 4).reshape(B, L, H, E)
        lse = lse.transpose(0, 1, 2, 4, 3).reshape(B, dil, lp, H)[:, :, :ls].transpose(0, 2, 1, 3).reshape(B, L, H)
        outs.append(o)
        lses.append(lse)
    alpha = jax.nn.softmax(jnp.stack(lses), axis=0)
    return jnp.einsum('pblh,pblhe->blhe', alpha, jnp.stack(outs))

def dilated_attn_sample(q, k_all, v_all, rel_bias):
    B, S, H, E = q.shape
    W = k_all.shape[1] - S
    outs, lses = [], []
    for window, dil in DILATED:
        nk = window // dil
        m_idx = np.arange(nk + 1)
        idx = W + np.arange(S)[:, None] - m_idx[None] * dil
        valid = idx >= 0
        idx = np.maximum(idx, 0)
        kg, vg = k_all[:, idx], v_all[:, idx]
        s = jnp.einsum('bjhe,bjmhe->bhjm', q, kg, preferred_element_type=jnp.float32) * (E ** -0.5)
        bias = rel_bias[t5_bucket(m_idx * dil)]
        s = s + jnp.transpose(bias)[:, None, :].astype(jnp.float32)
        s = jnp.where(valid[None, None], s, NEG_BIG)
        m = jnp.max(s, -1, keepdims=True)
        p = jnp.exp(s - m)
        den = jnp.sum(p, -1, keepdims=True)
        outs.append(jnp.einsum('bhjm,bjmhe->bjhe', p / den, vg.astype(jnp.float32)))
        lses.append(jnp.transpose((m + jnp.log(den))[..., 0], (0, 2, 1)))
    alpha = jax.nn.softmax(jnp.stack(lses), axis=0)
    return jnp.einsum('pblh,pblhe->blhe', alpha, jnp.stack(outs))

def odd_mixer(h, conv_prev, h0, pos, k_past, v_past, w_in, w_out, conv_w, conv_b, rgate_w, rgate_b,
              igate_w, igate_b, lru_lambda, rel_bias):
    B, L, _ = h.shape
    proj = h @ w_in
    gy, xb, q, k, v = jnp.split(proj, [D_C, 2 * D_C, 2 * D_C + D_D, 2 * D_C + 2 * D_D], axis=-1)
    hc, conv_last, h_last = rglru(xb, conv_prev, h0, pos, conv_w, conv_b, rgate_w, rgate_b,
                                  igate_w, igate_b, lru_lambda)
    yc = jax.nn.gelu(gy.astype(jnp.float32)) * hc
    q = q.reshape(B, L, H_D, DH_D)
    k = k.reshape(B, L, H_D, DH_D)
    v = v.reshape(B, L, H_D, DH_D)
    if k_past is None:
        o = dilated_attn_prompt(q, k, v, rel_bias)
        keep = min(WINDOW_MAX, L)
        k_rows, v_rows = k[:, L - keep:], v[:, L - keep:]
    else:
        o = dilated_attn_sample(q, jnp.concatenate([k_past, k], axis=1), jnp.concatenate([v_past, v], axis=1), rel_bias)
        k_rows, v_rows = k, v
    y = jnp.concatenate([yc, o.reshape(B, L, D_D)], axis=-1).astype(h.dtype) @ w_out
    return y, conv_last, h_last.astype(h.dtype), k_rows, v_rows

def hier_moe(x, router_group_w, router_group_b, router_expert_w, router_expert_b, exp_w_gate, exp_w_up, exp_w_down):
    B, L, D = x.shape
    f32 = jnp.float32
    t = x.reshape(B * L, D)
    pg = jax.nn.softmax((t @ router_group_w + router_group_b).astype(f32), axis=-1)
    top_pg, grp = lax.top_k(pg, 1)
    le = (t @ router_expert_w + router_expert_b).astype(f32).reshape(-1, N_GROUPS, EXP_PER_GROUP)
    le = jnp.take_along_axis(le, grp[:, :, None], axis=1)[:, 0]
    top_le, ei = lax.top_k(le, TOP_K_INNER)
    w2 = jax.nn.softmax(top_le, axis=-1) * top_pg
    eid = grp * EXP_PER_GROUP + ei
    gates = jnp.einsum('tk,tke->te', w2, jax.nn.one_hot(eid, N_EXPERTS, dtype=f32))
    hg = jnp.einsum('td,edf->tef', t, exp_w_gate)
    hu = jnp.einsum('td,edf->tef', t, exp_w_up)
    hid = jax.nn.silu(hg) * hu * gates[..., None].astype(hg.dtype)
    return jnp.einsum('tef,efd->td', hid, exp_w_down).reshape(B, L, D).astype(x.dtype)

def setup_inputs(seed: int = 0) -> dict:
    key = jax.random.key(seed)
    ks = iter(jax.random.split(key, 64))
    f32 = jnp.float32

    def normal(shape, scale):
        return scale * jax.random.normal(next(ks), shape, f32)

    def uniform(shape, lo, hi):
        return jax.random.uniform(next(ks), shape, f32, lo, hi)

    w_buf = min(WINDOW_MAX, PAST_LEN)
    d = D_MODEL
    inp = {}
    inp['x_prompt'] = normal((BATCH, SEQ, d), 1.0)
    inp['x_sample'] = normal((DEC_BATCH, DEC_SEQ, d), 1.0)
    inp['state_wkv'] = normal((N_EVEN, DEC_BATCH, H_A, DH_A, DH_A), 0.3)
    inp['state_shift'] = normal((N_EVEN, DEC_BATCH, A_PROJ), 1.0)
    inp['state_conv'] = normal((N_ODD, DEC_BATCH, CONV_W - 1, D_C), 1.0)
    inp['state_rglru'] = normal((N_ODD, DEC_BATCH, D_C), 0.5)
    inp['cache_k'] = normal((N_ODD, DEC_BATCH, w_buf, H_D, DH_D), 1.0)
    inp['cache_v'] = normal((N_ODD, DEC_BATCH, w_buf, H_D, DH_D), 1.0)
    inp['norm_mix'] = 1.0 + normal((DEPTH, d), 0.02)
    inp['norm_ffn'] = 1.0 + normal((DEPTH, d), 0.02)
    inp['norm_final'] = 1.0 + normal((d,), 0.02)
    inp['w_in_even'] = normal((N_EVEN, d, A_PROJ + 2 * D_B), d ** -0.5)
    inp['w_out_even'] = normal((N_EVEN, D_A + D_B, d), (D_A + D_B) ** -0.5)
    inp['shift_mu'] = uniform((N_EVEN, A_PROJ), 0.0, 1.0)
    inp['decay_w0'] = uniform((N_EVEN, D_A), -6.0, -1.0)
    inp['decay_up'] = normal((N_EVEN, R_DECAY, D_A), 0.5 * R_DECAY ** -0.5)
    inp['iclr_a0'] = normal((N_EVEN, D_A), 0.1)
    inp['iclr_up'] = normal((N_EVEN, R_ICLR, D_A), 0.5 * R_ICLR ** -0.5)
    inp['gate_up'] = normal((N_EVEN, R_GATE, D_A), R_GATE ** -0.5)
    inp['key_k'] = uniform((N_EVEN, D_A), 0.7, 1.0)
    inp['key_a'] = 1.0 + normal((N_EVEN, D_A), 0.05)
    inp['bonus_r_k'] = normal((N_EVEN, H_A, DH_A), 0.1)
    inp['lnx_g'] = 1.0 + normal((N_EVEN, D_A), 0.02)
    inp['lnx_b'] = normal((N_EVEN, D_A), 0.02)
    inp['sgu_norm_g'] = 1.0 + normal((N_EVEN, D_B), 0.02)
    inp['sgu_norm_b'] = normal((N_EVEN, D_B), 0.02)
    inp['sgu_w'] = normal((N_EVEN, H_B, CHUNK, CHUNK), CHUNK ** -0.5)
    inp['sgu_b'] = 1.0 + normal((N_EVEN, H_B, CHUNK), 0.02)
    inp['w_in_odd'] = normal((N_ODD, d, 2 * D_C + 3 * D_D), d ** -0.5)
    inp['w_out_odd'] = normal((N_ODD, D_C + D_D, d), (D_C + D_D) ** -0.5)
    inp['conv_w'] = normal((N_ODD, CONV_W, D_C), CONV_W ** -0.5)
    inp['conv_b'] = normal((N_ODD, D_C), 0.02)
    inp['rgate_w'] = normal((N_ODD, H_C, DH_C, DH_C), DH_C ** -0.5)
    inp['rgate_b'] = normal((N_ODD, D_C), 0.02)
    inp['igate_w'] = normal((N_ODD, H_C, DH_C, DH_C), DH_C ** -0.5)
    inp['igate_b'] = normal((N_ODD, D_C), 0.02)
    a_c = uniform((N_ODD, D_C), 0.9, 0.999)
    a_base = a_c ** (1.0 / LRU_C)
    inp['lru_lambda'] = jnp.log(a_base) - jnp.log1p(-a_base)
    inp['rel_bias'] = normal((N_BUCKETS, H_D), 0.5)
    inp['router_group_w'] = normal((DEPTH, d, N_GROUPS), d ** -0.5)
    inp['router_group_b'] = normal((DEPTH, N_GROUPS), 0.01)
    inp['router_expert_w'] = normal((DEPTH, d, N_EXPERTS), d ** -0.5)
    inp['router_expert_b'] = normal((DEPTH, N_EXPERTS), 0.01)
    inp['exp_w_gate'] = normal((DEPTH, N_EXPERTS, d, D_EXPERT), d ** -0.5)
    inp['exp_w_up'] = normal((DEPTH, N_EXPERTS, d, D_EXPERT), d ** -0.5)
    inp['exp_w_down'] = normal((DEPTH, N_EXPERTS, D_EXPERT, d), D_EXPERT ** -0.5)
    return inp

def reference(x_prompt, x_sample, state_wkv, state_shift, state_conv, state_rglru, cache_k, cache_v,
              norm_mix, norm_ffn, norm_final,
              w_in_even, w_out_even, shift_mu, decay_w0, decay_up, iclr_a0, iclr_up, gate_up, key_k, key_a,
              bonus_r_k, lnx_g, lnx_b, sgu_norm_g, sgu_norm_b, sgu_w, sgu_b,
              w_in_odd, w_out_odd, conv_w, conv_b, rgate_w, rgate_b, igate_w, igate_b, lru_lambda, rel_bias,
              router_group_w, router_group_b, router_expert_w, router_expert_b, exp_w_gate, exp_w_up, exp_w_down):
    B, L = x_prompt.shape[:2]
    DB, S = x_sample.shape[:2]
    dt = x_prompt.dtype
    pos_p = jnp.arange(L)
    pos_s = PAST_LEN + jnp.arange(S)
    xp, xs = x_prompt, x_sample
    wkv_p, shift_p, conv_p, lru_p, k_p, v_p = [], [], [], [], [], []
    wkv_s, shift_s, chunkv_s, conv_s, lru_s, k_s, v_s = [], [], [], [], [], [], []
    for l in range(DEPTH):
        j = l // 2
        hp = rmsnorm(xp, norm_mix[l])
        hs = rmsnorm(xs, norm_mix[l])
        if l % 2 == 0:
            ew = (w_in_even[j], w_out_even[j], shift_mu[j], decay_w0[j], decay_up[j], iclr_a0[j], iclr_up[j],
                  gate_up[j], key_k[j], key_a[j], bonus_r_k[j], lnx_g[j], lnx_b[j],
                  sgu_norm_g[j], sgu_norm_b[j], sgu_w[j], sgu_b[j])
            yp, sh_new, wkv_new, _ = even_mixer(hp, jnp.zeros((B, A_PROJ), dt),
                                                jnp.zeros((B, H_A, DH_A, DH_A), dt), CHUNK, *ew)
            ys, sh_new_s, wkv_new_s, vn_s = even_mixer(hs, state_shift[j], state_wkv[j], S, *ew)
            wkv_p.append(wkv_new)
            shift_p.append(sh_new)
            wkv_s.append(wkv_new_s)
            shift_s.append(sh_new_s)
            chunkv_s.append(vn_s)
        else:
            ow = (w_in_odd[j], w_out_odd[j], conv_w[j], conv_b[j], rgate_w[j], rgate_b[j],
                  igate_w[j], igate_b[j], lru_lambda[j], rel_bias)
            yp, cv, hl, kr, vr = odd_mixer(hp, jnp.zeros((B, CONV_W - 1, D_C), dt), jnp.zeros((B, D_C), dt),
                                           pos_p, None, None, *ow)
            ys, cv_s, hl_s, kr_s, vr_s = odd_mixer(hs, state_conv[j], state_rglru[j], pos_s,
                                                   cache_k[j], cache_v[j], *ow)
            conv_p.append(cv)
            lru_p.append(hl)
            k_p.append(kr)
            v_p.append(vr)
            conv_s.append(cv_s)
            lru_s.append(hl_s)
            k_s.append(kr_s)
            v_s.append(vr_s)
        xp = xp + yp
        xs = xs + ys
        mw = (router_group_w[l], router_group_b[l], router_expert_w[l], router_expert_b[l],
              exp_w_gate[l], exp_w_up[l], exp_w_down[l])
        xp = xp + hier_moe(rmsnorm(xp, norm_ffn[l]), *mw)
        xs = xs + hier_moe(rmsnorm(xs, norm_ffn[l]), *mw)
    y_prompt = rmsnorm(xp, norm_final)
    y_sample = rmsnorm(xs, norm_final)
    return (y_prompt, y_sample,
            jnp.stack(wkv_p), jnp.stack(shift_p), jnp.stack(conv_p), jnp.stack(lru_p), jnp.stack(k_p), jnp.stack(v_p),
            jnp.stack(wkv_s), jnp.stack(shift_s), jnp.stack(chunkv_s), jnp.stack(conv_s), jnp.stack(lru_s),
            jnp.stack(k_s), jnp.stack(v_s))


_drawn_inputs = setup_inputs


def setup_inputs(seed=0):
    import zlib

    import numpy as np

    out = dict(_drawn_inputs(seed))
    spreads = {}
    factors = {'norm_final': 24.654,
     'lnx_g': 24.723,
     'sgu_norm_g': 24.839,
     'sgu_norm_b': 22.296,
     'sgu_b': 19.403,
     'rgate_b': 8.0,
     'igate_b': 7.356,
     'router_group_b': 53.851,
     'router_expert_b': 46.321,
     'lnx_b': 5.651,
     'cache_k': 3.123,
     'norm_ffn': 5.882,
     'rel_bias': 3.436}
    for name, (base, spread) in spreads.items():
        noise = np.random.default_rng([zlib.crc32(name.encode()), seed]).standard_normal(out[name].shape)
        drawn = base * np.exp(spread * noise) if base else spread * noise
        out[name] = __import__('jax').numpy.asarray(drawn.astype(out[name].dtype))
    for name, factor in factors.items():
        out[name] = (out[name] * factor).astype(out[name].dtype)
    return out
```

```python
from contextlib import ExitStack

import concourse.bass as bass
from concourse import mybir

F32 = mybir.dt.float32
F32R = mybir.dt.float32r
ALU = mybir.AluOpType
ACT = mybir.ActivationFunctionType
AX = mybir.AxisListType.X

P = 128
D = 1024
KT = D // P
TP = 256
NB, NS = 8, 8
TS = NB * NS
T = TP + TS
HT = 4
A_TILES = 14
NE = 16
CHUNK_ELEMS = 2048
C = 64
N_CHUNKS = T // C
PAST = 1024
KEYS = PAST + NS
NEG = -1e30

IN0_CHUNKS, OUT_CHUNKS, IN1_CHUNKS, EXPERT_CHUNKS = 11, 4, 10, 6
MOE_CHUNKS = NE * EXPERT_CHUNKS
AT_IN0 = 0
AT_OUT0 = AT_IN0 + IN0_CHUNKS
AT_MOE0 = AT_OUT0 + OUT_CHUNKS
AT_IN1 = AT_MOE0 + MOE_CHUNKS
AT_OUT1 = AT_IN1 + IN1_CHUNKS
AT_MOE1 = AT_OUT1 + OUT_CHUNKS
STREAM = AT_MOE1 + MOE_CHUNKS
W_RING, RAW_RING = 2, 3

PARAMS = [("norm_mix0", 8), ("norm_mix1", 8), ("norm_ffn0", 8), ("norm_ffn1", 8), ("norm_final", 8),
          ("shift_mu", 14), ("decay_w0", 4), ("iclr_a0", 4), ("key_k", 4), ("key_a", 4), ("bonus", 4),
          ("lnx_g", 4), ("lnx_b", 4), ("sgu_g", 4), ("sgu_b", 4), ("conv_w", 16), ("conv_b", 4),
          ("rgate_b", 4), ("igate_b", 4), ("lambda", 4), ("router_b0", 1), ("router_b1", 1)]
CONSTS = [("ident", 128), ("ones", 128), ("head_ones", 128), ("reset", T), ("mask_prompt", 128),
          ("mask_sample", 128), ("diag8", 64), ("low8", 64), ("low16", 64), ("low32", 64), ("low64", 64),
          ("eye64", 64), ("own_batch", 8), ("tri", 128), ("first", 20), ("same_query", 16),
          ("own_head", 8), ("head_rows", 32)]


def columns(table):
    at, out = 0, {}
    for name, n in table:
        out[name] = (at, n)
        at += n
    return out, at


PCOL, NPARAM = columns(PARAMS)
CCOL, NCONST = columns(CONSTS)


def tiles_through(c):
    n = 0
    for i in range(c + 1):
        in_moe = AT_MOE0 <= i < AT_IN1 or AT_MOE1 <= i
        k = (i - AT_MOE0) % (AT_MOE1 - AT_MOE0)
        n += 4 if in_moe and (k in (MOE_CHUNKS - 2, MOE_CHUNKS - 1) or (k >= 4 and (k - 4) % 6 in (2, 3))) else 2
    return n


def tile(c, i):
    return tiles_through(c - 1) + i + 1


EXPERT_TILES = 16


def decoder_layers(nc, ins, outs, stop=None):
    with ExitStack() as ctx:
        def sb(name, shape, dt=F32):
            return ctx.enter_context(nc.sbuf_tensor(name, shape, dt))

        made = {}

        def S(name):
            if name not in made:
                made[name] = ctx.enter_context(nc.semaphore(name))
            return made[name]

        xt = sb("xt", [P, KT, T])
        h32 = sb("h32", [P, KT, T])
        h_hi = sb("h_hi", [P, KT, T], F32R)
        h_lo = sb("h_lo", [P, KT, T], F32R)
        raw = sb("raw", [P, RAW_RING, CHUNK_ELEMS])
        w_hi = sb("w_hi", [P, W_RING, CHUNK_ELEMS], F32R)
        w_lo = sb("w_lo", [P, W_RING, CHUNK_ELEMS], F32R)
        hid = sb("hid", [P, HT, T])
        hid_hi = sb("hid_hi", [P, HT, T], F32R)
        hid_lo = sb("hid_lo", [P, HT, T], F32R)
        consts = sb("consts", [P, NCONST])
        params = sb("params", [P, NPARAM])
        router = sb("router_sb", [P, 2, KT, 20])
        small = sb("small", [P, 380])
        ARENA = 22144
        arena = sb("arena", [P, ARENA])
        ps = ctx.enter_context(nc.psum_tensor("ps", [P, 8, 512], F32))

        def const(name, rows=P):
            at, n = CCOL[name]
            return consts[0:rows, at:at + n]

        def par(name, i):
            return params[:, PCOL[name][0] + i:PCOL[name][0] + i + 1]

        def par_over(name, n, inner):
            at = PCOL[name][0]
            return params[:, at:at + n].unsqueeze(2).broadcast_to((P, n, inner))

        def take(at, *shape, part=P):
            n = 1
            for s in shape:
                n *= s
            assert at + n <= ARENA, (at, n)
            v = arena[0:part, at:at + n]
            if len(shape) == 2:
                return v.rearrange("p (a b) -> p a b", a=shape[0])
            if len(shape) == 3:
                return v.rearrange("p (a b c) -> p a b c", a=shape[0], b=shape[1])
            if len(shape) == 4:
                return v.rearrange("p (a b c d) -> p a b c d", a=shape[0], b=shape[1], c=shape[2])
            return v

        ident, ones, head_ones = const("ident"), const("ones"), const("head_ones")

        lt = small[:, 0:60].rearrange("p (a b) -> p a b", a=3)
        ra = small[:, 60:120].rearrange("p (a b) -> p a b", a=3)
        rb = small[:, 120:180].rearrange("p (a b) -> p a b", a=3)
        rc = small[:, 180:240].rearrange("p (a b) -> p a b", a=3)
        gates_tok = small[:, 240:288].rearrange("p (a b) -> p a b", a=3)
        rs = small[:, 288:324].rearrange("p (a b) -> p a b", a=12)
        eps_norm = small[:, 324:325]
        eps_gn = small[:, 325:326]
        s_root, s_rstd = take(NE * T, T), take(NE * T + T, T)
        logits_ch = s_root[0:20, :]
        gates_ch = s_rstd[0:16, :]
        gate_all = take(0, NE * T)

        xs = take(0, A_TILES, T)
        s1, s2, s4, s5, s6 = (take(4480 + 1280 * i, HT, T) for i in range(5))
        s3 = hid[:, :, :]
        ar = h32[:, :, :].rearrange("p a b -> p (a b)").rearrange("p (j c w t) -> p j c w t", j=HT, c=N_CHUNKS, w=2)
        G0 = 10880
        gu, gv = take(G0, HT, T), take(G0 + 1280, HT, T)
        sbias = take(G0 + 2560, HT, T)
        vn_tok = take(G0 + 3840, 3, 512)
        sw = take(G0 + 5376, HT, P)
        sw8 = take(G0 + 5888, HT, TS, part=TS)
        p_ring = take(G0 + 6144, 4, 329)
        d_ring = take(G0 + 7460, 2, T)
        gb_m, gk_m = take(G0, 8, 128), take(G0 + 1024, 8, 128)
        dd, ee, pp, qq, d2, e2 = (take(G0 + 2048 + 512 * i, 8, 64) for i in range(6))
        lo16, lo32, lo64 = (take(G0 + 5120 + 512 * i, 8, 64) for i in range(3))
        v_tok, b_tok, k_tok = (take(G0 + 6656 + 512 * i, 8, 64) for i in range(3))
        swkv = take(G0 + 8192, HT, NB, 64)
        lora = take(G0 + 10240, 2, 512)
        state = sb("state", [P, HT, 64])
        w_end = small[:, 330:378].rearrange("p (a b) -> p a b", a=HT)
        state_flat = state[:, :, :].rearrange("p a b -> p (a b)")
        shift0 = state_flat[:, 0:112].rearrange("p (a b) -> p a b", a=A_TILES)
        shift_out = state_flat[:, 112:238].rearrange("p (a b) -> p a b", a=A_TILES)
        qe = h32[0:TS, 0:4, :].rearrange("p a b -> p (a b)")[:, 0:1024].rearrange("p (a b) -> p a b", a=2)
        ve = h32[0:TS, 4:8, :].rearrange("p a b -> p (a b)")[:, 0:1024].rearrange("p (a b) -> p a b", a=2)
        g_root, g_rstd = hid[:, 0, :], hid[:, 1, :]

        block = ctx.enter_context(nc.Block())

        steps = [0]

        def next_reads(eng, ins_):
            steps[0] += 1
            ins_.then_inc(S("vector_step"), 1)
            eng.wait_ge(S("vector_step"), steps[0])

        def chunk_view(w, slot, rows, tiles):
            return w[:, slot, :].rearrange("p (m k n) -> p m k n", m=tiles, k=rows)

        def load_chunk(eng, c, it=None):
            if c >= RAW_RING or it is not None:
                eng.wait_ge(S("w_lo_made"), c - RAW_RING + 1 + (0 if it is None else EXPERT_CHUNKS * it))
            src = ins["stream"][c] if it is None else ins["stream"][it * EXPERT_CHUNKS + c]
            eng.dma_start(raw[:, c % RAW_RING, :], src).then_inc(S(f"raw_loaded{c % RAW_RING}"), 16)

        def split_hi(eng, c, it=None):
            if c >= STREAM:
                return
            more = 0 if it is None else it * (16 * EXPERT_CHUNKS // RAW_RING)
            eng.wait_ge(S(f"raw_loaded{c % RAW_RING}"), 16 * (c // RAW_RING + 1) + more)
            if c >= W_RING:
                eng.wait_ge(S("tile_done"), tiles_through(c - W_RING) + (0 if it is None else EXPERT_TILES * it))
            eng.activation(w_hi[:, c % W_RING, :], raw[:, c % RAW_RING, :], ACT.Copy).then_inc(S("w_hi_made"), 1)

        def split_lo(eng, c, it=None):
            if c >= STREAM:
                return
            eng.wait_ge(S("w_hi_made"), c + 1 + (0 if it is None else EXPERT_CHUNKS * it))
            eng.tensor_tensor(w_lo[:, c % W_RING, :], raw[:, c % RAW_RING, :], w_hi[:, c % W_RING, :],
                              ALU.subtract).then_inc(S("w_lo_made"), 1)

        def tile_product(eng, bank, slot, m, rows, tiles, x_hi, x_lo):
            hi, lo = chunk_view(w_hi, slot, rows, tiles), chunk_view(w_lo, slot, rows, tiles)
            for k in range(rows):
                eng.matmul(ps[:, bank, 0:T], hi[:, m, k, :], x_hi[:, k, :], start=(k == 0), stop=False)
                eng.matmul(ps[:, bank, 0:T], hi[:, m, k, :], x_lo[:, k, :], start=False, stop=False)
                mm = eng.matmul(ps[:, bank, 0:T], lo[:, m, k, :], x_hi[:, k, :], start=False, stop=(k == rows - 1))
            return mm

        def norm_act(eng, i, split):
            for q in range(4):
                eng.activation(h32[:, 2 * q:2 * q + 2, :], xt[:, 2 * q:2 * q + 2, :], ACT.Square).then_inc(S("norm_sq"), 1)
            eng.wait_ge(S("norm_ms"), i + 1)
            eng.activation(s_root, ps[:, 0, 0:T], ACT.Sqrt, bias=eps_norm, scale=1.0 / D).then_inc(S("norm_root"), 1)
            if split:
                for q in range(2):
                    eng.wait_ge(S("norm_h"), KT * i + 4 * (q + 1))
                    eng.activation(h_hi[:, 4 * q:4 * q + 4, :], h32[:, 4 * q:4 * q + 4, :], ACT.Copy).then_inc(S("norm_hi"), 1)

        def norm_pe(eng, i):
            for k in range(KT):
                if k % 2 == 0:
                    eng.wait_ge(S("norm_sq"), 4 * i + k // 2 + 1)
                mm = eng.matmul(ps[:, 0, 0:T], ones, h32[:, k, :], start=(k == 0), stop=(k == KT - 1))
            mm.then_inc(S("norm_ms"), 1)

        def norm_dve(eng, i, weight, split):
            eng.wait_ge(S("norm_root"), i + 1)
            eng.reciprocal(s_rstd, s_root).then_inc(S("norm_rstd"), 1)
            eng.wait_ge(S("norm_rstd"), i + 1)
            for k in range(KT):
                eng.scalar_tensor_tensor(h32[:, k, :], xt[:, k, :], par(weight, k), s_rstd, ALU.mult, ALU.mult).then_inc(S("norm_h"), 1)
            if split:
                for q in range(2):
                    eng.wait_ge(S("norm_hi"), 2 * i + q + 1)
                    eng.tensor_tensor(h_lo[:, 4 * q:4 * q + 4, :], h32[:, 4 * q:4 * q + 4, :],
                                      h_hi[:, 4 * q:4 * q + 4, :], ALU.subtract).then_inc(S("norm_lo"), 1)

        def moe_pe(eng, layer, at):
            ni, e0 = 1 + 2 * layer, NE * layer
            norm_pe(eng, ni)
            for k in range(KT):
                eng.wait_ge(S("norm_h"), KT * ni + k + 1)
                mm = eng.matmul(ps[0:20, 4, 0:T], router[:, layer, k, :], h32[:, k, :], start=(k == 0), stop=(k == KT - 1))
            mm.then_inc(S("logits"), 1)

            def gate(c, e, it=None):
                more = 0 if it is None else HT * it
                for m in range(HT):
                    if m % 2 == 0:
                        eng.wait_ge(S("w_lo_made"), c + m // 2 + 1 + (0 if it is None else EXPERT_CHUNKS * it))
                    if e:
                        eng.wait_ge(S("silu_made"), HT * (e - 1) + m + 1 + more)
                    mm = tile_product(eng, m, (c + m // 2) % W_RING, m % 2, KT, 2, h_hi, h_lo)
                    mm.then_inc(S("tile_done"), 1)

            def up(c, e, it=None):
                more = 0 if it is None else 2 * HT * it
                for m in range(HT):
                    if m % 2 == 0:
                        eng.wait_ge(S("w_lo_made"), c + m // 2 + 1 + (0 if it is None else EXPERT_CHUNKS * it))
                    if e % NE:
                        eng.wait_ge(S("down_added"), 2 * HT * e - 3 + m + more)
                    mm = tile_product(eng, 4 + m, (c + m // 2) % W_RING, m % 2, KT, 2, h_hi, h_lo)
                    mm.then_inc(S("tile_done"), 1)

            def down(c, e, it=None):
                eng.wait_ge(S("hid_lo_made"), e + 1 + (0 if it is None else it))
                for half in range(2):
                    eng.wait_ge(S("w_lo_made"), c + half + 1 + (0 if it is None else EXPERT_CHUNKS * it))
                    for m in range(HT):
                        if half:
                            eng.wait_ge(S("down_added"), 2 * HT * e + m + 1 + (0 if it is None else 2 * HT * it))
                        mm = tile_product(eng, 4 + m, (c + half) % W_RING, m, HT, 4, hid_hi, hid_lo)
                        mm.then_inc(S("tile_done"), 1)

            for q in range(2):
                eng.wait_ge(S("norm_lo"), 2 * ni + q + 1)
            eng.wait_ge(S("logits_sb"), layer + 1)
            for i, (a, b) in enumerate(((0, 128), (128, 256), (256, 320))):
                mm = eng.transpose(ps[0:b - a, 5, 20 * i:20 * i + 20], logits_ch[:, a:b], ident[0:20, 0:20])
            mm.then_inc(S("logits_tok"), 1)
            gate(at, e0)
            eng.wait_ge(S("routed"), 2 * layer + 2)
            up(at + 2, e0)
            eng.wait_ge(S("gates_tok"), layer + 1)
            eng.wait_ge(S("silu_made"), HT * e0 + HT)
            for i, (a, b) in enumerate(((0, 128), (128, 256), (256, 320))):
                mm = eng.transpose(ps[0:16, 0, a:b], gates_tok[0:b - a, i, :], ident[0:b - a, 0:b - a])
            mm.then_inc(S("gates_back"), 1)
            eng.wait_ge(S("gates_ch"), layer + 1)
            for e in range(NE):
                if e >= 3:
                    eng.wait_ge(S("gate_rows"), 16 * layer + e - 2)
                eng.matmul(ps[:, 1 + e % 3, 0:T], ident[0:16, e:e + 1].broadcast_to((16, P)), gates_ch,
                           start=True, stop=True).then_inc(S("gate_bc"), 1)
            eng.wait_ge(S("gate_rows"), 16 * layer + NE)
            with eng.Fori(0, NE - 1) as it:
                gate(at + 4, e0 + 1, it)
                down(at + 6, e0, it)
                up(at + 8, e0 + 1, it)
            down(at + MOE_CHUNKS - 2, e0 + NE - 1)

        def moe_act(eng, layer, at):
            ni, e0 = 1 + 2 * layer, NE * layer
            split_hi(eng, at)
            split_hi(eng, at + 1)
            norm_act(eng, ni, True)
            eng.wait_ge(S("logits"), layer + 1)
            eng.activation(logits_ch, ps[0:20, 4, 0:T], ACT.Identity, bias=params[0:20, PCOL[f"router_b{layer}"][0]:][:, 0:1])\
               .then_inc(S("logits_sb"), 1)

            def silu(e, it=None):
                if e:
                    eng.wait_ge(S("hid_lo_made"), e + (0 if it is None else it))
                for m in range(HT):
                    eng.wait_ge(S("tile_done"), tile(at if it is None else at + 4, m) + (0 if it is None else EXPERT_TILES * it))
                    eng.activation(hid[:, m, :], ps[:, m, 0:T], ACT.Silu).then_inc(S("silu_made"), 1)
                    if m % 2:
                        split_hi(eng, (at + (2 if e == e0 else 6)) + m // 2, it)

            def hidden(e, it=None):
                eng.wait_ge(S("hid_made"), e + 1 + (0 if it is None else it))
                eng.activation(hid_hi[:, :, :], hid[:, :, :], ACT.Copy).then_inc(S("hid_hi_made"), 1)

            eng.wait_ge(S("group_shifted"), layer + 1)
            eng.activation(rb[:, :, 0:4], rb[:, :, 0:4], ACT.Exp).then_inc(S("router_exp"), 1)
            eng.wait_ge(S("pair_shifted"), layer + 1)
            eng.activation(rs[:, 7, :], rs[:, 6, :], ACT.Exp).then_inc(S("router_exp"), 1)
            silu(e0)
            split_hi(eng, at + 4)
            split_hi(eng, at + 5)
            eng.wait_ge(S("gates_back"), layer + 1)
            eng.activation(gates_ch, ps[0:16, 0, 0:T], ACT.Copy).then_inc(S("gates_ch"), 1)
            for e in range(NE):
                eng.wait_ge(S("gate_bc"), 16 * layer + e + 1)
                eng.activation(gate_all[:, T * e:T * e + T], ps[:, 1 + e % 3, 0:T], ACT.Copy).then_inc(S("gate_rows"), 1)
            hidden(e0)
            with eng.Fori(0, NE - 1) as it:
                silu(e0 + 1, it)
                for c in range(8, 12):
                    split_hi(eng, at + c, it)
                hidden(e0 + 1, it)

        def moe_dve(eng, layer, at):
            ni, e0 = 1 + 2 * layer, NE * layer
            split_lo(eng, at)
            split_lo(eng, at + 1)
            norm_dve(eng, ni, f"norm_ffn{layer}", True)
            def over(v, m):
                return v.broadcast_to((P, 3, m))

            eng.wait_ge(S("logits_tok"), layer + 1)
            eng.tensor_copy(lt[:, 0:2, :], ps[:, 5, 0:40].rearrange("p (a b) -> p a b", a=2)).then_inc(S("routed"), 1)
            eng.tensor_copy(lt[0:64, 2, :], ps[0:64, 5, 40:60]).then_inc(S("routed"), 1)
            eng.wait_ge(S("routed"), 2 * layer + 2)
            r = [rs[:, i, :].unsqueeze(2) for i in range(12)]
            first4 = const("first")[:, 0:4].unsqueeze(1).broadcast_to((P, 3, 4))
            first16 = const("first")[:, 4:20].unsqueeze(1).broadcast_to((P, 3, 16))
            lg, le = lt[:, :, 0:4], lt[:, :, 4:20]
            next_reads(eng, eng.tensor_reduce(r[0], lg, AX, ALU.max))
            next_reads(eng, eng.tensor_tensor(ra[:, :, 0:4], lg, over(r[0], 4), ALU.is_equal))
            next_reads(eng, eng.tensor_tensor(ra[:, :, 0:4], ra[:, :, 0:4], first4, ALU.mult))
            next_reads(eng, eng.tensor_reduce(r[1], ra[:, :, 0:4], AX, ALU.max))
            next_reads(eng, eng.tensor_tensor(ra[:, :, 0:4], ra[:, :, 0:4], over(r[1], 4), ALU.is_equal))
            eng.tensor_tensor(rb[:, :, 0:4], lg, over(r[0], 4), ALU.subtract).then_inc(S("group_shifted"), 1)
            for i in range(4):
                last = eng.tensor_copy(rc[:, :, 4 * i:4 * i + 4], ra[:, :, i:i + 1].broadcast_to((P, 3, 4)))
            next_reads(eng, last)
            next_reads(eng, eng.tensor_tensor(le, le, rc[:, :, 0:16], ALU.mult))
            next_reads(eng, eng.tensor_scalar(rc[:, :, 0:16], rc[:, :, 0:16], 1.0, -NEG, ALU.subtract, ALU.mult))
            next_reads(eng, eng.tensor_tensor(le, le, rc[:, :, 0:16], ALU.add))
            picks = (ra[:, :, 4:20], rc[:, :, 0:16])
            for i in range(2):
                best = r[2 + i]
                next_reads(eng, eng.tensor_reduce(best, le, AX, ALU.max))
                next_reads(eng, eng.tensor_tensor(picks[i], le, over(best, 16), ALU.is_equal))
                next_reads(eng, eng.tensor_tensor(picks[i], picks[i], first16, ALU.mult))
                next_reads(eng, eng.tensor_reduce(r[4 + i], picks[i], AX, ALU.max))
                next_reads(eng, eng.tensor_tensor(picks[i], picks[i], over(r[4 + i], 16), ALU.is_equal))
                if i == 0:
                    next_reads(eng, eng.tensor_scalar(gates_tok, picks[0], 2 * NEG, None, ALU.mult))
                    next_reads(eng, eng.tensor_tensor(le, le, gates_tok, ALU.add))
            eng.tensor_tensor(r[6], r[3], r[2], ALU.subtract).then_inc(S("pair_shifted"), 1)
            eng.wait_ge(S("router_exp"), 2 * layer + 2)
            next_reads(eng, eng.tensor_reduce(r[8], rb[:, :, 0:4], AX, ALU.add))
            next_reads(eng, eng.tensor_scalar(r[9], r[7], 1.0, None, ALU.add))
            next_reads(eng, eng.tensor_tensor(r[9], r[9], r[8], ALU.mult))
            next_reads(eng, eng.reciprocal(r[9], r[9]))
            next_reads(eng, eng.tensor_tensor(r[10], r[9], r[7], ALU.mult))
            next_reads(eng, eng.tensor_tensor(picks[0], picks[0], over(r[9], 16), ALU.mult))
            next_reads(eng, eng.tensor_tensor(picks[1], picks[1], over(r[10], 16), ALU.mult))
            eng.tensor_tensor(gates_tok, picks[0], picks[1], ALU.add).then_inc(S("gates_tok"), 1)

            def gated(e, it=None):
                at_e = T * (e - e0) + (0 if it is None else T * it)
                g = gate_all[:, bass.ds(at_e, T)] if it is not None else gate_all[:, at_e:at_e + T]
                eng.wait_ge(S("silu_made"), HT * (e + 1) + (0 if it is None else HT * it))
                eng.tensor_tensor(hid[:, :, :], hid[:, :, :], g.unsqueeze(1).broadcast_to((P, HT, T)), ALU.mult)\
                   .then_inc(S("gated"), 1)

            def hidden(e, it=None):
                more = 0 if it is None else it
                eng.wait_ge(S("gated"), e + 1 + more)
                eng.wait_ge(S("tile_done"), tile(at + 2 if it is None else at + 8, 3) + (0 if it is None else EXPERT_TILES * it))
                eng.tensor_tensor(hid[:, :, :], hid[:, :, :], ps[:, 4:8, 0:T], ALU.mult).then_inc(S("hid_made"), 1)
                eng.wait_ge(S("hid_hi_made"), e + 1 + more)
                eng.tensor_tensor(hid_lo[:, :, :], hid[:, :, :], hid_hi[:, :, :], ALU.subtract).then_inc(S("hid_lo_made"), 1)

            def add_down(e, it=None, c=None):
                for m in range(2 * HT):
                    more = 0 if it is None else 2 * HT * it
                    eng.wait_ge(S("tile_done"), tile(at + MOE_CHUNKS - 2 if it is None else at + 6, m) + (0 if it is None else EXPERT_TILES * it))
                    if e > e0 or it is not None:
                        v = 2 * HT * (e - 1) + m + 1
                        if v > 0:
                            eng.wait_ge(S("down_added"), v + more)
                    eng.tensor_tensor(xt[:, m, :], xt[:, m, :], ps[:, 4 + m % HT, 0:T], ALU.add).then_inc(S("down_added"), 1)
                    if m % HT == HT - 1 and c is not None:
                        split_lo(eng, c + m // HT, it)

            for c in range(2, 6):
                split_lo(eng, at + c)
            eng.wait_ge(S("gate_rows"), 16 * layer + NE)
            gated(e0)
            hidden(e0)
            with eng.Fori(0, NE - 1) as it:
                split_lo(eng, at + 6, it)
                split_lo(eng, at + 7, it)
                gated(e0 + 1, it)
                add_down(e0, it, at + 8)
                split_lo(eng, at + 10, it)
                split_lo(eng, at + 11, it)
                hidden(e0 + 1, it)
            add_down(e0 + NE - 1)

        def project_pe(eng, n, at, chunks, free=None):
            for i in range(2 * chunks):
                c = at + i // 2
                if i % 2 == 0:
                    eng.wait_ge(S("w_lo_made"), c + 1)
                if i >= 8:
                    eng.wait_ge(S(f"{n}_taken"), i - 7)
                mm = tile_product(eng, i % 8, c % W_RING, i % 2, KT, 2, h_hi, h_lo)
                mm.then_inc(S("tile_done"), 1)

        def out_proj_act(eng, at):
            for c in range(OUT_CHUNKS):
                split_hi(eng, at + c)

        def out_proj_dve(eng, n, at):
            split_lo(eng, at)
            split_lo(eng, at + 1)
            for i in range(KT):
                eng.wait_ge(S("tile_done"), tile(at, i))
                eng.tensor_tensor(xt[:, i, :], xt[:, i, :], ps[:, i, 0:T], ALU.add).then_inc(S(f"{n}_taken"), 1)
                if i in (1, 3):
                    split_lo(eng, at + 2 + i // 2)

        R_T, K_T, V_T = xs[:, 0:4, :], xs[:, 4:8, :], xs[:, 8:12, :]
        flat = lambda v: v.rearrange("p a b -> p (a b)")

        def prompt_sample(v, lead=0):
            return v[:, 0:TP], v[:, TP:T].rearrange("p (b s) -> p b s", b=NB)

        def ring_parts(j, lead):
            v = p_ring[:, j % 4, :]
            s = v[:, 257:329].rearrange("p (b s) -> p b s", b=NB)
            return v[:, 1 - lead:257 - lead], s[:, :, 1 - lead:9 - lead]

        def mix0_act(eng):
            split_hi(eng, AT_IN0)
            split_hi(eng, AT_IN0 + 1)
            eng.wait_ge(S("x_loaded"), 16)
            eng.wait_ge(S("constants_set"), 2)
            norm_act(eng, 0, True)
            eng.wait_ge(S("small_loaded"), 16 * 8)
            for i in range(2 * IN0_CHUNKS):
                eng.wait_ge(S("tile_done"), tile(AT_IN0, i))
                if i < A_TILES:
                    if i >= 4:
                        eng.wait_ge(S("shift_mixed"), i - 3)
                        eng.wait_ge(S("shift_kept"), i - 3)
                    else:
                        eng.wait_ge(S("constants_set"), 3)
                    a, b = ring_parts(i, 0)
                    pa, pb = prompt_sample(ps[:, i % 8, 0:T])
                    eng.activation(a, pa, ACT.Copy)
                    eng.activation(b, pb, ACT.Copy).then_inc(S("in0_taken"), 1)
                    v = p_ring[:, i % 4, 257:329].rearrange("p (b s) -> p b s", b=NB)
                    eng.activation(v[:, :, 0:1], shift0[:, i, :].unsqueeze(2), ACT.Copy).then_inc(S("ring_filled"), 1)
                elif i < A_TILES + HT:
                    eng.activation(gu[:, i - A_TILES, :], ps[:, i % 8, 0:T], ACT.Gelu_apprx_tanh).then_inc(S("in0_taken"), 1)
                else:
                    eng.activation(gv[:, i - A_TILES - HT, :], ps[:, i % 8, 0:T], ACT.Gelu_apprx_tanh).then_inc(S("in0_taken"), 1)
                if i % 2 and i // 2 + 2 < IN0_CHUNKS:
                    split_hi(eng, AT_IN0 + i // 2 + 2)
            eng.wait_ge(S("shift_mixed"), A_TILES)
            eng.activation(xs[0:64, 12, :], xs[0:64, 12, :], ACT.Tanh).then_inc(S("lora_in"), 1)
            eng.activation(xs[:, 13, :], xs[:, 13, :], ACT.Sigmoid).then_inc(S("lora_in"), 1)
            for j in range(HT):
                eng.wait_ge(S("lora_done"), j + 1)
                eng.activation(s1[:, j, :], ps[:, j, 0:T], ACT.Sigmoid, bias=par("decay_w0", j)).then_inc(S("decay_sig"), 1)
            for j in range(HT):
                eng.wait_ge(S("lora_done"), 4 + j + 1)
                eng.activation(s4[:, j, :], ps[:, 4 + j, 0:T], ACT.Sigmoid, bias=par("iclr_a0", j)).then_inc(S("iclr_made"), 1)
            eng.wait_ge(S("sgu_var"), 1)
            eng.activation(g_root, ps[:, 1, 0:T], ACT.Sqrt, bias=eps_norm, scale=1.0 / 512).then_inc(S("sgu_root"), 1)
            for i in range(3):
                eng.wait_ge(S("vn_turned"), i + 1)
                n = P if i < 2 else TS
                eng.activation(vn_tok[0:n, i, :], ps[0:n, 2 + i, :], ACT.Copy).then_inc(S("vn_tok_made"), 1)
            eng.wait_ge(S("gmlp_made"), HT)
            eng.activation(h_hi[:, 4:8, :], gu, ACT.Copy).then_inc(S("y_hi"), 1)
            eng.wait_ge(S("log_run"), HT)
            eng.activation(s3, s2, ACT.Exp).then_inc(S("decays_made"), 1)
            eng.wait_ge(S("log_prev"), 1)
            eng.activation(s1, s1, ACT.Exp).then_inc(S("decays_made"), 1)
            eng.activation(s2, s2, ACT.Exp, scale=-1.0).then_inc(S("decays_made"), 1)
            eng.wait_ge(S("kk_clamped"), 1)
            eng.activation(s5, s5, ACT.Sqrt).then_inc(S("kk_root"), 1)
            for g in range(3):
                wkv_group_act(eng, g)
            eng.wait_ge(S("gn_var"), HT)
            for j in range(HT):
                eng.activation(s5[:, j, :], ps[:, 4 + j, 0:T], ACT.Sqrt, bias=eps_gn, scale=1.0 / 64).then_inc(S("gn_root"), 1)
            eng.wait_ge(S("gn_scaled"), 1)
            for j in range(HT):
                eng.activation(s1[:, j, :], s1[:, j, :], ACT.Identity, bias=par("lnx_b", j), scale=par("lnx_g", j)).then_inc(S("gn_affine"), 1)
            eng.wait_ge(S("ya_made"), 1)
            eng.activation(h_hi[:, 0:4, :], s1, ACT.Copy).then_inc(S("y_hi"), 1)

        def mix0_dve(eng):
            eng.memset(small[:, 0:60], 0.0).then_inc(S("constants_set"), 1)
            eng.memset(eps_norm, 1e-6)
            eng.memset(eps_gn, 64e-5).then_inc(S("constants_set"), 1)
            eng.memset(p_ring[:, :, 0:1], 0.0).then_inc(S("constants_set"), 1)
            split_lo(eng, AT_IN0)
            split_lo(eng, AT_IN0 + 1)
            eng.wait_ge(S("small_loaded"), 16 * 8)
            norm_dve(eng, 0, "norm_mix0", True)
            for i in range(A_TILES):
                eng.wait_ge(S("ring_filled"), i + 1)
                if i >= 2:
                    eng.wait_ge(S("shift_mixed"), i - 1)
                d = prompt_sample(d_ring[:, i % 2, :])
                now, before, to = ring_parts(i, 0), ring_parts(i, 1), prompt_sample(xs[:, i, :])
                eng.tensor_tensor(d[0], before[0], now[0], ALU.subtract)
                eng.tensor_tensor(d[1], before[1], now[1], ALU.subtract).then_inc(S("shift_diff"), 1)
                eng.wait_ge(S("shift_diff"), i + 1)
                eng.scalar_tensor_tensor(to[0], d[0], par("shift_mu", i), now[0], ALU.mult, ALU.add)
                eng.scalar_tensor_tensor(to[1], d[1], par("shift_mu", i), now[1], ALU.mult, ALU.add).then_inc(S("shift_mixed"), 1)
                if i % 2 and i // 2 + 2 < IN0_CHUNKS:
                    split_lo(eng, AT_IN0 + i // 2 + 2)
            for c in range(A_TILES // 2 + 2, IN0_CHUNKS):
                split_lo(eng, AT_IN0 + c)
            eng.wait_ge(S("shift_mixed"), A_TILES)
            next_reads(eng, eng.tensor_tensor(s6, K_T, par_over("key_k", HT, T), ALU.mult))
            eng.tensor_tensor(s5, s6, s6, ALU.mult).then_inc(S("kk_sq"), 1)
            eng.wait_ge(S("decay_sig"), HT)
            next_reads(eng, eng.tensor_scalar(s1, s1, -0.6065306597126334, None, ALU.mult))
            for j in range(HT):
                eng.tensor_tensor_scan(s2[:, j, :], const("reset"), s1[:, j, :], 0.0, ALU.mult, ALU.add).then_inc(S("log_run"), 1)
            eng.wait_ge(S("log_run"), HT)
            eng.tensor_tensor(s1, s2, s1, ALU.subtract).then_inc(S("log_prev"), 1)
            eng.wait_ge(S("sgu_mean"), 1)
            next_reads(eng, eng.tensor_scalar(g_rstd, ps[:, 0, 0:T], 1.0 / 512, None, ALU.mult))
            eng.wait_ge(S("shift_kept"), A_TILES)
            next_reads(eng, eng.tensor_tensor(gv, gv, g_rstd.unsqueeze(1).broadcast_to((P, HT, T)), ALU.subtract))
            eng.tensor_tensor(sq_gv, gv, gv, ALU.mult).then_inc(S("sgu_sq"), 1)
            eng.wait_ge(S("sgu_root"), 1)
            next_reads(eng, eng.reciprocal(g_rstd, g_root))
            for j in range(HT):
                last = eng.scalar_tensor_tensor(gv[:, j, :], gv[:, j, :], par("sgu_g", j), g_rstd, ALU.mult, ALU.mult)
            next_reads(eng, last)
            eng.tensor_tensor(gv, gv, par_over("sgu_b", HT, T), ALU.add).then_inc(S("vn_made"), 1)
            eng.wait_ge(S("vn_made"), 1)
            eng.tensor_tensor(sw, sw, const("tri").unsqueeze(1).broadcast_to((P, HT, P)), ALU.mult)
            eng.tensor_tensor(sw8, sw8, const("mask_sample", TS)[:, 64:128].unsqueeze(1).broadcast_to((TS, HT, TS)), ALU.mult)\
               .then_inc(S("sgu_masked"), 1)
            for j in range(HT):
                eng.wait_ge(S("gated_sums"), j + 1)
                next_reads(eng, eng.tensor_tensor(sbias[:, j, :], sbias[:, j, :], ps[:, 4 + j, 0:T], ALU.add))
                eng.tensor_tensor(gu[:, j, :], gu[:, j, :], sbias[:, j, :], ALU.mult).then_inc(S("gmlp_made"), 1)
            eng.wait_ge(S("y_hi"), 1)
            eng.tensor_tensor(h_lo[:, 4:8, :], gu, h_hi[:, 4:8, :], ALU.subtract).then_inc(S("y_lo"), 1)
            eng.wait_ge(S("kk_sum"), HT)
            eng.tensor_scalar(s5, ps[:, 0:4, 0:T], 1e-24, None, ALU.max).then_inc(S("kk_clamped"), 1)
            eng.wait_ge(S("decays_made"), 1)
            v5 = lambda v: v.rearrange("p j (c t) -> p j c t", c=N_CHUNKS)
            eng.tensor_tensor(ar[:, :, :, 1, :], v5(R_T), v5(s3), ALU.mult)
            eng.tensor_copy(w_end[:, :, 0:4], v5(s3)[:, :, 0:4, C - 1])
            next_reads(eng, eng.tensor_copy(w_end[:, :, 4:12], s3[:, :, TP:T].rearrange("p j (b s) -> p j b s", b=NB)[:, :, :, NS - 1]))
            eng.wait_ge(S("iclr_made"), HT)
            for j in range(HT):
                last = eng.tensor_scalar(s3[:, j, :], s4[:, j, :], 1.0, par("key_a", j), ALU.subtract, ALU.mult)
            next_reads(eng, last)
            next_reads(eng, eng.scalar_tensor_tensor(flat(K_T), flat(s3), 1.0, flat(K_T), ALU.add, ALU.mult))
            eng.wait_ge(S("kk_root"), 1)
            next_reads(eng, eng.reciprocal(s5, s5))
            next_reads(eng, eng.tensor_tensor(s6, s6, s5, ALU.mult))
            next_reads(eng, eng.tensor_tensor(R_T, R_T, K_T, ALU.mult))
            eng.tensor_tensor(s5, R_T, par_over("bonus", HT, T), ALU.mult).then_inc(S("bonus_in"), 1)
            eng.wait_ge(S("decays_made"), 2)
            eng.tensor_tensor(ar[:, :, :, 0, :], v5(s6), v5(s1), ALU.mult)
            next_reads(eng, eng.scalar_tensor_tensor(flat(s4), flat(s4), -1.0, flat(s6), ALU.mult, ALU.mult))
            eng.wait_ge(S("decays_made"), 3)
            eng.tensor_tensor(s4, s4, s2, ALU.mult)
            eng.tensor_tensor(K_T, K_T, s2, ALU.mult).then_inc(S("wkv_operands"), 1)
            eng.wait_ge(S("bonus_sum"), HT)
            eng.tensor_tensor(R_T, V_T, ps[:, 0:4, 0:T], ALU.mult).then_inc(S("bonus_made"), 1)
            eng.wait_ge(S("wkv0_loaded"), 16)
            eng.wait_ge(S("shift_stored"), 16)
            eng.memset(state[:, :, :], 0.0).then_inc(S("state_made"), 1)
            eng.wait_ge(S("chunk_v_stored"), 16)
            for g in range(3):
                wkv_group_dve(eng, g)
            eng.wait_ge(S("gn_mean"), HT)
            next_reads(eng, eng.scalar_tensor_tensor(s1, ps[:, 0:4, 0:T], -1.0 / 64, s1, ALU.mult, ALU.add))
            eng.tensor_tensor(s5, s1, s1, ALU.mult).then_inc(S("gn_sq"), 1)
            eng.wait_ge(S("gn_root"), HT)
            next_reads(eng, eng.reciprocal(s5, s5))
            eng.tensor_tensor(s1, s1, s5, ALU.mult).then_inc(S("gn_scaled"), 1)
            eng.wait_ge(S("gn_affine"), HT)
            next_reads(eng, eng.tensor_tensor(s1, s1, R_T, ALU.add))
            eng.wait_ge(S("gate_up"), HT)
            eng.tensor_tensor(s1, s1, ps[:, 0:4, 0:T], ALU.mult).then_inc(S("ya_made"), 1)
            eng.wait_ge(S("y_hi"), 2)
            eng.tensor_tensor(h_lo[:, 0:4, :], s1, h_hi[:, 0:4, :], ALU.subtract).then_inc(S("y_lo"), 1)

        sq_gv = take(G0 + 6144, HT, T)

        def mix0_pe(eng):
            eng.wait_ge(S("small_loaded"), 16 * 8)
            norm_pe(eng, 0)
            eng.wait_ge(S("norm_lo"), 2)
            project_pe(eng, "in0", AT_IN0, IN0_CHUNKS)
            eng.wait_ge(S("in0_taken"), 2 * IN0_CHUNKS)
            eng.wait_ge(S("lora_in"), 2)
            for j in range(HT):
                eng.matmul(ps[:, j, 0:T], lora[0:64, 0, P * j:P * j + P], xs[0:64, 12, :], start=True, stop=True).then_inc(S("lora_done"), 1)
            for j in range(HT):
                eng.matmul(ps[:, 4 + j, 0:T], lora[64:128, 0, P * j:P * j + P], xs[64:128, 12, :], start=True, stop=True).then_inc(S("lora_done"), 1)
            eng.wait_ge(S("decay_sig"), HT)
            for j in range(HT):
                mm = eng.matmul(ps[:, 0, 0:T], ones, gv[:, j, :], start=(j == 0), stop=(j == HT - 1))
            mm.then_inc(S("sgu_mean"), 1)
            eng.wait_ge(S("sgu_sq"), 1)
            for j in range(HT):
                mm = eng.matmul(ps[:, 1, 0:T], ones, sq_gv[:, j, :], start=(j == 0), stop=(j == HT - 1))
            mm.then_inc(S("sgu_var"), 1)
            eng.wait_ge(S("vn_made"), 1)
            eng.wait_ge(S("iclr_made"), HT)
            for i, (a, b) in enumerate(((0, 128), (128, 256), (256, 320))):
                for j in range(HT):
                    mm = eng.transpose(ps[0:b - a, 2 + i, P * j:P * j + P], gv[:, j, a:b], ident)
                mm.then_inc(S("vn_turned"), 1)
            eng.wait_ge(S("sgu_masked"), 1)
            eng.wait_ge(S("vn_tok_made"), 3)
            for j in range(HT):
                for i in range(2):
                    eng.matmul(ps[:, 4 + j, P * i:P * i + P], vn_tok[:, i, P * j:P * j + P], sw[:, j, :], start=True, stop=True)
                eng.matmul(ps[:, 4 + j, TP:T], vn_tok[0:TS, 2, P * j:P * j + P], sw8[:, j, :], start=True, stop=True).then_inc(S("gated_sums"), 1)
            eng.wait_ge(S("kk_sq"), 1)
            for j in range(HT):
                eng.matmul(ps[:, j, 0:T], head_ones, s5[:, j, :], start=True, stop=True).then_inc(S("kk_sum"), 1)
            eng.wait_ge(S("bonus_in"), 1)
            for j in range(HT):
                eng.matmul(ps[:, j, 0:T], head_ones, s5[:, j, :], start=True, stop=True).then_inc(S("bonus_sum"), 1)
            eng.wait_ge(S("wkv_operands"), 1)
            eng.wait_ge(S("bonus_made"), 1)
            eng.wait_ge(S("y_lo"), 1)
            for g in range(3):
                wkv_group_pe(eng, g)
            eng.wait_ge(S("y_made"), 5)
            eng.wait_ge(S("sample_state"), 8)
            for j in range(HT):
                eng.matmul(ps[:, j, 0:T], head_ones, s1[:, j, :], start=True, stop=True).then_inc(S("gn_mean"), 1)
            eng.wait_ge(S("gn_sq"), 1)
            for j in range(HT):
                eng.matmul(ps[:, 4 + j, 0:T], head_ones, s5[:, j, :], start=True, stop=True).then_inc(S("gn_var"), 1)
            for j in range(HT):
                eng.matmul(ps[:, j, 0:T], lora[:, 1, P * j:P * j + P], xs[:, 13, :], start=True, stop=True).then_inc(S("gate_up"), 1)
            eng.wait_ge(S("y_lo"), 2)

        def heads():
            return [(h, 64 * (h % 2), h // 2, (h % 2) * HT + h // 2) for h in (0, 2, 4, 6, 1, 3, 5, 7)]

        def parts(g):
            return [(2 * g, 0), (2 * g + 1, 64)] if g < 2 else [(4, 0)]

        def half(bank, par, n=64):
            return ps[:, bank + par, 0:HT * n].rearrange("p (j t) -> p j t", j=HT)

        def wkv_group_pe(eng, g):
            rows = P if g < 2 else 64

            def each(fn):
                for h, ho, j, s in heads():
                    for c, o in parts(g):
                        mm = fn(h, ho, j, s, c, o)
                return mm

            def small(bank, lhs, rhs):
                return each(lambda h, ho, j, s, c, o: eng.matmul(
                    half(bank, h % 2)[o:o + 64, j, :], lhs[o:o + 64, s, :], rhs[o:o + 64, s, :], start=True, stop=True))

            if g:
                eng.wait_ge(S("y_made"), 2 * g)
                eng.wait_ge(S("state_made"), 2 * g + 1)
            each(lambda h, ho, j, s, c, o: eng.matmul(
                half(0, h % 2, 128)[o:o + 64, j, :], s4[ho:ho + 64, j, C * c:C * c + C],
                ar[ho:ho + 64, j, c, :, :].rearrange("p w t -> p (w t)"), start=True, stop=True)).then_inc(S("gram"), 1)
            each(lambda h, ho, j, s, c, o: eng.matmul(
                half(4, h % 2)[o:o + 64, j, :], ar[ho:ho + 64, j, c, 0, :], s4[ho:ho + 64, j, C * c:C * c + C],
                start=True, stop=True)).then_inc(S("gram"), 1)
            each(lambda h, ho, j, s, c, o: eng.matmul(
                half(2, h % 2, 128)[o:o + 64, j, :], K_T[ho:ho + 64, j, C * c:C * c + C],
                ar[ho:ho + 64, j, c, :, :].rearrange("p w t -> p (w t)"), start=True, stop=True)).then_inc(S("gram"), 1)
            a, b = C * parts(g)[0][0], C * parts(g)[0][0] + rows
            for bank, v in ((6, V_T), (7, s4)):
                for j in range(HT):
                    mm = eng.transpose(ps[0:rows, bank, P * j:P * j + P], v[:, j, a:b], ident)
                mm.then_inc(S("turned"), 1)
            n = 3 if g < 2 else 0
            eng.wait_ge(S("diag_made"), g + 1)
            eng.wait_ge(S("gram_kept"), 4 * g + 2)
            small(0, ee, dd).then_inc(S("solve"), 1)
            small(4, dd, ee).then_inc(S("solve"), 1)
            eng.wait_ge(S("gram_kept"), 4 * g + 4)
            for j in range(HT):
                mm = eng.transpose(ps[0:rows, 2, P * j:P * j + P], K_T[:, j, a:b], ident)
            mm.then_inc(S("turned"), 1)
            eng.wait_ge(S("tok_kept"), 3 * g + 2)
            base = SOLVES[g]
            eng.wait_ge(S("solve_kept"), base + 1)
            small(0, qq, d2).then_inc(S("solve"), 1)
            small(6, e2, d2).then_inc(S("solve"), 1)
            small(4, d2, qq).then_inc(S("solve"), 1)
            eng.wait_ge(S("solve_kept"), base + 2)
            small(0, qq, d2).then_inc(S("solve"), 1)
            small(4, d2, qq).then_inc(S("solve"), 1)
            for i, low in enumerate((lo16, lo32, lo64)[:n]):
                eng.wait_ge(S("solve_kept"), base + 3 + 2 * i)
                small(6, low, pp).then_inc(S("solve"), 1)
                eng.wait_ge(S("solve_kept"), base + 4 + 2 * i)
                small(0, qq, d2).then_inc(S("solve"), 1)
                if i < 2:
                    small(4, d2, qq).then_inc(S("solve"), 1)
            eng.wait_ge(S("solve_kept"), base + 3 + 2 * n)
            eng.wait_ge(S("tok_kept"), 3 * g + 3)
            each(lambda h, ho, j, s, c, o: eng.matmul(
                half(6, h % 2)[o:o + 64, j, :], gk_m[o:o + 64, s, 0:64], v_tok[o:o + 64, h, :], start=True, stop=True)).then_inc(S("akv"), 1)
            eng.wait_ge(S("akv_kept"), g + 1)
            for c, o in parts(g):
                if g < 2:
                    eng.wait_ge(S("state_made"), c + 1)
                    eng.wait_ge(S("y_made"), c)
                    for h, ho, j, s in heads():
                        mm = eng.matmul(half(0, h % 2)[o:o + 64, j, :], ar[ho:ho + 64, j, c, 0, :], state[ho:ho + 64, j, :], start=True, stop=True)
                    mm.then_inc(S("a_s"), 1)
                    for h, ho, j, s in heads():
                        mm = eng.matmul(half(4, h % 2)[ho:ho + 64, j, :], state[ho:ho + 64, j, :], ar[ho:ho + 64, j, c, 1, :], start=True, stop=True)
                    mm.then_inc(S("r_s"), 1)
                else:
                    for h, ho, j, s in heads():
                        for b in range(NB):
                            mm = eng.matmul(ps[ho:ho + 64, h % 2, P * j:P * j + P].rearrange("p (w t) -> p w t", w=2)[:, :, NS * b:NS * b + NS],
                                            swkv[ho:ho + 64, j, b, :], ar[ho:ho + 64, j, c, :, NS * b:NS * b + NS], start=True, stop=True)
                    mm.then_inc(S("sample_s"), 1)
                    eng.wait_ge(S("sample_as_kept"), 1)
                    for j in range(HT):
                        mm = eng.transpose(ps[0:TS, 2, P * j:P * j + P], d2_full[:, j, :], ident)
                    mm.then_inc(S("a_s"), 1)
                eng.wait_ge(S("rhs_made"), c + 1)
                for h, ho, j, s in heads():
                    mm = eng.matmul(ps[o:o + 64, 6, 64 * s:64 * s + 64], pp[o:o + 64, s, :], ee[o:o + 64, s, :], start=True, stop=True)
                mm.then_inc(S("q_done"), 1)
                eng.wait_ge(S("q_kept"), c + 1)
                for h, ho, j, s in heads():
                    out = ps[ho:ho + 64, 2, 64 * j:64 * j + 64]
                    eng.matmul(out, e2[o:o + 64, s, :], gb_m[o:o + 64, s, 64:128], start=True, stop=False)
                    mm = eng.matmul(out, v_tok[o:o + 64, h, :], gk_m[o:o + 64, s, 64:128], start=False, stop=True)
                mm.then_inc(S("y_rest"), 1)
                if g < 2:
                    for h, ho, j, s in heads():
                        out = ps[ho:ho + 64, 3, 64 * j:64 * j + 64]
                        eng.matmul(out, b_tok[o:o + 64, h, :], e2[o:o + 64, s, :], start=True, stop=False)
                        mm = eng.matmul(out, k_tok[o:o + 64, h, :], v_tok[o:o + 64, h, :], start=False, stop=True)
                    mm.then_inc(S("state_add"), 1)
                else:
                    for n_, (h, ho, j, s) in enumerate(heads()):
                        eng.wait_ge(S("qe_made"), n_ + 1)
                        eng.wait_ge(S("ve_made"), n_ + 1)
                        bank = SAMPLE_BANKS[n_ % 4]
                        if n_ >= 4:
                            eng.wait_ge(S("sample_state"), n_ - 3)
                        eng.matmul(ps[ho:ho + 64, bank, :], b_tok[0:64, h, :], qe[:, n_ % 2, :], start=True, stop=False)
                        eng.matmul(ps[ho:ho + 64, bank, :], k_tok[0:64, h, :], ve[:, n_ % 2, :], start=False, stop=True)\
                           .then_inc(S("sample_add"), 1)

        SOLVES = (0, 9, 18)
        SAMPLE_BANKS = (4, 5, 6, 7)
        d2_full = take(G0 + 2048 + 512 * 4, HT, TS)

        def wkv_group_act(eng, g):
            rows = P if g < 2 else 64
            for i, (bank, to) in enumerate(((6, v_tok), (7, b_tok), (2, k_tok))):
                eng.wait_ge(S("turned"), 3 * g + i + 1)
                eng.activation(to[0:rows, :, :].rearrange("p h v -> p (h v)"), ps[0:rows, bank, :], ACT.Copy).then_inc(S("tok_kept"), 1)

        def wkv_group_dve(eng, g):
            rows = P if g < 2 else 64
            n = 3 if g < 2 else 0
            base = SOLVES[g]
            mask = const("mask_prompt" if g < 2 else "mask_sample", rows)
            over = lambda m, k: m.unsqueeze(1).broadcast_to((rows, HT, k))
            done0 = sum(per_group(i) for i in range(g))

            def kept(ins_):
                ins_.then_inc(S("solve_kept"), 1)

            def wait_solve(k):
                eng.wait_ge(S("solve"), done0 + k)

            sl = lambda v: v[0:rows, :, :]
            q4 = lambda v, par: v[0:rows, HT * par:HT * par + HT, :]
            eng.wait_ge(S("gram"), 3 * g + 1)
            for par in range(2):
                eng.tensor_tensor(q4(gb_m, par), half(0, par, 128)[0:rows], over(mask, 128), ALU.mult).then_inc(S("gram_kept"), 1)
            eng.wait_ge(S("gram_kept"), 4 * g + 2)
            d8 = const("diag8", rows).unsqueeze(1).broadcast_to((rows, 8, 64))
            eye = const("eye64", rows).unsqueeze(1).broadcast_to((rows, 8, 64))
            next_reads(eng, eng.tensor_tensor(sl(dd), gb_m[0:rows, :, 0:64], d8, ALU.mult))
            eng.wait_ge(S("gram"), 3 * g + 2)
            for par in range(2):
                eng.tensor_tensor(q4(ee, par), half(4, par)[0:rows], over(const("low8", rows), 64), ALU.mult)
                for low, name in ((lo16, "low16"), (lo32, "low32"), (lo64, "low64"))[:n]:
                    eng.tensor_tensor(q4(low, par), half(4, par)[0:rows], over(const(name, rows), 64), ALU.mult)
            eng.tensor_tensor(sl(pp), sl(dd), eye, ALU.add).then_inc(S("diag_made"), 1)
            eng.wait_ge(S("gram"), 3 * g + 3)
            for par in range(2):
                eng.tensor_tensor(q4(gk_m, par), half(2, par, 128)[0:rows], over(mask, 128), ALU.mult).then_inc(S("gram_kept"), 1)
            eng.wait_ge(S("gram_kept"), 4 * g + 4)
            next_reads(eng, eng.tensor_tensor(sl(qq), sl(ee), eye, ALU.add))

            def take2(to, bank, add=None):
                for par in range(2):
                    if add is None:
                        last = eng.tensor_copy(q4(to, par), half(bank, par)[0:rows])
                    else:
                        last = eng.tensor_tensor(q4(to, par), q4(to, par), half(bank, par)[0:rows], ALU.add)
                return last

            wait_solve(1)
            take2(d2, 0)
            wait_solve(2)
            kept(take2(e2, 4))
            wait_solve(5)
            take2(pp, 0, True)
            take2(d2, 6)
            kept(take2(qq, 4, True))
            eng.wait_ge(S("solve_kept"), base + 2)
            wait_solve(7)
            take2(pp, 0, True)
            kept(take2(qq, 4, True))
            at = 7
            for i in range(n):
                eng.wait_ge(S("solve_kept"), base + 3 + 2 * i)
                wait_solve(at + 1)
                kept(take2(d2, 6))
                wait_solve(at + 2 + (i < 2))
                last = take2(pp, 0, True)
                if i < 2:
                    last = take2(qq, 4, True)
                kept(last)
                at += 2 + (i < 2)
            eng.wait_ge(S("akv"), g + 1)
            take2(dd, 6).then_inc(S("akv_kept"), 1)
            eng.wait_ge(S("akv_kept"), g + 1)
            for c, o in parts(g):
                r = slice(o, o + 64)
                y = s1[:, :, C * c:C * c + C]
                if g == 2:
                    eng.wait_ge(S("sample_s"), 1)
                    for par in range(2):
                        ho = 64 * par
                        v = ps[ho:ho + 64, par, :].rearrange("p (j w t) -> p j w t", j=HT, w=2)
                        eng.tensor_copy(d2_full[ho:ho + 64], v[:, :, 0, :])
                        last = eng.tensor_copy(y[ho:ho + 64], v[:, :, 1, :])
                    last.then_inc(S("sample_as_kept"), 1)
                    eng.wait_ge(S("sample_as_kept"), 1)
                eng.wait_ge(S("a_s"), c + 1)
                for par in range(2):
                    src = half(0, par)[r] if g < 2 else ps[r, 2, :].rearrange("p (j w t) -> p j w t", j=HT, w=2)[:, :, par, :]
                    last = eng.tensor_tensor(ee[r, HT * par:HT * par + HT, :], dd[r, HT * par:HT * par + HT, :], src, ALU.add)
                last.then_inc(S("rhs_made"), 1)
                if g < 2:
                    eng.wait_ge(S("r_s"), c + 1)
                    for par in range(2):
                        ho = 64 * par
                        last = eng.tensor_copy(y[ho:ho + 64], half(4, par)[ho:ho + 64])
                    next_reads(eng, last)
                eng.wait_ge(S("q_done"), c + 1)
                eng.tensor_copy(e2[r, :, :], ps[r, 6, :].rearrange("p (s v) -> p s v", s=8)).then_inc(S("q_kept"), 1)
                eng.wait_ge(S("y_rest"), c + 1)
                eng.tensor_tensor(y, y, ps[:, 2, 0:256].rearrange("p (j t) -> p j t", j=HT), ALU.add).then_inc(S("y_made"), 1)
                if g < 2:
                    eng.wait_ge(S("state_add"), c + 1)
                    next_reads(eng, eng.tensor_tensor(state[:, :, :], state[:, :, :], ps[:, 3, 0:256].rearrange("p (j t) -> p j t", j=HT), ALU.add))
                    eng.tensor_tensor(state[:, :, :], state[:, :, :], w_end[:, :, c:c + 1].broadcast_to((P, HT, 64)), ALU.mult)\
                       .then_inc(S("state_made"), 1)
                    eng.wait_ge(S("state_made"), c + 2)
            if g == 2:
                own = const("own_batch", TS).unsqueeze(2).broadcast_to((TS, NB, 64))
                eng.wait_ge(S("q_kept"), 5)

                def spread(n_):
                    h, ho, j, s = heads()[n_]
                    if n_ >= 2:
                        eng.wait_ge(S("sample_add"), n_ - 1)
                    eng.tensor_tensor(qe[:, n_ % 2, :].rearrange("p (b v) -> p b v", b=NB), e2[0:TS, s, :].unsqueeze(1).broadcast_to((TS, NB, 64)),
                                      own, ALU.mult).then_inc(S("qe_made"), 1)

                spread(0)
                spread(1)
                for n_, (h, ho, j, s) in enumerate(heads()):
                    eng.wait_ge(S("sample_add"), n_ + 1)
                    if n_ + 2 < 8:
                        spread(n_ + 2)
                    v = swkv[ho:ho + 64, j, :, :]
                    bank = SAMPLE_BANKS[n_ % 4]
                    next_reads(eng, eng.tensor_tensor(v, v, ps[ho:ho + 64, bank, :].rearrange("p (b v) -> p b v", b=NB), ALU.add))
                    eng.tensor_tensor(v, v, w_end[ho:ho + 64, j, 4:12].unsqueeze(2).broadcast_to((64, NB, 64)), ALU.mult)\
                       .then_inc(S("sample_state"), 1)

        def wkv_group_pool(eng):
            own = const("own_batch", TS).unsqueeze(2).broadcast_to((TS, NB, 64))
            eng.wait_ge(S("sample_s"), 1)
            eng.wait_ge(S("tok_kept"), 9)
            for n_, (h, ho, j, s) in enumerate(heads()):
                if n_ >= 2:
                    eng.wait_ge(S("sample_add"), n_ - 1)
                eng.tensor_tensor(ve[:, n_ % 2, :].rearrange("p (b v) -> p b v", b=NB), v_tok[0:TS, h, :].unsqueeze(1).broadcast_to((TS, NB, 64)),
                                  own, ALU.mult).then_inc(S("ve_made"), 1)

        def per_group(g):
            return 7 + (8 if g < 2 else 0)


        def mix0_pool(eng):
            eng.wait_ge(S("small_loaded"), 16 * 8)
            for i in range(A_TILES):
                eng.wait_ge(S("ring_filled"), i + 1)
                v = p_ring[:, i % 4, :]
                eng.tensor_copy(shift_out[:, i, 0:1], v[:, 256:257])
                eng.tensor_copy(shift_out[:, i, 1:9], v[:, 257:329].rearrange("p (b s) -> p b s", b=NB)[:, :, NS]).then_inc(S("shift_kept"), 1)


        KV_RING = 4
        kv = take(5760, KV_RING, 2048)
        bias_p, bias_s = take(13952, 8, 384), take(17024, 1280)
        lru_w = take(18304, 2, HT, P)
        conv0, lru0 = take(19328, HT, NB, 3), take(19424, HT, NB)
        count_p, count_s = take(19456, 384), take(19840, 1280)
        XW = 3 + TP + NB * (3 + NS)
        xe = take(19456, HT, XW)
        lru_m = take(20844, HT, T)
        lru_t = take(19456, HT, T)
        q1, k1, v1, gy = (take(1280 * i, HT, T) for i in range(4))
        xc, lru_a, lru_i = h32[:, 0:4, :], h32[:, 4:8, :], hid[:, :, :]
        v1_tok = take(3840, 3, 512)
        score_s = take(18304, 2, 1088)
        pt_s = h32[:, :, :].rearrange("p a b -> p (a b)")[:, 0:2304].rearrange("p (a b c) -> p a b c", a=2, b=9)
        o_masked = take(20480, 512)
        qx = hid[:, :, :].rearrange("p a b -> p (a b)")[:, 0:1024].rearrange("p (r b j n) -> p r b j n", r=2, b=2, j=HT)
        score_p = take(20992, 2, 384)
        pt_p = (take(5376, 384), take(21760, 384))
        conv_out = state_flat[:, 0:108].rearrange("p (a b) -> p a b", a=HT)
        lru_out = state_flat[:, 108:144].rearrange("p (a b) -> p a b", a=HT)
        stat_p = state_flat[:, 144:156].rearrange("p (r w n) -> p r w n", r=2, w=3)
        stat_s = state_flat[:, 156:164].rearrange("p (r w) -> p r w", r=2)
        lam = state_flat[:, 164:192].rearrange("p (w j) -> p w j", w=7)

        KV_UNITS = [(what, b, half) for what, pair in (("k", 0), ("k", 1), ("v", 0), ("k", 2), ("v", 1), ("k", 3), ("v", 2), ("v", 3))
                    for b in (2 * pair, 2 * pair + 1) for half in (0, 1)]
        kv_at = {u: n for n, u in enumerate(KV_UNITS)}

        def load_kv(eng, n):
            what, b, half = KV_UNITS[n]
            if n >= KV_RING:
                eng.wait_ge(S("kv_used"), n - KV_RING + 1)
            eng.dma_start(kv[:, n % KV_RING, :], ins[f"cache_{what}"][2 * b + half]).then_inc(S(f"kv_loaded{n % KV_RING}"), 16)

        def kv_ready(eng, what, b, half):
            n = kv_at[what, b, half]
            eng.wait_ge(S(f"kv_loaded{n % KV_RING}"), 16 * (n // KV_RING + 1))
            return kv[:, n % KV_RING, :].rearrange("p (a b) -> p a b", a=4)

        def xe_parts(j, lead):
            v = xe[:, j, :]
            s = v[:, 3 + TP:XW].rearrange("p (b s) -> p b s", b=NB)
            return v[:, 3 - lead:3 - lead + TP], s[:, :, 3 - lead:3 - lead + NS]

        def mix1_act(eng):
            split_hi(eng, AT_IN1)
            split_hi(eng, AT_IN1 + 1)
            eng.wait_ge(S("lam_abs"), 1)
            eng.activation(lam[:, 1, :], lam[:, 1, :], ACT.Exp, scale=-1.0).then_inc(S("lam_logs"), 1)
            eng.wait_ge(S("lam_u"), 1)
            eng.activation(lam[:, 3, :], lam[:, 2, :], ACT.Ln).then_inc(S("lam_logs"), 1)
            eng.wait_ge(S("down_added"), 2 * HT * NE)
            norm_act(eng, 2, True)
            eng.wait_ge(S("biases_made"), 1)
            eng.wait_ge(S("xe_lead"), 1)
            for i in range(2 * IN1_CHUNKS):
                eng.wait_ge(S("tile_done"), tile(AT_IN1, i))
                src, j = ps[:, i % 8, 0:T], i % HT
                if i < 4:
                    eng.activation(gy[:, j, :], src, ACT.Gelu_apprx_tanh).then_inc(S("in1_taken"), 1)
                elif i < 8:
                    a, b = xe_parts(j, 0)
                    pa, pb = prompt_sample(src)
                    eng.activation(a, pa, ACT.Copy)
                    eng.activation(b, pb, ACT.Copy).then_inc(S("in1_taken"), 1)
                elif i < 12:
                    eng.activation(q1[:, j, :], src, ACT.Copy, scale=0.125).then_inc(S("in1_taken"), 1)
                else:
                    eng.activation((k1 if i < 16 else v1)[:, j, :], src, ACT.Copy).then_inc(S("in1_taken"), 1)
                if i % 2 and i // 2 + 2 < IN1_CHUNKS:
                    split_hi(eng, AT_IN1 + i // 2 + 2)
            for j in range(HT):
                eng.wait_ge(S("lru_gate"), j + 1)
                eng.activation(lru_a[:, j, :], ps[:, j, 0:T], ACT.Sigmoid, bias=par("rgate_b", j)).then_inc(S("lru_sig"), 1)
            for j in range(HT):
                eng.wait_ge(S("lru_gate"), HT + j + 1)
                eng.activation(lru_i[:, j, :], ps[:, 4 + j, 0:T], ACT.Sigmoid, bias=par("igate_b", j)).then_inc(S("lru_sig"), 1)
            eng.wait_ge(S("log_a"), 1)
            eng.activation(lru_m, lru_a, ACT.Tanh, scale=-1.0).then_inc(S("lru_exps"), 1)
            eng.activation(lru_a, lru_a, ACT.Exp).then_inc(S("lru_exps"), 1)
            eng.wait_ge(S("lru_square"), 1)
            eng.activation(lru_m, lru_m, ACT.Sqrt).then_inc(S("lru_mult"), 1)
            eng.wait_ge(S("yc_made"), 1)
            eng.activation(h_hi[:, 0:4, :], gy, ACT.Copy).then_inc(S("y_hi"), 1)
            eng.wait_ge(S("y_lo"), 3)
            for i in range(3):
                n = P if i < 2 else TS
                eng.wait_ge(S("v1_turned"), i + 1)
                eng.activation(v1_tok[0:n, i, :], ps[0:n, 5 + i, :], ACT.Copy).then_inc(S("v1_tok_made"), 1)

            def prompt_exp(h):
                r = h % 2
                eng.wait_ge(S("p_max"), h + 1)
                eng.activation(score_p[:, r, 0:P], score_p[:, r, 0:P], ACT.Exp, bias=stat_p[:, r, 0, 0:1], accum_out=stat_p[:, r, 1, 0:1])
                eng.activation(score_p[:, r, P:384], score_p[:, r, P:384], ACT.Exp, bias=stat_p[:, r, 0, 1:2], accum_out=stat_p[:, r, 1, 1:2])\
                   .then_inc(S("p_exp"), 1)

            def prompt_turned(h):
                eng.wait_ge(S("p_turned"), h + 1)
                eng.activation(pt_p[h % 2], ps[:, 2 + h % 2, 0:384], ACT.Copy).then_inc(S("p_tok_made"), 1)

            for h in range(9):
                if h < 8:
                    prompt_exp(h)
                if h >= 1:
                    prompt_turned(h - 1)

            def sample_exp(p):
                r = p % 2
                eng.wait_ge(S("s_max"), p + 1)
                eng.activation(score_s[:, r, :], score_s[:, r, :], ACT.Exp, bias=stat_s[:, r, 1:2], accum_out=stat_s[:, r, 2:3])\
                   .then_inc(S("s_exp"), 1)

            def sample_turned(p):
                r = p % 2
                for n, (a, b, rows) in enumerate(((0, 4, P), (4, 8, P), (8, 9, 64))):
                    eng.wait_ge(S("s_turned"), 3 * p + n + 1)
                    eng.activation(pt_s[0:rows, r, a:b, :].rearrange("p a b -> p (a b)"), ps[0:rows, 6 + n % 2, 0:P * (b - a)], ACT.Copy)\
                       .then_inc(S("s_tok_made"), 1)

            for p in range(5):
                if p < 4:
                    sample_exp(p)
                if p >= 1:
                    sample_turned(p - 1)
            eng.wait_ge(S("attn_out"), 2 + 4)
            eng.activation(h_hi[:, 4:8, :], q1, ACT.Copy).then_inc(S("y_hi"), 1)

        def mix1_dve(eng):
            split_lo(eng, AT_IN1)
            split_lo(eng, AT_IN1 + 1)
            at = PCOL["lambda"][0]
            l = params[:, at:at + HT]
            eng.wait_ge(S("states_stored"), 32)
            next_reads(eng, eng.tensor_scalar(lam[:, 0, :], l, -1.0, None, ALU.mult))
            eng.tensor_tensor(lam[:, 1, :], lam[:, 0, :], l, ALU.max).then_inc(S("lam_abs"), 1)
            eng.wait_ge(S("lam_logs"), 1)
            eng.tensor_scalar(lam[:, 2, :], lam[:, 1, :], 1.0, None, ALU.add).then_inc(S("lam_u"), 1)
            eng.wait_ge(S("lam_u"), 1)
            next_reads(eng, eng.tensor_scalar(lam[:, 4, :], lam[:, 2, :], 1.0, None, ALU.subtract))
            next_reads(eng, eng.tensor_tensor(lam[:, 4, :], lam[:, 1, :], lam[:, 4, :], ALU.subtract))
            next_reads(eng, eng.reciprocal(lam[:, 5, :], lam[:, 2, :]))
            next_reads(eng, eng.tensor_tensor(lam[:, 4, :], lam[:, 4, :], lam[:, 5, :], ALU.mult))
            eng.wait_ge(S("lam_logs"), 2)
            next_reads(eng, eng.tensor_tensor(lam[:, 4, :], lam[:, 4, :], lam[:, 3, :], ALU.add))
            next_reads(eng, eng.tensor_scalar(lam[:, 0, :], lam[:, 0, :], 0.0, None, ALU.max))
            next_reads(eng, eng.tensor_tensor(lam[:, 4, :], lam[:, 4, :], lam[:, 0, :], ALU.add))
            next_reads(eng, eng.tensor_scalar(lam[:, 6, :], lam[:, 4, :], -8.0, None, ALU.mult))
            norm_dve(eng, 2, "norm_mix1", True)
            eng.wait_ge(S("biases_made"), 1)
            eng.wait_ge(S("lru_loaded"), 48)
            eng.memset(xe[:, :, 0:3], 0.0)
            for j in range(HT):
                last = eng.tensor_copy(xe[:, j, 3 + TP:XW].rearrange("p (b s) -> p b s", b=NB)[:, :, 0:3], conv0[:, j, :, :])
            last.then_inc(S("xe_lead"), 1)
            eng.wait_ge(S("norm_lo"), 6)
            split_lo(eng, AT_IN1 + 2)
            split_lo(eng, AT_IN1 + 3)
            split_lo(eng, AT_IN1 + 4)
            for j in range(HT):
                eng.wait_ge(S("in1_taken"), 4 + j + 1)
                eng.wait_ge(S("xe_lead"), 1)
                to = prompt_sample(xc[:, j, :])
                for tap in range(4):
                    src = xe_parts(j, 3 - tap)
                    for n in range(2):
                        if tap == 0:
                            last = eng.tensor_scalar(to[n], src[n], par("conv_w", j), par("conv_b", j), ALU.mult, ALU.add)
                        else:
                            last = eng.scalar_tensor_tensor(to[n], src[n], par("conv_w", HT * tap + j), to[n], ALU.mult, ALU.add)
                    next_reads(eng, last)
                if j % 2:
                    split_lo(eng, AT_IN1 + 5 + j // 2)
            eng.tensor_copy(conv_out[:, :, 0:3], xe[:, :, TP:TP + 3])
            for j in range(HT):
                last = eng.tensor_copy(conv_out[:, j, 3:27].rearrange("p (b s) -> p b s", b=NB),
                                       xe[:, j, 3 + TP:XW].rearrange("p (b s) -> p b s", b=NB)[:, :, NS:NS + 3])
            last.then_inc(S("xc_made"), 1)
            for c in range(7, IN1_CHUNKS):
                split_lo(eng, AT_IN1 + c)
            eng.wait_ge(S("lru_sig"), HT)
            for j in range(HT):
                last = eng.tensor_scalar(lru_a[:, j, :], lru_a[:, j, :], lam[:, 6, j:j + 1], None, ALU.mult)
            last.then_inc(S("log_a"), 1)
            eng.wait_ge(S("lru_sig"), 2 * HT)
            next_reads(eng, eng.tensor_tensor(lru_i, lru_i, xc, ALU.mult))
            eng.wait_ge(S("lru_exps"), 2)
            next_reads(eng, eng.tensor_tensor(lru_t, lru_a, lru_a, ALU.mult))
            eng.scalar_tensor_tensor(flat(lru_m), flat(lru_t), 1.0, flat(lru_m), ALU.add, ALU.mult).then_inc(S("lru_square"), 1)
            eng.wait_ge(S("lru_mult"), 1)
            next_reads(eng, eng.memset(lru_m[:, :, 0:1], 1.0))
            next_reads(eng, eng.tensor_tensor(lru_m, lru_m, lru_i, ALU.mult))
            starts = lambda v: v[:, :, TP:T].rearrange("p j (b s) -> p j b s", b=NB)[:, :, :, 0]
            next_reads(eng, eng.tensor_tensor(lru0, lru0, starts(lru_a), ALU.mult))
            next_reads(eng, eng.tensor_tensor(starts(lru_m), starts(lru_m), lru0, ALU.add))
            next_reads(eng, eng.memset(starts(lru_a), 0.0))
            for j in range(HT):
                last = eng.tensor_tensor_scan(lru_i[:, j, :], lru_a[:, j, :], lru_m[:, j, :], 0.0, ALU.mult, ALU.add)
            next_reads(eng, last)
            eng.tensor_copy(lru_out[:, :, 0:1], lru_i[:, :, TP - 1:TP])
            eng.tensor_copy(lru_out[:, :, 1:9], lru_i[:, :, TP:T].rearrange("p j (b s) -> p j b s", b=NB)[:, :, :, NS - 1])\
               .then_inc(S("lru_kept"), 1)
            eng.tensor_tensor(gy, gy, lru_i, ALU.mult).then_inc(S("yc_made"), 1)
            eng.wait_ge(S("y_hi"), 3)
            eng.tensor_tensor(h_lo[:, 0:4, :], gy, h_hi[:, 0:4, :], ALU.subtract).then_inc(S("y_lo"), 1)
            eng.wait_ge(S("y_lo"), 3)
            eng.memset(v1_tok[64:128, 2, :], 0.0)
            for r in range(2):
                last = eng.memset(pt_s[64:128, r, 8, :], 0.0)
            last.then_inc(S("pads_zeroed"), 1)

            def prompt_max(h):
                r = h % 2
                eng.wait_ge(S("p_scores"), h + 1)
                if h >= 2:
                    eng.wait_ge(S("p_turned"), h - 1)
                next_reads(eng, eng.tensor_tensor(score_p[:, r, :], ps[:, r, 0:384], bias_p[:, h, :], ALU.add))
                eng.tensor_reduce(stat_p[:, r, 2, 0:1], score_p[:, r, 0:P], AX, ALU.max)
                next_reads(eng, eng.tensor_reduce(stat_p[:, r, 2, 1:2], score_p[:, r, P:384], AX, ALU.max))
                eng.tensor_scalar(stat_p[:, r, 0, :], stat_p[:, r, 2, :], -1.0, None, ALU.mult).then_inc(S("p_max"), 1)

            def prompt_norm(h):
                r = h % 2
                eng.wait_ge(S("p_exp"), h + 1)
                next_reads(eng, eng.reciprocal(stat_p[:, r, 2, :], stat_p[:, r, 1, :]))
                eng.tensor_scalar(score_p[:, r, 0:P], score_p[:, r, 0:P], stat_p[:, r, 2, 0:1], None, ALU.mult)
                eng.tensor_scalar(score_p[:, r, P:384], score_p[:, r, P:384], stat_p[:, r, 2, 1:2], None, ALU.mult)\
                   .then_inc(S("p_normed"), 1)

            for h in range(9):
                if h < 8:
                    prompt_max(h)
                if h >= 1:
                    prompt_norm(h - 1)
            for j in range(0, HT, 2):
                eng.wait_ge(S("p_out"), 2 * j + 4)
                eng.tensor_copy(q1[:, j:j + 2, 0:TP], ps[:, 4 + j // 2, :].rearrange("p (j t) -> p j t", j=2)).then_inc(S("attn_out"), 1)

            def sample_queries(p):
                r = p % 2
                if p >= 2:
                    eng.wait_ge(S("s_scores"), p - 1)
                for bb in range(2):
                    a = TP + NS * (2 * p + bb)
                    last = eng.tensor_tensor(qx[:, r, bb, :, :].rearrange("p j (h q) -> p j h q", h=8),
                                             q1[:, :, a:a + NS].unsqueeze(2).broadcast_to((P, HT, 8, NS)),
                                             const("head_rows").rearrange("p (j h) -> p j h", j=HT).unsqueeze(3).broadcast_to((P, HT, 8, NS)),
                                             ALU.mult)
                last.then_inc(S("qx_made"), 1)

            def sample_max(p):
                r = p % 2
                eng.wait_ge(S("s_scores"), p + 1)
                if p >= 2:
                    eng.wait_ge(S("s_turned"), 3 * (p - 1))
                eng.tensor_tensor(score_s[:, r, 0:1024].rearrange("p (a b) -> p a b", a=2), ps[:, 0:2, :],
                                  bias_s[:, 0:1024].rearrange("p (a b) -> p a b", a=2), ALU.add)
                last = eng.tensor_tensor(score_s[:, r, 1024:1088], ps[:, 2, 0:TS], bias_s[:, 1024 + TS * p:1024 + TS * p + TS], ALU.add)
                last.then_inc(S("s_biased"), 1)
                eng.wait_ge(S("s_biased"), p + 1)
                next_reads(eng, eng.tensor_reduce(stat_s[:, r, 0:1], score_s[:, r, :], AX, ALU.max))
                eng.tensor_scalar(stat_s[:, r, 1:2], stat_s[:, r, 0:1], -1.0, None, ALU.mult).then_inc(S("s_max"), 1)

            def sample_out(p):
                r = p % 2
                eng.wait_ge(S("s_exp"), p + 1)
                next_reads(eng, eng.reciprocal(stat_s[:, r, 3:4], stat_s[:, r, 2:3]))
                eng.wait_ge(S("s_values"), p + 1)
                eng.scalar_tensor_tensor(o_masked.rearrange("p (h e) -> p h e", h=8), ps[:, 3 + r, :].rearrange("p (h e) -> p h e", h=8),
                                         stat_s[:, r, 3:4], const("own_head").unsqueeze(2).broadcast_to((P, 8, 64)), ALU.mult, ALU.mult)\
                   .then_inc(S("s_masked"), 1)
                eng.wait_ge(S("s_out"), p + 1)
                eng.tensor_copy(q1[:, :, TP + 16 * p:TP + 16 * p + 16], ps[:, 5, 0:64].rearrange("p (j n) -> p j n", j=HT))\
                   .then_inc(S("attn_out"), 1)

            sample_queries(0)
            sample_queries(1)
            for p in range(5):
                if p < 4:
                    sample_max(p)
                    if p + 2 < 4:
                        sample_queries(p + 2)
                if p >= 1:
                    sample_out(p - 1)
            eng.wait_ge(S("y_hi"), 4)
            eng.tensor_tensor(h_lo[:, 4:8, :], q1, h_hi[:, 4:8, :], ALU.subtract).then_inc(S("y_lo"), 1)

        def mix1_pe(eng):
            norm_pe(eng, 2)
            eng.wait_ge(S("norm_lo"), 6)
            project_pe(eng, "in1", AT_IN1, IN1_CHUNKS)
            eng.wait_ge(S("in1_taken"), 2 * IN1_CHUNKS)
            eng.wait_ge(S("xc_made"), 1)
            for n in range(2):
                for j in range(HT):
                    eng.matmul(ps[:, HT * n + j, 0:T], lru_w[:, n, j, :], xc[:, j, :], start=True, stop=True).then_inc(S("lru_gate"), 1)
            eng.wait_ge(S("lru_sig"), 2 * HT)
            for i, (a, b) in enumerate(((0, 128), (128, 256), (256, 320))):
                for j in range(HT):
                    mm = eng.transpose(ps[0:b - a, 5 + i, P * j:P * j + P], v1[:, j, a:b], ident)
                mm.then_inc(S("v1_turned"), 1)

            def prompt_scores(h):
                o, j = 64 * (h % 2), h // 2
                if h >= 2:
                    eng.wait_ge(S("p_max"), h - 1)
                eng.matmul(ps[:, h % 2, 0:P], q1[o:o + 64, j, 0:P], k1[o:o + 64, j, 0:P], start=True, stop=True)
                eng.matmul(ps[:, h % 2, P:384], q1[o:o + 64, j, P:TP], k1[o:o + 64, j, 0:TP], start=True, stop=True).then_inc(S("p_scores"), 1)

            def prompt_turn(h):
                eng.wait_ge(S("p_normed"), h + 1)
                if h >= 2:
                    eng.wait_ge(S("p_tok_made"), h - 1)
                for i in range(3):
                    mm = eng.transpose(ps[:, 2 + h % 2, P * i:P * i + P], score_p[:, h % 2, P * i:P * i + P], ident)
                mm.then_inc(S("p_turned"), 1)

            def prompt_values(h):
                o, j = 64 * (h % 2), h // 2
                if h == 0:
                    eng.wait_ge(S("v1_tok_made"), 3)
                eng.wait_ge(S("p_tok_made"), h + 1)
                out, pt = ps[o:o + 64, 4 + j // 2, TP * (j % 2):TP * (j % 2) + TP], pt_p[h % 2]
                eng.matmul(out[:, 0:P], v1_tok[:, 0, 64 * h:64 * h + 64], pt[:, 0:P], start=True, stop=True)
                eng.matmul(out[:, P:TP], v1_tok[:, 0, 64 * h:64 * h + 64], pt[:, P:TP], start=True, stop=False)
                eng.matmul(out[:, P:TP], v1_tok[:, 1, 64 * h:64 * h + 64], pt[:, TP:384], start=False, stop=True).then_inc(S("p_out"), 1)

            for h in range(10):
                if h < 8:
                    prompt_scores(h)
                if 1 <= h < 9:
                    prompt_turn(h - 1)
                if h >= 2:
                    prompt_values(h - 2)

            def sample_scores(p):
                r = p % 2
                eng.wait_ge(S("qx_made"), p + 1)
                if p:
                    eng.wait_ge(S("s_biased"), p)
                for bb in range(2):
                    o = 64 * bb
                    for half in range(2):
                        keys = kv_ready(eng, "k", 2 * p + bb, half)
                        for j in range(HT):
                            mm = eng.matmul(ps[o:o + 64, half, :], qx[:, r, bb, j, :], keys[:, j, :], start=(j == 0), stop=(j == HT - 1))
                        mm.then_inc(S("kv_used"), 1)
                    for j in range(HT):
                        mm = eng.matmul(ps[o:o + 64, 2, 0:TS], qx[:, r, bb, j, :], k1[:, j, TP:T], start=(j == 0), stop=(j == HT - 1))
                mm.then_inc(S("s_scores"), 1)

            def sample_values(p):
                r = p % 2
                eng.wait_ge(S("s_exp"), p + 1)
                for n, (a, b, rows) in enumerate(((0, 4, P), (4, 8, P), (8, 9, 64))):
                    if 3 * p + n >= 2:
                        eng.wait_ge(S("s_tok_made"), 3 * p + (0, 0, 1)[n])
                    for i in range(a, b):
                        mm = eng.transpose(ps[0:rows, 6 + n % 2, P * (i - a):P * (i - a) + P], score_s[:, r, P * i:P * i + rows], ident)
                    mm.then_inc(S("s_turned"), 1)
                eng.wait_ge(S("s_tok_made"), 3 * p + 3)
                eng.wait_ge(S("pads_zeroed"), 1)
                if p >= 2:
                    eng.wait_ge(S("s_masked"), p - 1)
                for bb in range(2):
                    o = 64 * bb
                    for half in range(2):
                        values = kv_ready(eng, "v", 2 * p + bb, half)
                        for i in range(4):
                            mm = eng.matmul(ps[o:o + 64, 3 + r, :], pt_s[:, r, 4 * half + i, o:o + 64], values[:, i, :],
                                            start=(half == 0 and i == 0), stop=False)
                        mm.then_inc(S("kv_used"), 1)
                    mm = eng.matmul(ps[o:o + 64, 3 + r, :], pt_s[:, r, 8, o:o + 64], v1_tok[:, 2, :], start=False, stop=True)
                mm.then_inc(S("s_values"), 1)
                eng.wait_ge(S("s_masked"), p + 1)
                if p:
                    eng.wait_ge(S("attn_out"), 2 + p)
                for j in range(HT):
                    mm = eng.matmul(ps[:, 5, 16 * j:16 * j + 16], o_masked[:, P * j:P * j + P], const("same_query"), start=True, stop=True)
                mm.then_inc(S("s_out"), 1)

            eng.wait_ge(S("attn_out"), 2)
            for p in range(5):
                if p < 4:
                    sample_scores(p)
                if p >= 1:
                    sample_values(p - 1)
            eng.wait_ge(S("y_lo"), 3)
            eng.wait_ge(S("y_lo"), 4)
            project_pe(eng, "out1", AT_OUT1, OUT_CHUNKS)

        def mix1_pool(eng):
            eng.wait_ge(S("bias_loaded"), 64)
            for h in range(8):
                eng.tensor_tensor(bias_p[:, h, :], bias_p[:, h, :], count_p, ALU.add)
            eng.tensor_tensor(bias_s, bias_s, count_s, ALU.add).then_inc(S("biases_made"), 1)

        @block.sync
        def _(eng):
            eng.dma_start(xt[:, :, :], ins["x"]).then_inc(S("x_loaded"), 16)
            load_chunk(eng, 0)
            for to, name in ((consts[:, :], "consts"), (params[:, :], "params"), (router[:, :, :, :], "router"),
                             (shift0, "shift0"), (lora, "lora"), (sw, "sgu_w"), (sw8, "sgu_w8")):
                eng.dma_start(to, ins[name]).then_inc(S("small_loaded"), 16)
            eng.dma_start(sbias, ins["sgu_bias"].broadcast_to((P, HT, T))).then_inc(S("small_loaded"), 16)
            eng.dma_start(swkv, ins["wkv0"]).then_inc(S("wkv0_loaded"), 16)
            for c in range(1, AT_MOE0 + 6):
                load_chunk(eng, c)
            eng.wait_ge(S("out0_taken"), 1)
            eng.wait_ge(S("states_stored"), 32)
            for to, name in ((bias_p, "bias_prompt"), (bias_s, "bias_sample"), (count_p, "count_prompt"), (count_s, "count_sample")):
                eng.dma_start(to, ins[name]).then_inc(S("bias_loaded"), 16)
            for to, name in ((lru_w, "lru_gates"), (conv0, "conv0"), (lru0, "lru0")):
                eng.dma_start(to, ins[name]).then_inc(S("lru_loaded"), 16)
            for n in range(KV_RING):
                load_kv(eng, n)
            with eng.Fori(0, NE - 1) as it:
                for c in range(6, 12):
                    load_chunk(eng, AT_MOE0 + c, it)
            for c in range(AT_IN1, AT_OUT1 + RAW_RING):
                load_chunk(eng, c)
            for n in range(KV_RING, len(KV_UNITS)):
                load_kv(eng, n)
            for c in range(AT_OUT1 + RAW_RING, AT_MOE1 + 6):
                load_chunk(eng, c)
            with eng.Fori(0, NE - 1) as it:
                for c in range(6, 12):
                    load_chunk(eng, AT_MOE1 + c, it)
            for q in range(2):
                eng.wait_ge(S("norm_h"), 4 * KT + 4 * q + 4)
                eng.dma_start(outs["y"][:, 4 * q:4 * q + 4, :], h32[:, 4 * q:4 * q + 4, :]).then_inc(S("y_stored"), 16)
            eng.wait_ge(S("y_stored"), 32)

        @block.scalar
        def _(eng):
            mix0_act(eng)
            out_proj_act(eng, AT_OUT0)
            eng.wait_ge(S("out0_taken"), KT)
            moe_act(eng, 0, AT_MOE0)
            mix1_act(eng)
            out_proj_act(eng, AT_OUT1)
            eng.wait_ge(S("out1_taken"), KT)
            eng.wait_ge(S("rows_stored"), 64)
            moe_act(eng, 1, AT_MOE1)
            eng.wait_ge(S("down_added"), 4 * HT * NE)
            norm_act(eng, 4, False)

        @block.vector
        def _(eng):
            mix0_dve(eng)
            out_proj_dve(eng, "out0", AT_OUT0)
            moe_dve(eng, 0, AT_MOE0)
            mix1_dve(eng)
            out_proj_dve(eng, "out1", AT_OUT1)
            moe_dve(eng, 1, AT_MOE1)
            norm_dve(eng, 4, "norm_final", False)

        @block.tensor
        def _(eng):
            mix0_pe(eng)
            project_pe(eng, "out0", AT_OUT0, OUT_CHUNKS)
            moe_pe(eng, 0, AT_MOE0)
            mix1_pe(eng)
            moe_pe(eng, 1, AT_MOE1)
            norm_pe(eng, 4)

        @block.gpsimd
        def _(eng):
            mix0_pool(eng)
            eng.wait_ge(S("vn_made"), 1)
            eng.dma_start(outs["chunk_v"], gv[:, :, TP:T]).then_inc(S("chunk_v_stored"), 16)
            eng.wait_ge(S("shift_kept"), A_TILES)
            eng.dma_start(outs["shift"], shift_out).then_inc(S("shift_stored"), 16)
            wkv_group_pool(eng)
            eng.wait_ge(S("state_made"), 5)
            eng.dma_start(outs["wkv_p"], state[:, :, :]).then_inc(S("states_stored"), 16)
            eng.wait_ge(S("sample_state"), 8)
            eng.dma_start(outs["wkv_s"], swkv).then_inc(S("states_stored"), 16)
            mix1_pool(eng)
            eng.wait_ge(S("in1_taken"), 2 * IN1_CHUNKS)
            eng.dma_start(outs["key"], k1).then_inc(S("rows_stored"), 16)
            eng.dma_start(outs["value"], v1).then_inc(S("rows_stored"), 16)
            eng.wait_ge(S("xc_made"), 1)
            eng.dma_start(outs["conv"], conv_out).then_inc(S("rows_stored"), 16)
            eng.wait_ge(S("lru_kept"), 1)
            eng.dma_start(outs["lru"], lru_out).then_inc(S("rows_stored"), 16)
            eng.wait_ge(S("rows_stored"), 64)
            for name, n in (("chunk_v_stored", 16), ("shift_stored", 16), ("states_stored", 32)):
                eng.wait_ge(S(name), n)


def lay_consts():
    import numpy as np

    c = np.zeros((P, NCONST), np.float32)

    def put(name, a):
        at, n = CCOL[name]
        c[:a.shape[0], at:at + n] = a

    i, j = np.arange(64)[:, None], np.arange(64)[None, :]
    twice = lambda a: np.concatenate([a, a], 0).astype(np.float32)
    block = lambda n: (i // n) == (j // n)
    put("ident", np.eye(P))
    put("ones", np.ones((P, P)))
    put("head_ones", np.kron(np.eye(2), np.ones((64, 64))))
    t = np.arange(T)
    starts = np.where(t < TP, t % C == 0, (t - TP) % NS == 0)
    put("reset", np.broadcast_to(1.0 - starts, (P, T)))
    put("mask_prompt", twice(np.concatenate([i < j, i <= j], 1)))
    put("mask_sample", twice(np.concatenate([(i < j) & block(8), (i <= j) & block(8)], 1)))
    put("diag8", twice((i < j) & block(8)))
    put("low8", twice((i > j) & block(8)))
    put("low16", twice((i > j) & block(16) & ~block(8)))
    put("low32", twice((i > j) & block(32) & ~block(16)))
    put("low64", twice((i > j) & ~block(32)))
    put("eye64", twice(i == j))
    put("own_batch", (np.arange(TS)[:, None] // NS == np.arange(NB)[None]).astype(np.float32))
    ii, jj = np.arange(P)[:, None], np.arange(P)[None]
    put("tri", (ii <= jj).astype(np.float32))
    put("first", np.broadcast_to(np.concatenate([4.0 - np.arange(4), 16.0 - np.arange(16)]), (P, 20)))
    r = np.arange(P)
    put("same_query", ((r // 64)[:, None] == np.arange(16)[None] // 8) & ((r % 8)[:, None] == np.arange(16)[None] % 8))
    put("own_head", ((r % 64) // 8)[:, None] == np.arange(8)[None])
    put("head_rows", ((r // 64)[:, None] + 2 * (np.arange(32) // 8)[None]) == (np.arange(32) % 8)[None])
    return c


def multiplicity(dist):
    import numpy as np

    n = sum(((dist >= 0) & (dist <= w) & (dist % d == 0)).astype(np.int64) for w, d in ((128, 1), (512, 4), (2048, 16)))
    return np.where(n > 0, np.log(np.maximum(n, 1)), NEG).astype(np.float32)


def bucket(dist):
    import numpy as np

    scaled = np.log(np.maximum(dist, 1) / 16) / np.log(2048 / 16)
    large = np.minimum(16 + (scaled * 16).astype(np.int32), 31)
    return np.where(dist < 16, dist, large).astype(np.int32)


def lay_out(inputs):
    import numpy as np

    g = {k: np.asarray(v) for k, v in inputs.items()}
    col = lambda v: v.reshape(-1, P).T
    stack = lambda w: w.reshape(-1, P, w.shape[1]).transpose(1, 0, 2)
    a = {}
    x = np.concatenate([g["x_prompt"].reshape(TP, D), g["x_sample"].reshape(TS, D)], 0)
    a["x"] = x.T.reshape(KT, P, T).transpose(1, 0, 2)
    stream = np.empty((STREAM, P, CHUNK_ELEMS), np.float32)

    def place(at, w, tiles):
        k, m = w.shape[0] // P, w.shape[1] // P
        stream[at:at + m // tiles] = w.reshape(k, P, m // tiles, tiles, P).transpose(2, 1, 3, 0, 4).reshape(-1, P, CHUNK_ELEMS)

    place(AT_IN0, g["w_in_even"][0], 2)
    place(AT_OUT0, g["w_out_even"][0], 2)
    place(AT_IN1, g["w_in_odd"][0], 2)
    place(AT_OUT1, g["w_out_odd"][0], 2)
    for layer, at in enumerate((AT_MOE0, AT_MOE1)):
        for e in range(NE):
            b = at + EXPERT_CHUNKS * e - (2 if e else 0)
            place(b, g["exp_w_gate"][layer, e], 2)
            place(b + (4 if e else 2), g["exp_w_up"][layer, e], 2)
            place(at + MOE_CHUNKS - 2 if e == NE - 1 else at + EXPERT_CHUNKS * (e + 1), g["exp_w_down"][layer, e], 4)
    a["stream"] = stream
    p = np.zeros((P, NPARAM), np.float32)

    def put(name, v):
        at, n = PCOL[name]
        p[:v.shape[0], at:at + n] = v

    for l in range(2):
        put(f"norm_mix{l}", col(g["norm_mix"][l]))
        put(f"norm_ffn{l}", col(g["norm_ffn"][l]))
        put(f"router_b{l}", np.concatenate([g["router_group_b"][l], g["router_expert_b"][l]])[:, None])
    put("norm_final", col(g["norm_final"]))
    for name, key in (("shift_mu", "shift_mu"), ("decay_w0", "decay_w0"), ("iclr_a0", "iclr_a0"), ("key_k", "key_k"),
                      ("key_a", "key_a"), ("bonus", "bonus_r_k"), ("lnx_g", "lnx_g"), ("lnx_b", "lnx_b"),
                      ("sgu_g", "sgu_norm_g"), ("sgu_b", "sgu_norm_b"), ("conv_b", "conv_b"), ("rgate_b", "rgate_b"),
                      ("igate_b", "igate_b"), ("lambda", "lru_lambda")):
        put(name, col(g[key][0].reshape(-1)))
    put("conv_w", np.concatenate([col(g["conv_w"][0, i]) for i in range(4)], 1))
    a["params"] = p
    a["consts"] = lay_consts()
    a["router"] = np.stack([stack(np.concatenate([g["router_group_w"][l], g["router_expert_w"][l]], 1)) for l in range(2)], 1)
    a["shift0"] = g["state_shift"][0].T.reshape(A_TILES, P, NB).transpose(1, 0, 2)
    a["lora"] = np.stack([np.concatenate([g["decay_up"][0], g["iclr_up"][0]], 0), g["gate_up"][0]], 1)
    a["wkv0"] = g["state_wkv"][0].reshape(NB, HT, 2, 64, 64).transpose(2, 4, 1, 0, 3).reshape(P, HT, NB, 64)
    a["sgu_w"] = g["sgu_w"][0].transpose(2, 0, 1)
    a["sgu_w8"] = np.tile(g["sgu_w"][0][:, :NS, :NS].transpose(2, 0, 1), (NB, 1, NB))
    a["sgu_bias"] = np.concatenate([np.tile(g["sgu_b"][0], (1, 2)), np.tile(g["sgu_b"][0][:, :NS], (1, NB))], 1)[None]
    a["conv0"] = g["state_conv"][0].transpose(2, 0, 1).reshape(HT, P, NB, 3).transpose(1, 0, 2, 3)
    a["lru0"] = g["state_rglru"][0].T.reshape(HT, P, NB).transpose(1, 0, 2)
    gate = np.zeros((P, 2, HT, P), np.float32)
    for n, key in enumerate(("rgate_w", "igate_w")):
        for h in range(8):
            o = 64 * (h % 2)
            gate[o:o + 64, n, h // 2, o:o + 64] = g[key][0, h]
    a["lru_gates"] = gate
    q, k = np.arange(TP)[:, None], np.arange(TP)[None]
    rel = g["rel_bias"]
    full = rel[bucket(np.maximum(q - k, 0))]
    full = full.reshape(2, P, TP, 8).transpose(1, 3, 0, 2)
    a["bias_prompt"] = np.concatenate([full[:, :, 0, :P], full[:, :, 1]], 2)
    m = multiplicity(q - k).reshape(2, P, TP).transpose(1, 0, 2)
    a["count_prompt"] = np.concatenate([m[:, 0, :P], m[:, 1]], 1)
    s = np.tile(np.arange(NS), 16)[:, None]
    head = ((r := np.arange(P)) % 64 // 8)[:, None]
    dist = np.concatenate([PAST + s - np.arange(PAST)[None], np.tile(s - np.arange(TS)[None] % NS, (1, 4))], 1)
    a["bias_sample"] = rel[bucket(np.maximum(dist, 0)), head]
    own = np.concatenate([np.arange(TS)[None] // NS == 2 * p + (r // 64)[:, None] for p in range(4)], 1)
    a["count_sample"] = multiplicity(np.where(np.concatenate([np.ones((P, PAST), bool), own], 1), dist, -1))
    ck = g["cache_k"][0].reshape(NB, 2, 512, HT, 2, 64)
    a["cache_k"] = ck.transpose(0, 1, 4, 5, 3, 2).reshape(NB * 2, P, HT * 512)
    cv = g["cache_v"][0].reshape(NB, 2, 4, P, 512)
    a["cache_v"] = cv.transpose(0, 1, 3, 2, 4).reshape(NB * 2, P, 4 * 512)
    return {n: np.ascontiguousarray(v) for n, v in a.items()}


OUTS = {"y": (P, KT, T), "shift": (P, A_TILES, 9), "wkv_p": (P, HT, 64), "wkv_s": (P, HT, NB, 64), "chunk_v": (P, HT, TS),
        "conv": (P, HT, 27), "lru": (P, HT, 9), "key": (P, HT, T), "value": (P, HT, T)}


def gather(o):
    rows = lambda v: v.transpose(2, 1, 0).reshape(v.shape[2], -1)
    y, k, v = rows(o["y"]), rows(o["key"]), rows(o["value"])
    shift, lru = rows(o["shift"]), rows(o["lru"])
    conv = rows(o["conv"])
    wkv_p = o["wkv_p"].reshape(2, 64, HT, 64).transpose(2, 0, 3, 1).reshape(1, 1, 8, 64, 64)
    wkv_s = o["wkv_s"].reshape(2, 64, HT, NB, 64).transpose(3, 2, 0, 4, 1).reshape(1, NB, 8, 64, 64)
    return (y[None, :TP], y[TP:].reshape(NB, NS, D), wkv_p, shift[None, :1], conv[None, None, :3], lru[None, :1],
            k[:TP].reshape(1, 1, TP, 8, 64), v[:TP].reshape(1, 1, TP, 8, 64),
            wkv_s, shift[None, 1:], rows(o["chunk_v"]).reshape(1, NB, NS, 512), conv[3:].reshape(1, NB, 3, 512),
            lru[None, 1:], k[TP:].reshape(1, NB, NS, 8, 64), v[TP:].reshape(1, NB, NS, 8, 64))


def kernel(**inputs):
    import numpy as np
    import concourse.bacc as bacc
    from concourse.bass_utils import run_bass_kernel_spmd

    nc = bacc.Bacc("TRN2", target_bir_lowering=False, num_devices=1)
    arrays = {f"in_{n}": v for n, v in lay_out(inputs).items()}
    ins = {n[3:]: nc.dram_tensor(n, v.shape, F32, kind="ExternalInput").ap() for n, v in arrays.items()}
    outs = {n: nc.dram_tensor(f"out_{n}", s, F32, kind="ExternalOutput").ap() for n, s in OUTS.items()}
    decoder_layers(nc, ins, outs)
    r = run_bass_kernel_spmd(nc, [arrays], core_ids=[0])
    return tuple(np.ascontiguousarray(v) for v in gather({n: r.results[0][f"out_{n}"] for n in OUTS}))
```

```python
from contextlib import ExitStack

import concourse.bass as bass
from concourse import mybir

F32 = mybir.dt.float32
F32R = mybir.dt.float32r
ALU = mybir.AluOpType
ACT = mybir.ActivationFunctionType
AX = mybir.AxisListType.X

P = 128
D = 1024
KT = D // P
TP = 256
NB, NS = 8, 8
TS = NB * NS
T = TP + TS
HT = 4
A_TILES = 14
NE = 16
CHUNK_ELEMS = 2048
C = 64
N_CHUNKS = T // C
PAST = 1024
NEAR = 512
FAR = (PAST - NEAR) // 2
OLD_KEYS = FAR + NEAR
NEG = -1e30

IN0_CHUNKS, OUT_CHUNKS, IN1_CHUNKS, EXPERT_CHUNKS = 11, 4, 10, 6
MOE_CHUNKS = NE * EXPERT_CHUNKS
AT_IN0 = 0
AT_OUT0 = AT_IN0 + IN0_CHUNKS
AT_MOE0 = AT_OUT0 + OUT_CHUNKS
AT_IN1 = AT_MOE0 + MOE_CHUNKS
AT_OUT1 = AT_IN1 + IN1_CHUNKS
AT_MOE1 = AT_OUT1 + OUT_CHUNKS
STREAM = AT_MOE1 + MOE_CHUNKS
W_RING, RAW_RING = 2, 3

PARAMS = [("norm_mix0", 8), ("norm_mix1", 8), ("norm_ffn0", 8), ("norm_ffn1", 8), ("norm_final", 8),
          ("shift_mu", 14), ("decay_w0", 4), ("iclr_a0", 4), ("key_k", 4), ("key_a", 4), ("bonus", 4),
          ("lnx_g", 4), ("lnx_b", 4), ("sgu_g", 4), ("sgu_b", 4), ("conv_w", 16), ("conv_b", 4),
          ("rgate_b", 4), ("igate_b", 4), ("lambda", 4), ("router_b0", 1), ("router_b1", 1)]
CONSTS = [("ident", 128), ("ones", 128), ("head_ones", 128), ("reset", T), ("mask_prompt", 128),
          ("mask_sample", 128), ("diag8", 64), ("low8", 64), ("low16", 64), ("low32", 64), ("low64", 64),
          ("eye64", 64), ("own_batch", 8), ("tri", 128), ("first", 20), ("same_query", 16),
          ("own_head", 8), ("head_rows", 32)]


def columns(table):
    at, out = 0, {}
    for name, n in table:
        out[name] = (at, n)
        at += n
    return out, at


PCOL, NPARAM = columns(PARAMS)
CCOL, NCONST = columns(CONSTS)


def tiles_through(c):
    n = 0
    for i in range(c + 1):
        in_moe = AT_MOE0 <= i < AT_IN1 or AT_MOE1 <= i
        k = (i - AT_MOE0) % (AT_MOE1 - AT_MOE0)
        n += 4 if in_moe and (k in (MOE_CHUNKS - 2, MOE_CHUNKS - 1) or (k >= 4 and (k - 4) % 6 in (2, 3))) else 2
    return n


def tile(c, i):
    return tiles_through(c - 1) + i + 1


EXPERT_TILES = 16


def decoder_layers(nc, ins, outs, stop=None):
    with ExitStack() as ctx:
        def sb(name, shape, dt=F32):
            return ctx.enter_context(nc.sbuf_tensor(name, shape, dt))

        made = {}

        def S(name):
            if name not in made:
                made[name] = ctx.enter_context(nc.semaphore(name))
            return made[name]

        xt = sb("xt", [P, KT, T])
        h32 = sb("h32", [P, KT, T])
        h_hi = sb("h_hi", [P, KT, T], F32R)
        h_lo = sb("h_lo", [P, KT, T], F32R)
        raw = sb("raw", [P, RAW_RING, CHUNK_ELEMS])
        w_hi = sb("w_hi", [P, W_RING, CHUNK_ELEMS], F32R)
        w_lo = sb("w_lo", [P, W_RING, CHUNK_ELEMS], F32R)
        hid = sb("hid", [P, HT, T])
        hid_hi = sb("hid_hi", [P, HT, T], F32R)
        hid_lo = sb("hid_lo", [P, HT, T], F32R)
        consts = sb("consts", [P, NCONST])
        params = sb("params", [P, NPARAM])
        router = sb("router_sb", [P, 2, KT, 20])
        small = sb("small", [P, 380])
        ARENA = 22144
        arena = sb("arena", [P, ARENA])
        ps = ctx.enter_context(nc.psum_tensor("ps", [P, 8, 512], F32))

        def const(name, rows=P):
            at, n = CCOL[name]
            return consts[0:rows, at:at + n]

        def par(name, i):
            return params[:, PCOL[name][0] + i:PCOL[name][0] + i + 1]

        def par_over(name, n, inner):
            at = PCOL[name][0]
            return params[:, at:at + n].unsqueeze(2).broadcast_to((P, n, inner))

        def take(at, *shape, part=P):
            n = 1
            for s in shape:
                n *= s
            assert at + n <= ARENA, (at, n)
            v = arena[0:part, at:at + n]
            if len(shape) == 2:
                return v.rearrange("p (a b) -> p a b", a=shape[0])
            if len(shape) == 3:
                return v.rearrange("p (a b c) -> p a b c", a=shape[0], b=shape[1])
            if len(shape) == 4:
                return v.rearrange("p (a b c d) -> p a b c d", a=shape[0], b=shape[1], c=shape[2])
            return v

        ident, ones, head_ones = const("ident"), const("ones"), const("head_ones")

        lt = small[:, 0:60].rearrange("p (a b) -> p a b", a=3)
        ra = small[:, 60:120].rearrange("p (a b) -> p a b", a=3)
        rb = small[:, 120:180].rearrange("p (a b) -> p a b", a=3)
        rc = small[:, 180:240].rearrange("p (a b) -> p a b", a=3)
        gates_tok = small[:, 240:288].rearrange("p (a b) -> p a b", a=3)
        rs = small[:, 288:324].rearrange("p (a b) -> p a b", a=12)
        eps_norm = small[:, 324:325]
        eps_gn = small[:, 325:326]
        s_root, s_rstd = take(NE * T, T), take(NE * T + T, T)
        logits_ch = s_root[0:20, :]
        gates_ch = s_rstd[0:16, :]
        gate_all = take(0, NE * T)

        xs = take(0, A_TILES, T)
        s1, s2, s4, s5, s6 = (take(4480 + 1280 * i, HT, T) for i in range(5))
        s3 = hid[:, :, :]
        ar = h32[:, :, :].rearrange("p a b -> p (a b)").rearrange("p (j c w t) -> p j c w t", j=HT, c=N_CHUNKS, w=2)
        G0 = 10880
        gu, gv = take(G0, HT, T), take(G0 + 1280, HT, T)
        sbias = take(G0 + 2560, HT, T)
        vn_tok = take(G0 + 3840, 3, 512)
        sw = take(G0 + 5376, HT, P)
        sw8 = take(G0 + 5888, HT, TS, part=TS)
        p_ring = take(G0 + 6144, 4, 329)
        d_ring = take(G0 + 7460, 2, T)
        gb_m, gk_m = take(G0, 8, 128), take(G0 + 1024, 8, 128)
        dd, ee, pp, qq, d2, e2 = (take(G0 + 2048 + 512 * i, 8, 64) for i in range(6))
        lo16, lo32, lo64 = (take(G0 + 5120 + 512 * i, 8, 64) for i in range(3))
        v_tok, b_tok, k_tok = (take(G0 + 6656 + 512 * i, 8, 64) for i in range(3))
        swkv = take(G0 + 8192, HT, NB, 64)
        lora = take(G0 + 10240, 2, 512)
        state = sb("state", [P, HT, 64])
        w_end = small[:, 330:378].rearrange("p (a b) -> p a b", a=HT)
        state_flat = state[:, :, :].rearrange("p a b -> p (a b)")
        shift0 = state_flat[:, 0:112].rearrange("p (a b) -> p a b", a=A_TILES)
        shift_out = state_flat[:, 112:238].rearrange("p (a b) -> p a b", a=A_TILES)
        qe = h32[0:TS, 0:4, :].rearrange("p a b -> p (a b)")[:, 0:1024].rearrange("p (a b) -> p a b", a=2)
        ve = h32[0:TS, 4:8, :].rearrange("p a b -> p (a b)")[:, 0:1024].rearrange("p (a b) -> p a b", a=2)
        g_root, g_rstd = hid[:, 0, :], hid[:, 1, :]

        block = ctx.enter_context(nc.Block())

        steps = [0]

        def next_reads(eng, ins_):
            steps[0] += 1
            ins_.then_inc(S("vector_step"), 1)
            eng.wait_ge(S("vector_step"), steps[0])

        def chunk_view(w, slot, rows, tiles):
            return w[:, slot, :].rearrange("p (m k n) -> p m k n", m=tiles, k=rows)

        def load_chunk(eng, c, it=None):
            if c >= RAW_RING or it is not None:
                eng.wait_ge(S("w_lo_made"), c - RAW_RING + 1 + (0 if it is None else EXPERT_CHUNKS * it))
            src = ins["stream"][c] if it is None else ins["stream"][it * EXPERT_CHUNKS + c]
            eng.dma_start(raw[:, c % RAW_RING, :], src).then_inc(S(f"raw_loaded{c % RAW_RING}"), 16)

        def split_hi(eng, c, it=None):
            if c >= STREAM:
                return
            more = 0 if it is None else it * (16 * EXPERT_CHUNKS // RAW_RING)
            eng.wait_ge(S(f"raw_loaded{c % RAW_RING}"), 16 * (c // RAW_RING + 1) + more)
            if c >= W_RING:
                eng.wait_ge(S("tile_done"), tiles_through(c - W_RING) + (0 if it is None else EXPERT_TILES * it))
            eng.activation(w_hi[:, c % W_RING, :], raw[:, c % RAW_RING, :], ACT.Copy).then_inc(S("w_hi_made"), 1)

        def split_lo(eng, c, it=None):
            if c >= STREAM:
                return
            eng.wait_ge(S("w_hi_made"), c + 1 + (0 if it is None else EXPERT_CHUNKS * it))
            eng.tensor_tensor(w_lo[:, c % W_RING, :], raw[:, c % RAW_RING, :], w_hi[:, c % W_RING, :],
                              ALU.subtract).then_inc(S("w_lo_made"), 1)

        def tile_product(eng, bank, slot, m, rows, tiles, x_hi, x_lo):
            hi, lo = chunk_view(w_hi, slot, rows, tiles), chunk_view(w_lo, slot, rows, tiles)
            for k in range(rows):
                eng.matmul(ps[:, bank, 0:T], hi[:, m, k, :], x_hi[:, k, :], start=(k == 0), stop=False)
                eng.matmul(ps[:, bank, 0:T], hi[:, m, k, :], x_lo[:, k, :], start=False, stop=False)
                mm = eng.matmul(ps[:, bank, 0:T], lo[:, m, k, :], x_hi[:, k, :], start=False, stop=(k == rows - 1))
            return mm

        def norm_act(eng, i, split):
            for q in range(4):
                eng.activation(h32[:, 2 * q:2 * q + 2, :], xt[:, 2 * q:2 * q + 2, :], ACT.Square).then_inc(S("norm_sq"), 1)
            eng.wait_ge(S("norm_ms"), i + 1)
            eng.activation(s_root, ps[:, 0, 0:T], ACT.Sqrt, bias=eps_norm, scale=1.0 / D).then_inc(S("norm_root"), 1)
            if split:
                norm_split_hi(eng, i)

        def norm_split_hi(eng, i):
            for q in range(2):
                eng.wait_ge(S("norm_h"), KT * i + 4 * (q + 1))
                eng.activation(h_hi[:, 4 * q:4 * q + 4, :], h32[:, 4 * q:4 * q + 4, :], ACT.Copy).then_inc(S("norm_hi"), 1)

        def norm_pe(eng, i):
            for k in range(KT):
                if k % 2 == 0:
                    eng.wait_ge(S("norm_sq"), 4 * i + k // 2 + 1)
                mm = eng.matmul(ps[:, 0, 0:T], ones, h32[:, k, :], start=(k == 0), stop=(k == KT - 1))
            mm.then_inc(S("norm_ms"), 1)

        def norm_dve(eng, i, weight, split):
            eng.wait_ge(S("norm_root"), i + 1)
            eng.reciprocal(s_rstd, s_root).then_inc(S("norm_rstd"), 1)
            eng.wait_ge(S("norm_rstd"), i + 1)
            for k in range(KT):
                eng.scalar_tensor_tensor(h32[:, k, :], xt[:, k, :], par(weight, k), s_rstd, ALU.mult, ALU.mult).then_inc(S("norm_h"), 1)
            if split:
                norm_split_lo(eng, i)

        def norm_split_lo(eng, i):
            for q in range(2):
                eng.wait_ge(S("norm_hi"), 2 * i + q + 1)
                eng.tensor_tensor(h_lo[:, 4 * q:4 * q + 4, :], h32[:, 4 * q:4 * q + 4, :],
                                  h_hi[:, 4 * q:4 * q + 4, :], ALU.subtract).then_inc(S("norm_lo"), 1)

        def dense_products(eng, e0):
            def gate(c, e, it=None):
                more = 0 if it is None else HT * it
                for m in range(HT):
                    if m % 2 == 0:
                        eng.wait_ge(S("w_lo_made"), c + m // 2 + 1 + (0 if it is None else EXPERT_CHUNKS * it))
                    if e:
                        eng.wait_ge(S("silu_made"), HT * (e - 1) + m + 1 + more)
                    mm = tile_product(eng, m, (c + m // 2) % W_RING, m % 2, KT, 2, h_hi, h_lo)
                    mm.then_inc(S("tile_done"), 1)

            def up(c, e, it=None):
                more = 0 if it is None else 2 * HT * it
                for m in range(HT):
                    if m % 2 == 0:
                        eng.wait_ge(S("w_lo_made"), c + m // 2 + 1 + (0 if it is None else EXPERT_CHUNKS * it))
                    if e % NE:
                        eng.wait_ge(S("down_added"), 2 * HT * e - 3 + m + more)
                    mm = tile_product(eng, 4 + m, (c + m // 2) % W_RING, m % 2, KT, 2, h_hi, h_lo)
                    mm.then_inc(S("tile_done"), 1)

            def down(c, e, it=None):
                eng.wait_ge(S("hid_lo_made"), e + 1 + (0 if it is None else it))
                for half in range(2):
                    eng.wait_ge(S("w_lo_made"), c + half + 1 + (0 if it is None else EXPERT_CHUNKS * it))
                    for m in range(HT):
                        if half:
                            eng.wait_ge(S("down_added"), 2 * HT * e + m + 1 + (0 if it is None else 2 * HT * it))
                        mm = tile_product(eng, 4 + m, (c + half) % W_RING, m, HT, 4, hid_hi, hid_lo)
                        mm.then_inc(S("tile_done"), 1)

            return gate, up, down

        def moe_pe(eng, layer, at):
            ni, e0 = 1 + 2 * layer, NE * layer
            norm_pe(eng, ni)
            for k in range(KT):
                eng.wait_ge(S("norm_h"), KT * ni + k + 1)
                mm = eng.matmul(ps[0:20, 4, 0:T], router[:, layer, k, :], h32[:, k, :], start=(k == 0), stop=(k == KT - 1))
            mm.then_inc(S("logits"), 1)

            eng.wait_ge(S("logits_sb"), layer + 1)
            for i, (a, b) in enumerate(TOKEN_TILES):
                mm = eng.transpose(ps[0:b - a, 5, 20 * i:20 * i + 20], logits_ch[:, a:b], ident[0:20, 0:20])
            mm.then_inc(S("logits_tok"), 1)
            eng.wait_ge(S("group_shifted"), layer + 1)
            hot = [ra[0:b - a, i, 0:4] for i, (a, b) in enumerate(TOKEN_TILES)]
            for i, (a, b) in enumerate(TOKEN_TILES):
                n = b - a
                for k in range(i):
                    eng.matmul(ps[0:n, 6, 4 * i:4 * i + 4], ones[:, 0:n], hot[k], start=(k == 0), stop=False)
                eng.matmul(ps[0:n, 6, 4 * i:4 * i + 4], const("tri")[0:n, 0:n], hot[i], start=(i == 0), stop=True)
            for i, (a, b) in enumerate(TOKEN_TILES):
                eng.matmul(ps[:, 6, 12:16], ones[0:b - a, :], hot[i], start=(i == 0), stop=(i == 2))
            eng.matmul(ps[:, 7, 0:P], ones, const("tri"), start=True, stop=True).then_inc(S("placed"), 1)
            with eng.If(read_flag(eng, layer)):
                sorted_pe(eng, layer, at)
            with eng.Else():
                dense_pe(eng, layer, at)

        def dense_pe(eng, layer, at):
            ni, e0 = 1 + 2 * layer, NE * layer
            gate, up, down = dense_products(eng, e0)
            for q in range(2):
                eng.wait_ge(S("norm_lo"), 2 * ni + q + 1)
            gate(at, e0)
            eng.wait_ge(S("routed"), 2 * layer + 2)
            up(at + 2, e0)
            eng.wait_ge(S("gates_tok"), layer + 1)
            eng.wait_ge(S("silu_made"), HT * e0 + HT)
            for i, (a, b) in enumerate(((0, 128), (128, 256), (256, 320))):
                mm = eng.transpose(ps[0:16, 0, a:b], gates_tok[0:b - a, i, :], ident[0:b - a, 0:b - a])
            mm.then_inc(S("gates_back"), 1)
            eng.wait_ge(S("gates_ch"), layer + 1)
            for e in range(NE):
                if e >= 3:
                    eng.wait_ge(S("gate_rows"), 16 * layer + e - 2)
                eng.matmul(ps[:, 1 + e % 3, 0:T], ident[0:16, e:e + 1].broadcast_to((16, P)), gates_ch,
                           start=True, stop=True).then_inc(S("gate_bc"), 1)
            eng.wait_ge(S("gate_rows"), 16 * layer + NE)
            with eng.Fori(0, NE - 1) as it:
                gate(at + 4, e0 + 1, it)
                down(at + 6, e0, it)
                up(at + 8, e0 + 1, it)
            down(at + MOE_CHUNKS - 2, e0 + NE - 1)
            for name, n in (("turned_route", 10), ("gathered", 4), ("hid_turned", NE), ("moved", 32)):
                eng.sem_inc(S(name), n)

        def moe_act(eng, layer, at):
            ni, e0 = 1 + 2 * layer, NE * layer
            split_hi(eng, at)
            split_hi(eng, at + 1)
            norm_act(eng, ni, False)
            eng.wait_ge(S("logits"), layer + 1)
            eng.activation(logits_ch, ps[0:20, 4, 0:T], ACT.Identity, bias=params[0:20, PCOL[f"router_b{layer}"][0]:][:, 0:1])\
               .then_inc(S("logits_sb"), 1)

            eng.wait_ge(S("group_shifted"), layer + 1)
            eng.activation(rb[:, :, 0:4], rb[:, :, 0:4], ACT.Exp).then_inc(S("router_exp"), 1)
            eng.wait_ge(S("pair_shifted"), layer + 1)
            eng.activation(rs[:, 7, :], rs[:, 6, :], ACT.Exp).then_inc(S("router_exp"), 1)
            with eng.If(read_flag(eng, layer)):
                sorted_act(eng, layer, at)
            with eng.Else():
                dense_act(eng, layer, at)

        def dense_act(eng, layer, at):
            ni, e0 = 1 + 2 * layer, NE * layer
            norm_split_hi(eng, ni)

            def silu(e, it=None):
                if e:
                    eng.wait_ge(S("hid_lo_made"), e + (0 if it is None else it))
                for m in range(HT):
                    eng.wait_ge(S("tile_done"), tile(at if it is None else at + 4, m) + (0 if it is None else EXPERT_TILES * it))
                    eng.activation(hid[:, m, :], ps[:, m, 0:T], ACT.Silu).then_inc(S("silu_made"), 1)
                    if m % 2:
                        split_hi(eng, (at + (2 if e == e0 else 6)) + m // 2, it)

            def hidden(e, it=None):
                eng.wait_ge(S("hid_made"), e + 1 + (0 if it is None else it))
                eng.activation(hid_hi[:, :, :], hid[:, :, :], ACT.Copy).then_inc(S("hid_hi_made"), 1)

            silu(e0)
            split_hi(eng, at + 4)
            split_hi(eng, at + 5)
            eng.wait_ge(S("gates_back"), layer + 1)
            eng.activation(gates_ch, ps[0:16, 0, 0:T], ACT.Copy).then_inc(S("gates_ch"), 1)
            for e in range(NE):
                eng.wait_ge(S("gate_bc"), 16 * layer + e + 1)
                eng.activation(gate_all[:, T * e:T * e + T], ps[:, 1 + e % 3, 0:T], ACT.Copy).then_inc(S("gate_rows"), 1)
            hidden(e0)
            with eng.Fori(0, NE - 1) as it:
                silu(e0 + 1, it)
                for c in range(8, 12):
                    split_hi(eng, at + c, it)
                hidden(e0 + 1, it)
            for name, n in (("route_kept", 10), ("x_hi_made", 4), ("y_kept", 4)):
                eng.sem_inc(S(name), n)

        def moe_dve(eng, layer, at):
            ni, e0 = 1 + 2 * layer, NE * layer
            split_lo(eng, at)
            split_lo(eng, at + 1)
            norm_dve(eng, ni, f"norm_ffn{layer}", False)
            def over(v, m):
                return v.broadcast_to((P, 3, m))

            eng.wait_ge(S("logits_tok"), layer + 1)
            eng.tensor_copy(lt[:, 0:2, :], ps[:, 5, 0:40].rearrange("p (a b) -> p a b", a=2)).then_inc(S("routed"), 1)
            eng.tensor_copy(lt[0:64, 2, :], ps[0:64, 5, 40:60]).then_inc(S("routed"), 1)
            eng.wait_ge(S("routed"), 2 * layer + 2)
            r = [rs[:, i, :].unsqueeze(2) for i in range(12)]
            first4 = const("first")[:, 0:4].unsqueeze(1).broadcast_to((P, 3, 4))
            first16 = const("first")[:, 4:20].unsqueeze(1).broadcast_to((P, 3, 16))
            lg, le = lt[:, :, 0:4], lt[:, :, 4:20]
            next_reads(eng, eng.tensor_reduce(r[0], lg, AX, ALU.max))
            next_reads(eng, eng.tensor_tensor(ra[:, :, 0:4], lg, over(r[0], 4), ALU.is_equal))
            next_reads(eng, eng.tensor_tensor(ra[:, :, 0:4], ra[:, :, 0:4], first4, ALU.mult))
            next_reads(eng, eng.tensor_reduce(r[1], ra[:, :, 0:4], AX, ALU.max))
            next_reads(eng, eng.tensor_tensor(ra[:, :, 0:4], ra[:, :, 0:4], over(r[1], 4), ALU.is_equal))
            eng.tensor_tensor(rb[:, :, 0:4], lg, over(r[0], 4), ALU.subtract).then_inc(S("group_shifted"), 1)
            for i in range(4):
                last = eng.tensor_copy(rc[:, :, 4 * i:4 * i + 4], ra[:, :, i:i + 1].broadcast_to((P, 3, 4)))
            next_reads(eng, last)
            next_reads(eng, eng.tensor_tensor(le, le, rc[:, :, 0:16], ALU.mult))
            next_reads(eng, eng.tensor_scalar(rc[:, :, 0:16], rc[:, :, 0:16], 1.0, -NEG, ALU.subtract, ALU.mult))
            next_reads(eng, eng.tensor_tensor(le, le, rc[:, :, 0:16], ALU.add))
            picks = (ra[:, :, 4:20], rc[:, :, 0:16])
            for i in range(2):
                best = r[2 + i]
                next_reads(eng, eng.tensor_reduce(best, le, AX, ALU.max))
                next_reads(eng, eng.tensor_tensor(picks[i], le, over(best, 16), ALU.is_equal))
                next_reads(eng, eng.tensor_tensor(picks[i], picks[i], first16, ALU.mult))
                next_reads(eng, eng.tensor_reduce(r[4 + i], picks[i], AX, ALU.max))
                next_reads(eng, eng.tensor_tensor(picks[i], picks[i], over(r[4 + i], 16), ALU.is_equal))
                if i == 0:
                    next_reads(eng, eng.tensor_scalar(gates_tok, picks[0], 2 * NEG, None, ALU.mult))
                    next_reads(eng, eng.tensor_tensor(le, le, gates_tok, ALU.add))
            eng.tensor_tensor(r[6], r[3], r[2], ALU.subtract).then_inc(S("pair_shifted"), 1)
            eng.wait_ge(S("router_exp"), 2 * layer + 2)
            next_reads(eng, eng.tensor_reduce(r[8], rb[:, :, 0:4], AX, ALU.add))
            next_reads(eng, eng.tensor_scalar(r[9], r[7], 1.0, None, ALU.add))
            next_reads(eng, eng.tensor_tensor(r[9], r[9], r[8], ALU.mult))
            next_reads(eng, eng.reciprocal(r[9], r[9]))
            next_reads(eng, eng.tensor_tensor(r[10], r[9], r[7], ALU.mult))
            next_reads(eng, eng.tensor_tensor(picks[0], picks[0], over(r[9], 16), ALU.mult))
            next_reads(eng, eng.tensor_tensor(picks[1], picks[1], over(r[10], 16), ALU.mult))
            eng.tensor_tensor(gates_tok, picks[0], picks[1], ALU.add).then_inc(S("gates_tok"), 1)

            eng.wait_ge(S("placed"), layer + 1)
            keys = rb[:, :, 4:8]
            eng.tensor_tensor(keys[:, 0:2, :], ra[:, 0:2, 0:4], ps[:, 6, 0:8].rearrange("p (a b) -> p a b", a=2), ALU.mult)
            eng.tensor_tensor(keys[0:64, 2, :], ra[0:64, 2, 0:4], ps[0:64, 6, 8:12], ALU.mult)
            eng.tensor_copy(places, ps[:, 7, 0:P])
            next_reads(eng, eng.tensor_reduce(rs[:, 11, 0:1], ps[:, 6, 12:16], AX, ALU.max))
            eng.tensor_scalar(flag, rs[:, 11, 0:1], float(P) + 0.5, None, ALU.is_lt).then_inc(S("flag_made"), 1)
            eng.wait_ge(S("flag_made"), layer + 1)
            with eng.If(read_flag(eng, layer)):
                sorted_dve(eng, layer, at)
            with eng.Else():
                dense_dve(eng, layer, at)

        def dense_dve(eng, layer, at):
            ni, e0 = 1 + 2 * layer, NE * layer
            norm_split_lo(eng, ni)

            def gated(e, it=None):
                at_e = T * (e - e0) + (0 if it is None else T * it)
                g = gate_all[:, bass.ds(at_e, T)] if it is not None else gate_all[:, at_e:at_e + T]
                eng.wait_ge(S("silu_made"), HT * (e + 1) + (0 if it is None else HT * it))
                eng.tensor_tensor(hid[:, :, :], hid[:, :, :], g.unsqueeze(1).broadcast_to((P, HT, T)), ALU.mult)\
                   .then_inc(S("gated"), 1)

            def hidden(e, it=None):
                more = 0 if it is None else it
                eng.wait_ge(S("gated"), e + 1 + more)
                eng.wait_ge(S("tile_done"), tile(at + 2 if it is None else at + 8, 3) + (0 if it is None else EXPERT_TILES * it))
                eng.tensor_tensor(hid[:, :, :], hid[:, :, :], ps[:, 4:8, 0:T], ALU.mult).then_inc(S("hid_made"), 1)
                eng.wait_ge(S("hid_hi_made"), e + 1 + more)
                eng.tensor_tensor(hid_lo[:, :, :], hid[:, :, :], hid_hi[:, :, :], ALU.subtract).then_inc(S("hid_lo_made"), 1)

            def add_down(e, it=None, c=None):
                for m in range(2 * HT):
                    more = 0 if it is None else 2 * HT * it
                    eng.wait_ge(S("tile_done"), tile(at + MOE_CHUNKS - 2 if it is None else at + 6, m) + (0 if it is None else EXPERT_TILES * it))
                    if e > e0 or it is not None:
                        v = 2 * HT * (e - 1) + m + 1
                        if v > 0:
                            eng.wait_ge(S("down_added"), v + more)
                    eng.tensor_tensor(xt[:, m, :], xt[:, m, :], ps[:, 4 + m % HT, 0:T], ALU.add).then_inc(S("down_added"), 1)
                    if m % HT == HT - 1 and c is not None:
                        split_lo(eng, c + m // HT, it)

            for c in range(2, 6):
                split_lo(eng, at + c)
            eng.wait_ge(S("gate_rows"), 16 * layer + NE)
            gated(e0)
            hidden(e0)
            with eng.Fori(0, NE - 1) as it:
                split_lo(eng, at + 6, it)
                split_lo(eng, at + 7, it)
                gated(e0 + 1, it)
                add_down(e0, it, at + 8)
                split_lo(eng, at + 10, it)
                split_lo(eng, at + 11, it)
                hidden(e0 + 1, it)
            add_down(e0 + NE - 1)
            for name, n in (("select_made", 4), ("x_lo_made", 4)):
                eng.sem_inc(S(name), n)

        def read_flag(eng, layer):
            eng.wait_ge(S("flag_made"), layer + 1)
            return eng.value_load(flag[0:1, 0:1], min_val=0, max_val=1)

        TOKEN_TILES = ((0, 128), (128, 256), (256, 320))
        flag = small[:, 378:379].bitcast(mybir.dt.int32)
        h_tok = take(0, 3, D)
        select = take(3072, 4, 3, P)
        places = take(4608, P)
        h32_flat = h32[:, :, :].rearrange("p a b -> p (a b)")
        y32 = h32_flat[:, 0:D]
        PG = T + NE
        placed_rows = h32_flat[:, D:D + 4 * PG]
        x_hi, x_lo = (v[:, :, :].rearrange("p a b -> p (a b)")[:, 0:D].rearrange("p (k n) -> p k n", k=KT) for v in (h_hi, h_lo))
        h_tok_hid = hid[:, :, :].rearrange("p a b -> p (a b)")[:, 0:512]
        ht_hi, ht_lo = (v[:, :, :].rearrange("p a b -> p (a b)")[:, 0:512].rearrange("p (k n) -> p k n", k=HT) for v in (hid_hi, hid_lo))
        GATE_BANK, UP_BANK, TURN_BANK, DOWN_BANK, MOVE_BANK = 0, 1, 2, 3, 5

        def expert_chunk(at, e):
            return at + (EXPERT_CHUNKS * e - 2 if e else 0)

        def per(it, n):
            return 0 if it is None else it * n

        def chunk_it(it):
            return None if it is None else it * 4

        def sorted_pe(eng, layer, at):
            e0 = NE * layer

            def halves(c, e, q, it, bank, x_wait=None, between=None):
                for n in range(2):
                    eng.wait_ge(S("w_lo_made"), c + n + 1 + per(it, 24))
                    slot = (c + n) % W_RING
                    hi, lo = chunk_view(w_hi, slot, KT, 2), chunk_view(w_lo, slot, KT, 2)
                    out = ps[:, bank, 256 * n:256 * n + 256].rearrange("p (m n) -> p m n", m=2)
                    for k in range(KT):
                        eng.matmul(out, x_hi[:, k, :], hi[:, :, k, :], start=(k == 0), stop=False)
                        eng.matmul(out, x_hi[:, k, :], lo[:, :, k, :], start=False, stop=False)
                        mm = eng.matmul(out, x_lo[:, k, :], hi[:, :, k, :], start=False, stop=(k == KT - 1))
                    mm.then_inc(S("tile_done"), 2)
                    if n == 0 and between is not None:
                        between()

            def turn(e, it):
                eng.wait_ge(S("hid_made"), e0 + e + 1 + per(it, 4))
                if e0 + e:
                    eng.wait_ge(S("hid_lo_made"), e0 + e + per(it, 4))
                for f in range(HT):
                    mm = eng.transpose(ps[:, TURN_BANK, P * f:P * f + P], h_tok_hid[:, P * f:P * f + P], ident)
                mm.then_inc(S("hid_turned"), 1)

            def down(c, e, it):
                eng.wait_ge(S("hid_lo_made"), e0 + e + 1 + per(it, 4))
                if e % 4 == 0 and 4 * layer + e // 4:
                    eng.wait_ge(S("y_kept"), 4 * layer + e // 4 + per(it, 1))
                for n in range(2):
                    eng.wait_ge(S("w_lo_made"), c + n + 1 + per(it, 24))
                    slot = (c + n) % W_RING
                    hi, lo = chunk_view(w_hi, slot, HT, 4), chunk_view(w_lo, slot, HT, 4)
                    out = ps[:, DOWN_BANK + n, :].rearrange("p (m n) -> p m n", m=4)
                    for k in range(HT):
                        eng.matmul(out, ht_hi[:, k, :], hi[:, :, k, :], start=(e % 4 == 0 and k == 0), stop=False)
                        eng.matmul(out, ht_hi[:, k, :], lo[:, :, k, :], start=False, stop=False)
                        mm = eng.matmul(out, ht_lo[:, k, :], hi[:, :, k, :], start=False, stop=(e % 4 == 3 and k == HT - 1))
                    mm.then_inc(S("tile_done"), 4)

            def gather(q, it):
                if 4 * layer + q:
                    eng.wait_ge(S("x_lo_made"), 4 * layer + q + per(it, 1))
                if q:
                    eng.wait_ge(S("down_added"), 2 * HT * e0 + 32 * (q - 1) + per(it, 32)) if e0 or q > 1 else None
                for k in range(KT):
                    for i, (a, b) in enumerate(TOKEN_TILES):
                        if it is None:
                            to = select[0:b - a, q, i, :]
                        else:
                            to = arena[0:b - a, bass.ds(it * 384 + (3072 + 384 * q + P * i), P)]
                        mm = eng.matmul(ps[:, MOVE_BANK + k // 4, P * (k % 4):P * (k % 4) + P], h_tok[0:b - a, i, P * k:P * k + P], to,
                                        start=(i == 0), stop=(i == 2))
                mm.then_inc(S("gathered"), 1)

            def scatter(q, it):
                eng.wait_ge(S("y_kept"), 4 * layer + q + 1 + per(it, 1))
                for k in range(KT):
                    if k >= 3:
                        eng.wait_ge(S("down_added"), 2 * HT * e0 + 32 * q + 4 * (k - 2) + per(it, 32))
                    if it is None:
                        rows = h32_flat[:, D + PG * q:D + PG * q + T]
                    else:
                        rows = h32_flat[:, bass.ds(it * PG + (D + PG * q), T)]
                    eng.matmul(ps[:, MOVE_BANK + k % 3, 0:T], y32[:, P * k:P * k + P], rows, start=True, stop=True).then_inc(S("moved"), 1)

            def group(q, it):
                gather(q, it)
                eng.wait_ge(S("x_lo_made"), 4 * layer + q + 1 + per(it, 1))
                for i in range(4):
                    e = 4 * q + i
                    c = expert_chunk(at, e)
                    if e0 + e:
                        eng.wait_ge(S("silu_made"), HT * (e0 + e) + per(it, 16))
                    halves(c, e, q, it, GATE_BANK, between=(lambda: turn(e - 1, it)) if e else None)
                    if e:
                        down(c + 2, e - 1, it)
                    if e0 + e:
                        eng.wait_ge(S("hid_made"), e0 + e + per(it, 4))
                    halves(c + (4 if e else 2), e, q, it, UP_BANK)
                    if i == 0 and q:
                        scatter(q - 1, it)

            base = 10 * layer
            for i, (a, b) in enumerate(TOKEN_TILES):
                for half in range(2):
                    for k in range(4):
                        ct = 4 * half + k
                        mm = eng.transpose(ps[0:b - a, 1 + 2 * i + half, P * k:P * k + P], h32[:, ct, a:b], ident)
                    mm.then_inc(S("turned_route"), 1)
            eng.wait_ge(S("route_kept"), base + 6)
            for g in range(4):
                eng.wait_ge(S("select_made"), 4 * layer + g + 1)
                for i, (a, b) in enumerate(TOKEN_TILES):
                    eng.transpose(ps[:, 1 + g, a:b], select[0:b - a, g, i, :], ident[0:b - a, 0:b - a])
                for i, (a, b) in enumerate(TOKEN_TILES):
                    mm = eng.matmul(ps[:, 1 + g, T:PG], select[0:b - a, g, i, :], gates_tok[0:b - a, i, :], start=(i == 0), stop=(i == 2))
                mm.then_inc(S("turned_route"), 1)
            eng.wait_ge(S("route_kept"), base + 10)
            group(0, None)
            with eng.Fori(0, 3) as it:
                group(1, it)
            turn(NE - 1, None)
            down(at + MOE_CHUNKS - 2, NE - 1, None)
            scatter(3, None)
            for name, n in (("gates_back", 1), ("gate_bc", NE)):
                eng.sem_inc(S(name), n)

        def sorted_act(eng, layer, at):
            e0, base = NE * layer, 10 * layer
            for i, (a, b) in enumerate(TOKEN_TILES):
                for half in range(2):
                    eng.wait_ge(S("turned_route"), base + 2 * i + half + 1)
                    eng.activation(h_tok[0:b - a, i, 512 * half:512 * half + 512], ps[0:b - a, 1 + 2 * i + half, :], ACT.Copy).then_inc(S("route_kept"), 1)
            for g in range(4):
                eng.wait_ge(S("turned_route"), base + 7 + g)
                eng.activation(h32_flat[:, D + PG * g:D + PG * g + PG], ps[:, 1 + g, 0:PG], ACT.Copy).then_inc(S("route_kept"), 1)

            def hid_split(e, it):
                eng.wait_ge(S("hid_turned"), e0 + e + 1 + per(it, 4))
                eng.activation(ht_hi, ps[:, TURN_BANK, :].rearrange("p (k n) -> p k n", k=HT), ACT.Copy).then_inc(S("hid_hi_made"), 1)

            def y_keep(q, c, it):
                eng.wait_ge(S("tile_done"), tiles_through(c) + per(it, 64))
                if q or it is not None:
                    eng.wait_ge(S("moved"), 32 * layer + 8 * q + per(it, 8)) if layer or q else None
                eng.activation(y32.rearrange("p (a b) -> p a b", a=2), ps[:, DOWN_BANK:DOWN_BANK + 2, :], ACT.Copy).then_inc(S("y_kept"), 1)

            def group(q, it):
                eng.wait_ge(S("gathered"), 4 * layer + q + 1 + per(it, 1))
                eng.activation(x_hi.rearrange("p (a b) n -> p a b n", a=2), ps[:, MOVE_BANK:MOVE_BANK + 2, :].rearrange("p a (b n) -> p a b n", b=4), ACT.Copy)\
                   .then_inc(S("x_hi_made"), 1)
                for i in range(4):
                    e = 4 * q + i
                    c = expert_chunk(at, e)
                    split_hi(eng, c + 2, chunk_it(it))
                    if e:
                        hid_split(e - 1, it)
                    split_hi(eng, c + 3, chunk_it(it))
                    eng.wait_ge(S("tile_done"), tiles_through(c + 1) + per(it, 64))
                    eng.activation(h_tok_hid, ps[:, GATE_BANK, :], ACT.Silu).then_inc(S("silu_made"), HT)
                    split_hi(eng, c + 4, chunk_it(it))
                    split_hi(eng, c + 5, chunk_it(it))
                    if i == 0 and q:
                        y_keep(q - 1, c + 3, it)
                    if e:
                        split_hi(eng, c + 6, chunk_it(it))
                        split_hi(eng, c + 7, chunk_it(it))

            group(0, None)
            with eng.Fori(0, 3) as it:
                group(1, it)
            hid_split(NE - 1, None)
            y_keep(3, at + MOE_CHUNKS - 1, None)
            for name, n in (("norm_hi", 2), ("gates_ch", 1), ("gate_rows", NE)):
                eng.sem_inc(S(name), n)

        def sorted_dve(eng, layer, at):
            e0 = NE * layer
            for g in range(4):
                for i, (a, b) in enumerate(TOKEN_TILES):
                    last = eng.tensor_scalar(select[0:b - a, g, i, :], places[0:b - a, :], rb[0:b - a, i, 4 + g:5 + g], None, ALU.is_equal)
                last.then_inc(S("select_made"), 1)

            def hid_split(e, it):
                eng.wait_ge(S("hid_hi_made"), e0 + e + 1 + per(it, 4))
                eng.tensor_tensor(ht_lo, ps[:, TURN_BANK, :].rearrange("p (k n) -> p k n", k=HT), ht_hi, ALU.subtract).then_inc(S("hid_lo_made"), 1)

            def add(q, it):
                for k in range(KT):
                    eng.wait_ge(S("moved"), 32 * layer + 8 * q + k + 1 + per(it, 8))
                    eng.tensor_tensor(xt[:, k, :], xt[:, k, :], ps[:, MOVE_BANK + k % 3, 0:T], ALU.add).then_inc(S("down_added"), 4)

            def group(q, it):
                eng.wait_ge(S("x_hi_made"), 4 * layer + q + 1 + per(it, 1))
                eng.tensor_tensor(x_lo.rearrange("p (a b) n -> p a b n", a=2), ps[:, MOVE_BANK:MOVE_BANK + 2, :].rearrange("p a (b n) -> p a b n", b=4),
                                  x_hi.rearrange("p (a b) n -> p a b n", a=2), ALU.subtract).then_inc(S("x_lo_made"), 1)
                for i in range(4):
                    e = 4 * q + i
                    c = expert_chunk(at, e)
                    split_lo(eng, c + 2, chunk_it(it))
                    if e:
                        hid_split(e - 1, it)
                    split_lo(eng, c + 3, chunk_it(it))
                    g = D + PG * q + T + e
                    gate = h32_flat[:, g:g + 1] if it is None else h32_flat[:, bass.ds(it * (PG + 4) + g, 1)]
                    eng.wait_ge(S("silu_made"), HT * (e0 + e + 1) + per(it, 16))
                    eng.tensor_scalar(h_tok_hid, h_tok_hid, gate, None, ALU.mult).then_inc(S("gated"), 1)
                    split_lo(eng, c + 4, chunk_it(it))
                    split_lo(eng, c + 5, chunk_it(it)) if e else None
                    if e:
                        split_lo(eng, c + 6, chunk_it(it))
                    eng.wait_ge(S("gated"), e0 + e + 1 + per(it, 4))
                    eng.wait_ge(S("tile_done"), tiles_through(c + (5 if e else 3)) + per(it, 64))
                    eng.tensor_tensor(h_tok_hid, h_tok_hid, ps[:, UP_BANK, :], ALU.mult).then_inc(S("hid_made"), 1)
                    split_lo(eng, c + (7 if e else 5), chunk_it(it))
                    if i == 0 and q:
                        add(q - 1, it)

            group(0, None)
            with eng.Fori(0, 3) as it:
                group(1, it)
            hid_split(NE - 1, None)
            add(3, None)
            eng.sem_inc(S("norm_lo"), 2)

        def project_pe(eng, n, at, chunks, free=None):
            for i in range(2 * chunks):
                c = at + i // 2
                if i % 2 == 0:
                    eng.wait_ge(S("w_lo_made"), c + 1)
                if i >= 8:
                    eng.wait_ge(S(f"{n}_taken"), i - 7)
                mm = tile_product(eng, i % 8, c % W_RING, i % 2, KT, 2, h_hi, h_lo)
                mm.then_inc(S("tile_done"), 1)

        def out_proj_act(eng, at):
            for c in range(OUT_CHUNKS):
                split_hi(eng, at + c)

        def out_proj_dve(eng, n, at):
            split_lo(eng, at)
            split_lo(eng, at + 1)
            for i in range(KT):
                eng.wait_ge(S("tile_done"), tile(at, i))
                eng.tensor_tensor(xt[:, i, :], xt[:, i, :], ps[:, i, 0:T], ALU.add).then_inc(S(f"{n}_taken"), 1)
                if i in (1, 3):
                    split_lo(eng, at + 2 + i // 2)

        R_T, K_T, V_T = xs[:, 0:4, :], xs[:, 4:8, :], xs[:, 8:12, :]
        flat = lambda v: v.rearrange("p a b -> p (a b)")

        def prompt_sample(v, lead=0):
            return v[:, 0:TP], v[:, TP:T].rearrange("p (b s) -> p b s", b=NB)

        def ring_parts(j, lead):
            v = p_ring[:, j % 4, :]
            s = v[:, 257:329].rearrange("p (b s) -> p b s", b=NB)
            return v[:, 1 - lead:257 - lead], s[:, :, 1 - lead:9 - lead]

        def mix0_act(eng):
            eng.wait_ge(S("x_loaded"), 16)
            eng.wait_ge(S("constants_set"), 2)
            norm_act(eng, 0, True)
            split_hi(eng, AT_IN0)
            split_hi(eng, AT_IN0 + 1)
            eng.wait_ge(S("small_loaded"), 16 * 8)
            for i in range(2 * IN0_CHUNKS):
                eng.wait_ge(S("tile_done"), tile(AT_IN0, i))
                if i < A_TILES:
                    if i >= 4:
                        eng.wait_ge(S("shift_mixed"), i - 3)
                        eng.wait_ge(S("shift_kept"), i - 3)
                    else:
                        eng.wait_ge(S("constants_set"), 3)
                    a, b = ring_parts(i, 0)
                    pa, pb = prompt_sample(ps[:, i % 8, 0:T])
                    eng.activation(a, pa, ACT.Copy)
                    eng.activation(b, pb, ACT.Copy).then_inc(S("in0_taken"), 1)
                    v = p_ring[:, i % 4, 257:329].rearrange("p (b s) -> p b s", b=NB)
                    eng.activation(v[:, :, 0:1], shift0[:, i, :].unsqueeze(2), ACT.Copy).then_inc(S("ring_filled"), 1)
                elif i < A_TILES + HT:
                    eng.activation(gu[:, i - A_TILES, :], ps[:, i % 8, 0:T], ACT.Gelu_apprx_tanh).then_inc(S("in0_taken"), 1)
                else:
                    eng.activation(gv[:, i - A_TILES - HT, :], ps[:, i % 8, 0:T], ACT.Gelu_apprx_tanh).then_inc(S("in0_taken"), 1)
                if i % 2 and i // 2 + 2 < IN0_CHUNKS:
                    split_hi(eng, AT_IN0 + i // 2 + 2)
            eng.wait_ge(S("shift_mixed"), A_TILES)
            eng.activation(xs[0:64, 12, :], xs[0:64, 12, :], ACT.Tanh).then_inc(S("lora_in"), 1)
            eng.activation(xs[:, 13, :], xs[:, 13, :], ACT.Sigmoid).then_inc(S("lora_in"), 1)
            for j in range(HT):
                eng.wait_ge(S("lora_done"), j + 1)
                eng.activation(s1[:, j, :], ps[:, j, 0:T], ACT.Sigmoid, bias=par("decay_w0", j)).then_inc(S("decay_sig"), 1)
            for j in range(HT):
                eng.wait_ge(S("lora_done"), 4 + j + 1)
                eng.activation(s4[:, j, :], ps[:, 4 + j, 0:T], ACT.Sigmoid, bias=par("iclr_a0", j)).then_inc(S("iclr_made"), 1)
            eng.wait_ge(S("sgu_sums"), 2)
            eng.activation(g_root, ps[:, 1, 0:T], ACT.Sqrt, bias=eps_norm, scale=1.0 / 512).then_inc(S("sgu_root"), 1)
            for i in range(3):
                eng.wait_ge(S("vn_turned"), i + 1)
                n = P if i < 2 else TS
                eng.activation(vn_tok[0:n, i, :], ps[0:n, 2 + i, :], ACT.Copy).then_inc(S("vn_tok_made"), 1)
            eng.wait_ge(S("gmlp_made"), HT)
            eng.activation(h_hi[:, 4:8, :], gu, ACT.Copy).then_inc(S("y_hi"), 1)
            eng.wait_ge(S("log_run"), HT)
            eng.activation(s3, s2, ACT.Exp).then_inc(S("decays_made"), 1)
            eng.wait_ge(S("log_prev"), 1)
            eng.activation(s1, s1, ACT.Exp).then_inc(S("decays_made"), 1)
            eng.activation(s2, s2, ACT.Exp, scale=-1.0).then_inc(S("decays_made"), 1)
            eng.wait_ge(S("kk_clamped"), 1)
            eng.activation(s5, s5, ACT.Sqrt).then_inc(S("kk_root"), 1)
            for g in range(3):
                wkv_group_act(eng, g)
            eng.wait_ge(S("head_sums"), 16)
            for j in range(HT):
                eng.activation(s5[:, j, :], ps[:, 4 + j, 0:T], ACT.Sqrt, bias=eps_gn, scale=1.0 / 64).then_inc(S("gn_root"), 1)
            eng.wait_ge(S("gn_scaled"), 1)
            for j in range(HT):
                eng.activation(s1[:, j, :], s1[:, j, :], ACT.Identity, bias=par("lnx_b", j), scale=par("lnx_g", j)).then_inc(S("gn_affine"), 1)
            eng.wait_ge(S("ya_made"), 1)
            eng.activation(h_hi[:, 0:4, :], s1, ACT.Copy).then_inc(S("y_hi"), 1)

        def mix0_dve(eng):
            eng.memset(small[:, 0:60], 0.0).then_inc(S("constants_set"), 1)
            eng.memset(eps_norm, 1e-6)
            eng.memset(eps_gn, 64e-5).then_inc(S("constants_set"), 1)
            eng.memset(p_ring[:, :, 0:1], 0.0).then_inc(S("constants_set"), 1)
            eng.wait_ge(S("small_loaded"), 16 * 8)
            norm_dve(eng, 0, "norm_mix0", True)
            split_lo(eng, AT_IN0)
            split_lo(eng, AT_IN0 + 1)
            for i in range(A_TILES):
                eng.wait_ge(S("ring_filled"), i + 1)
                if i >= 2:
                    eng.wait_ge(S("shift_mixed"), i - 1)
                d = prompt_sample(d_ring[:, i % 2, :])
                now, before, to = ring_parts(i, 0), ring_parts(i, 1), prompt_sample(xs[:, i, :])
                eng.tensor_tensor(d[0], before[0], now[0], ALU.subtract)
                eng.tensor_tensor(d[1], before[1], now[1], ALU.subtract).then_inc(S("shift_diff"), 1)
                eng.wait_ge(S("shift_diff"), i + 1)
                eng.scalar_tensor_tensor(to[0], d[0], par("shift_mu", i), now[0], ALU.mult, ALU.add)
                eng.scalar_tensor_tensor(to[1], d[1], par("shift_mu", i), now[1], ALU.mult, ALU.add).then_inc(S("shift_mixed"), 1)
                if i % 2 and i // 2 + 2 < IN0_CHUNKS:
                    split_lo(eng, AT_IN0 + i // 2 + 2)
            for c in range(A_TILES // 2 + 2, IN0_CHUNKS):
                split_lo(eng, AT_IN0 + c)
            eng.wait_ge(S("shift_mixed"), A_TILES)
            next_reads(eng, eng.tensor_tensor(s6, K_T, par_over("key_k", HT, T), ALU.mult))
            eng.tensor_tensor(s5, s6, s6, ALU.mult).then_inc(S("kk_sq"), 1)
            eng.wait_ge(S("decay_sig"), HT)
            next_reads(eng, eng.tensor_scalar(s1, s1, -0.6065306597126334, None, ALU.mult))
            for j in range(HT):
                eng.tensor_tensor_scan(s2[:, j, :], const("reset"), s1[:, j, :], 0.0, ALU.mult, ALU.add).then_inc(S("log_run"), 1)
            eng.wait_ge(S("log_run"), HT)
            eng.tensor_tensor(s1, s2, s1, ALU.subtract).then_inc(S("log_prev"), 1)
            eng.wait_ge(S("sgu_sums"), 1)
            next_reads(eng, eng.tensor_scalar(g_rstd, ps[:, 0, 0:T], 1.0 / 512, None, ALU.mult))
            eng.wait_ge(S("shift_kept"), A_TILES)
            next_reads(eng, eng.tensor_tensor(gv, gv, g_rstd.unsqueeze(1).broadcast_to((P, HT, T)), ALU.subtract))
            eng.tensor_tensor(sq_gv, gv, gv, ALU.mult).then_inc(S("sgu_sq"), 1)
            eng.wait_ge(S("sgu_root"), 1)
            next_reads(eng, eng.reciprocal(g_rstd, g_root))
            for j in range(HT):
                last = eng.scalar_tensor_tensor(gv[:, j, :], gv[:, j, :], par("sgu_g", j), g_rstd, ALU.mult, ALU.mult)
            next_reads(eng, last)
            eng.tensor_tensor(gv, gv, par_over("sgu_b", HT, T), ALU.add).then_inc(S("vn_made"), 1)
            eng.wait_ge(S("vn_made"), 1)
            eng.tensor_tensor(sw, sw, const("tri").unsqueeze(1).broadcast_to((P, HT, P)), ALU.mult)
            eng.tensor_tensor(sw8, sw8, const("mask_sample", TS)[:, 64:128].unsqueeze(1).broadcast_to((TS, HT, TS)), ALU.mult)\
               .then_inc(S("sgu_masked"), 1)
            for j in range(HT):
                eng.wait_ge(S("gated_sums"), j + 1)
                next_reads(eng, eng.tensor_tensor(sbias[:, j, :], sbias[:, j, :], ps[:, 4 + j, 0:T], ALU.add))
                eng.tensor_tensor(gu[:, j, :], gu[:, j, :], sbias[:, j, :], ALU.mult).then_inc(S("gmlp_made"), 1)
            eng.wait_ge(S("y_hi"), 1)
            eng.tensor_tensor(h_lo[:, 4:8, :], gu, h_hi[:, 4:8, :], ALU.subtract).then_inc(S("y_lo"), 1)
            eng.wait_ge(S("head_sums"), 4)
            eng.tensor_scalar(s5, ps[:, 0:4, 0:T], 1e-24, None, ALU.max).then_inc(S("kk_clamped"), 1)
            eng.wait_ge(S("decays_made"), 1)
            v5 = lambda v: v.rearrange("p j (c t) -> p j c t", c=N_CHUNKS)
            eng.tensor_tensor(ar[:, :, :, 1, :], v5(R_T), v5(s3), ALU.mult)
            eng.tensor_copy(w_end[:, :, 0:4], v5(s3)[:, :, 0:4, C - 1])
            next_reads(eng, eng.tensor_copy(w_end[:, :, 4:12], s3[:, :, TP:T].rearrange("p j (b s) -> p j b s", b=NB)[:, :, :, NS - 1]))
            eng.wait_ge(S("iclr_made"), HT)
            for j in range(HT):
                last = eng.tensor_scalar(s3[:, j, :], s4[:, j, :], 1.0, par("key_a", j), ALU.subtract, ALU.mult)
            next_reads(eng, last)
            next_reads(eng, eng.scalar_tensor_tensor(flat(K_T), flat(s3), 1.0, flat(K_T), ALU.add, ALU.mult))
            eng.wait_ge(S("kk_root"), 1)
            next_reads(eng, eng.reciprocal(s5, s5))
            next_reads(eng, eng.tensor_tensor(s6, s6, s5, ALU.mult))
            next_reads(eng, eng.tensor_tensor(R_T, R_T, K_T, ALU.mult))
            eng.tensor_tensor(s5, R_T, par_over("bonus", HT, T), ALU.mult).then_inc(S("bonus_in"), 1)
            eng.wait_ge(S("decays_made"), 2)
            eng.tensor_tensor(ar[:, :, :, 0, :], v5(s6), v5(s1), ALU.mult)
            next_reads(eng, eng.scalar_tensor_tensor(flat(s4), flat(s4), -1.0, flat(s6), ALU.mult, ALU.mult))
            eng.wait_ge(S("decays_made"), 3)
            eng.tensor_tensor(s4, s4, s2, ALU.mult)
            eng.tensor_tensor(K_T, K_T, s2, ALU.mult).then_inc(S("wkv_operands"), 1)
            eng.wait_ge(S("head_sums"), 8)
            eng.tensor_tensor(R_T, V_T, ps[:, 0:4, 0:T], ALU.mult).then_inc(S("bonus_made"), 1)
            eng.wait_ge(S("wkv0_loaded"), 16)
            eng.wait_ge(S("shift_stored"), 16)
            eng.memset(state[:, :, :], 0.0).then_inc(S("state_made"), 1)
            eng.wait_ge(S("chunk_v_stored"), 16)
            for g in range(3):
                wkv_group_dve(eng, g)
            eng.wait_ge(S("head_sums"), 12)
            next_reads(eng, eng.scalar_tensor_tensor(s1, ps[:, 0:4, 0:T], -1.0 / 64, s1, ALU.mult, ALU.add))
            eng.tensor_tensor(s5, s1, s1, ALU.mult).then_inc(S("gn_sq"), 1)
            eng.wait_ge(S("gn_root"), HT)
            next_reads(eng, eng.reciprocal(s5, s5))
            eng.tensor_tensor(s1, s1, s5, ALU.mult).then_inc(S("gn_scaled"), 1)
            eng.wait_ge(S("gn_affine"), HT)
            next_reads(eng, eng.tensor_tensor(s1, s1, R_T, ALU.add))
            eng.wait_ge(S("gate_up"), HT)
            eng.tensor_tensor(s1, s1, ps[:, 0:4, 0:T], ALU.mult).then_inc(S("ya_made"), 1)
            eng.wait_ge(S("y_hi"), 2)
            eng.tensor_tensor(h_lo[:, 0:4, :], s1, h_hi[:, 0:4, :], ALU.subtract).then_inc(S("y_lo"), 1)

        sq_gv = take(G0 + 6144, HT, T)

        def mix0_pe(eng):
            eng.wait_ge(S("small_loaded"), 16 * 8)
            norm_pe(eng, 0)
            eng.wait_ge(S("norm_lo"), 2)
            project_pe(eng, "in0", AT_IN0, IN0_CHUNKS)
            eng.wait_ge(S("in0_taken"), 2 * IN0_CHUNKS)
            eng.wait_ge(S("lora_in"), 2)
            for j in range(HT):
                eng.matmul(ps[:, j, 0:T], lora[0:64, 0, P * j:P * j + P], xs[0:64, 12, :], start=True, stop=True).then_inc(S("lora_done"), 1)
            for j in range(HT):
                eng.matmul(ps[:, 4 + j, 0:T], lora[64:128, 0, P * j:P * j + P], xs[64:128, 12, :], start=True, stop=True).then_inc(S("lora_done"), 1)
            eng.wait_ge(S("decay_sig"), HT)
            for j in range(HT):
                mm = eng.matmul(ps[:, 0, 0:T], ones, gv[:, j, :], start=(j == 0), stop=(j == HT - 1))
            mm.then_inc(S("sgu_sums"), 1)
            eng.wait_ge(S("sgu_sq"), 1)
            for j in range(HT):
                mm = eng.matmul(ps[:, 1, 0:T], ones, sq_gv[:, j, :], start=(j == 0), stop=(j == HT - 1))
            mm.then_inc(S("sgu_sums"), 1)
            eng.wait_ge(S("vn_made"), 1)
            eng.wait_ge(S("iclr_made"), HT)
            for i, (a, b) in enumerate(((0, 128), (128, 256), (256, 320))):
                for j in range(HT):
                    mm = eng.transpose(ps[0:b - a, 2 + i, P * j:P * j + P], gv[:, j, a:b], ident)
                mm.then_inc(S("vn_turned"), 1)
            eng.wait_ge(S("sgu_masked"), 1)
            eng.wait_ge(S("vn_tok_made"), 3)
            for j in range(HT):
                for i in range(2):
                    eng.matmul(ps[:, 4 + j, P * i:P * i + P], vn_tok[:, i, P * j:P * j + P], sw[:, j, :], start=True, stop=True)
                eng.matmul(ps[:, 4 + j, TP:T], vn_tok[0:TS, 2, P * j:P * j + P], sw8[:, j, :], start=True, stop=True).then_inc(S("gated_sums"), 1)
            eng.wait_ge(S("kk_sq"), 1)
            for j in range(HT):
                eng.matmul(ps[:, j, 0:T], head_ones, s5[:, j, :], start=True, stop=True).then_inc(S("head_sums"), 1)
            eng.wait_ge(S("bonus_in"), 1)
            for j in range(HT):
                eng.matmul(ps[:, j, 0:T], head_ones, s5[:, j, :], start=True, stop=True).then_inc(S("head_sums"), 1)
            eng.wait_ge(S("wkv_operands"), 1)
            eng.wait_ge(S("bonus_made"), 1)
            eng.wait_ge(S("y_lo"), 1)
            for g in range(3):
                wkv_group_pe(eng, g)
            eng.wait_ge(S("y_made"), 5)
            eng.wait_ge(S("sample_state"), 8)
            for j in range(HT):
                eng.matmul(ps[:, j, 0:T], head_ones, s1[:, j, :], start=True, stop=True).then_inc(S("head_sums"), 1)
            eng.wait_ge(S("gn_sq"), 1)
            for j in range(HT):
                eng.matmul(ps[:, 4 + j, 0:T], head_ones, s5[:, j, :], start=True, stop=True).then_inc(S("head_sums"), 1)
            for j in range(HT):
                eng.matmul(ps[:, j, 0:T], lora[:, 1, P * j:P * j + P], xs[:, 13, :], start=True, stop=True).then_inc(S("gate_up"), 1)
            eng.wait_ge(S("y_lo"), 2)

        def heads():
            return [(h, 64 * (h % 2), h // 2, (h % 2) * HT + h // 2) for h in (0, 2, 4, 6, 1, 3, 5, 7)]

        def parts(g):
            return [(2 * g, 0), (2 * g + 1, 64)] if g < 2 else [(4, 0)]

        def half(bank, par, n=64):
            return ps[:, bank + par, 0:HT * n].rearrange("p (j t) -> p j t", j=HT)

        def wkv_group_pe(eng, g):
            rows = P if g < 2 else 64

            def each(fn):
                for h, ho, j, s in heads():
                    for c, o in parts(g):
                        mm = fn(h, ho, j, s, c, o)
                return mm

            def small(bank, lhs, rhs):
                return each(lambda h, ho, j, s, c, o: eng.matmul(
                    half(bank, h % 2)[o:o + 64, j, :], lhs[o:o + 64, s, :], rhs[o:o + 64, s, :], start=True, stop=True))

            if g:
                eng.wait_ge(S("y_made"), 2 * g)
                eng.wait_ge(S("state_made"), 2 * g + 1)
            each(lambda h, ho, j, s, c, o: eng.matmul(
                half(0, h % 2, 128)[o:o + 64, j, :], s4[ho:ho + 64, j, C * c:C * c + C],
                ar[ho:ho + 64, j, c, :, :].rearrange("p w t -> p (w t)"), start=True, stop=True)).then_inc(S("gram"), 1)
            each(lambda h, ho, j, s, c, o: eng.matmul(
                half(4, h % 2)[o:o + 64, j, :], ar[ho:ho + 64, j, c, 0, :], s4[ho:ho + 64, j, C * c:C * c + C],
                start=True, stop=True)).then_inc(S("gram"), 1)
            each(lambda h, ho, j, s, c, o: eng.matmul(
                half(2, h % 2, 128)[o:o + 64, j, :], K_T[ho:ho + 64, j, C * c:C * c + C],
                ar[ho:ho + 64, j, c, :, :].rearrange("p w t -> p (w t)"), start=True, stop=True)).then_inc(S("gram"), 1)
            a, b = C * parts(g)[0][0], C * parts(g)[0][0] + rows
            for bank, v in ((6, V_T), (7, s4)):
                for j in range(HT):
                    mm = eng.transpose(ps[0:rows, bank, P * j:P * j + P], v[:, j, a:b], ident)
                mm.then_inc(S("turned"), 1)
            n = 3 if g < 2 else 0
            eng.wait_ge(S("diag_made"), g + 1)
            eng.wait_ge(S("gram_kept"), 4 * g + 2)
            small(0, ee, dd).then_inc(S("solve"), 1)
            small(4, dd, ee).then_inc(S("solve"), 1)
            eng.wait_ge(S("gram_kept"), 4 * g + 4)
            for j in range(HT):
                mm = eng.transpose(ps[0:rows, 2, P * j:P * j + P], K_T[:, j, a:b], ident)
            mm.then_inc(S("turned"), 1)
            eng.wait_ge(S("tok_kept"), 3 * g + 2)
            base = SOLVES[g]
            eng.wait_ge(S("solve_kept"), base + 1)
            small(0, qq, d2).then_inc(S("solve"), 1)
            small(6, e2, d2).then_inc(S("solve"), 1)
            small(4, d2, qq).then_inc(S("solve"), 1)
            eng.wait_ge(S("solve_kept"), base + 2)
            small(0, qq, d2).then_inc(S("solve"), 1)
            small(4, d2, qq).then_inc(S("solve"), 1)
            for i, low in enumerate((lo16, lo32, lo64)[:n]):
                eng.wait_ge(S("solve_kept"), base + 3 + 2 * i)
                small(6, low, pp).then_inc(S("solve"), 1)
                eng.wait_ge(S("solve_kept"), base + 4 + 2 * i)
                small(0, qq, d2).then_inc(S("solve"), 1)
                if i < 2:
                    small(4, d2, qq).then_inc(S("solve"), 1)
            eng.wait_ge(S("solve_kept"), base + 3 + 2 * n)
            eng.wait_ge(S("tok_kept"), 3 * g + 3)
            each(lambda h, ho, j, s, c, o: eng.matmul(
                half(6, h % 2)[o:o + 64, j, :], gk_m[o:o + 64, s, 0:64], v_tok[o:o + 64, h, :], start=True, stop=True)).then_inc(S("akv"), 1)
            eng.wait_ge(S("akv_kept"), g + 1)
            for c, o in parts(g):
                if g < 2:
                    eng.wait_ge(S("state_made"), c + 1)
                    eng.wait_ge(S("y_made"), c)
                    for h, ho, j, s in heads():
                        mm = eng.matmul(half(0, h % 2)[o:o + 64, j, :], ar[ho:ho + 64, j, c, 0, :], state[ho:ho + 64, j, :], start=True, stop=True)
                    mm.then_inc(S("a_s"), 1)
                    for h, ho, j, s in heads():
                        mm = eng.matmul(half(4, h % 2)[ho:ho + 64, j, :], state[ho:ho + 64, j, :], ar[ho:ho + 64, j, c, 1, :], start=True, stop=True)
                    mm.then_inc(S("r_s"), 1)
                else:
                    for h, ho, j, s in heads():
                        for b in range(NB):
                            mm = eng.matmul(ps[ho:ho + 64, h % 2, P * j:P * j + P].rearrange("p (w t) -> p w t", w=2)[:, :, NS * b:NS * b + NS],
                                            swkv[ho:ho + 64, j, b, :], ar[ho:ho + 64, j, c, :, NS * b:NS * b + NS], start=True, stop=True)
                    mm.then_inc(S("sample_s"), 1)
                    eng.wait_ge(S("sample_as_kept"), 1)
                    for j in range(HT):
                        mm = eng.transpose(ps[0:TS, 2, P * j:P * j + P], d2_full[:, j, :], ident)
                    mm.then_inc(S("a_s"), 1)
                eng.wait_ge(S("rhs_made"), c + 1)
                for h, ho, j, s in heads():
                    mm = eng.matmul(ps[o:o + 64, 6, 64 * s:64 * s + 64], pp[o:o + 64, s, :], ee[o:o + 64, s, :], start=True, stop=True)
                mm.then_inc(S("q_done"), 1)
                eng.wait_ge(S("q_kept"), c + 1)
                for h, ho, j, s in heads():
                    out = ps[ho:ho + 64, 2, 64 * j:64 * j + 64]
                    eng.matmul(out, e2[o:o + 64, s, :], gb_m[o:o + 64, s, 64:128], start=True, stop=False)
                    mm = eng.matmul(out, v_tok[o:o + 64, h, :], gk_m[o:o + 64, s, 64:128], start=False, stop=True)
                mm.then_inc(S("y_rest"), 1)
                if g < 2:
                    for h, ho, j, s in heads():
                        out = ps[ho:ho + 64, 3, 64 * j:64 * j + 64]
                        eng.matmul(out, b_tok[o:o + 64, h, :], e2[o:o + 64, s, :], start=True, stop=False)
                        mm = eng.matmul(out, k_tok[o:o + 64, h, :], v_tok[o:o + 64, h, :], start=False, stop=True)
                    mm.then_inc(S("state_add"), 1)
                else:
                    for n_, (h, ho, j, s) in enumerate(heads()):
                        eng.wait_ge(S("qe_made"), n_ + 1)
                        eng.wait_ge(S("ve_made"), n_ + 1)
                        bank = SAMPLE_BANKS[n_ % 4]
                        if n_ >= 4:
                            eng.wait_ge(S("sample_state"), n_ - 3)
                        eng.matmul(ps[ho:ho + 64, bank, :], b_tok[0:64, h, :], qe[:, n_ % 2, :], start=True, stop=False)
                        eng.matmul(ps[ho:ho + 64, bank, :], k_tok[0:64, h, :], ve[:, n_ % 2, :], start=False, stop=True)\
                           .then_inc(S("sample_add"), 1)

        SOLVES = (0, 9, 18)
        SAMPLE_BANKS = (4, 5, 6, 7)
        d2_full = take(G0 + 2048 + 512 * 4, HT, TS)

        def wkv_group_act(eng, g):
            rows = P if g < 2 else 64
            for i, (bank, to) in enumerate(((6, v_tok), (7, b_tok), (2, k_tok))):
                eng.wait_ge(S("turned"), 3 * g + i + 1)
                eng.activation(to[0:rows, :, :].rearrange("p h v -> p (h v)"), ps[0:rows, bank, :], ACT.Copy).then_inc(S("tok_kept"), 1)

        def wkv_group_dve(eng, g):
            rows = P if g < 2 else 64
            n = 3 if g < 2 else 0
            base = SOLVES[g]
            mask = const("mask_prompt" if g < 2 else "mask_sample", rows)
            over = lambda m, k: m.unsqueeze(1).broadcast_to((rows, HT, k))
            done0 = sum(per_group(i) for i in range(g))

            def kept(ins_):
                ins_.then_inc(S("solve_kept"), 1)

            def wait_solve(k):
                eng.wait_ge(S("solve"), done0 + k)

            sl = lambda v: v[0:rows, :, :]
            q4 = lambda v, par: v[0:rows, HT * par:HT * par + HT, :]
            eng.wait_ge(S("gram"), 3 * g + 1)
            for par in range(2):
                eng.tensor_tensor(q4(gb_m, par), half(0, par, 128)[0:rows], over(mask, 128), ALU.mult).then_inc(S("gram_kept"), 1)
            eng.wait_ge(S("gram_kept"), 4 * g + 2)
            d8 = const("diag8", rows).unsqueeze(1).broadcast_to((rows, 8, 64))
            eye = const("eye64", rows).unsqueeze(1).broadcast_to((rows, 8, 64))
            next_reads(eng, eng.tensor_tensor(sl(dd), gb_m[0:rows, :, 0:64], d8, ALU.mult))
            eng.wait_ge(S("gram"), 3 * g + 2)
            for par in range(2):
                eng.tensor_tensor(q4(ee, par), half(4, par)[0:rows], over(const("low8", rows), 64), ALU.mult)
                for low, name in ((lo16, "low16"), (lo32, "low32"), (lo64, "low64"))[:n]:
                    eng.tensor_tensor(q4(low, par), half(4, par)[0:rows], over(const(name, rows), 64), ALU.mult)
            eng.tensor_tensor(sl(pp), sl(dd), eye, ALU.add).then_inc(S("diag_made"), 1)
            eng.wait_ge(S("gram"), 3 * g + 3)
            for par in range(2):
                eng.tensor_tensor(q4(gk_m, par), half(2, par, 128)[0:rows], over(mask, 128), ALU.mult).then_inc(S("gram_kept"), 1)
            eng.wait_ge(S("gram_kept"), 4 * g + 4)
            next_reads(eng, eng.tensor_tensor(sl(qq), sl(ee), eye, ALU.add))

            def take2(to, bank, add=None):
                for par in range(2):
                    if add is None:
                        last = eng.tensor_copy(q4(to, par), half(bank, par)[0:rows])
                    else:
                        last = eng.tensor_tensor(q4(to, par), q4(to, par), half(bank, par)[0:rows], ALU.add)
                return last

            wait_solve(1)
            take2(d2, 0)
            wait_solve(2)
            kept(take2(e2, 4))
            wait_solve(5)
            take2(pp, 0, True)
            take2(d2, 6)
            kept(take2(qq, 4, True))
            eng.wait_ge(S("solve_kept"), base + 2)
            wait_solve(7)
            take2(pp, 0, True)
            kept(take2(qq, 4, True))
            at = 7
            for i in range(n):
                eng.wait_ge(S("solve_kept"), base + 3 + 2 * i)
                wait_solve(at + 1)
                kept(take2(d2, 6))
                wait_solve(at + 2 + (i < 2))
                last = take2(pp, 0, True)
                if i < 2:
                    last = take2(qq, 4, True)
                kept(last)
                at += 2 + (i < 2)
            eng.wait_ge(S("akv"), g + 1)
            take2(dd, 6).then_inc(S("akv_kept"), 1)
            eng.wait_ge(S("akv_kept"), g + 1)
            for c, o in parts(g):
                r = slice(o, o + 64)
                y = s1[:, :, C * c:C * c + C]
                if g == 2:
                    eng.wait_ge(S("sample_s"), 1)
                    for par in range(2):
                        ho = 64 * par
                        v = ps[ho:ho + 64, par, :].rearrange("p (j w t) -> p j w t", j=HT, w=2)
                        eng.tensor_copy(d2_full[ho:ho + 64], v[:, :, 0, :])
                        last = eng.tensor_copy(y[ho:ho + 64], v[:, :, 1, :])
                    last.then_inc(S("sample_as_kept"), 1)
                    eng.wait_ge(S("sample_as_kept"), 1)
                eng.wait_ge(S("a_s"), c + 1)
                for par in range(2):
                    src = half(0, par)[r] if g < 2 else ps[r, 2, :].rearrange("p (j w t) -> p j w t", j=HT, w=2)[:, :, par, :]
                    last = eng.tensor_tensor(ee[r, HT * par:HT * par + HT, :], dd[r, HT * par:HT * par + HT, :], src, ALU.add)
                last.then_inc(S("rhs_made"), 1)
                if g < 2:
                    eng.wait_ge(S("r_s"), c + 1)
                    for par in range(2):
                        ho = 64 * par
                        last = eng.tensor_copy(y[ho:ho + 64], half(4, par)[ho:ho + 64])
                    next_reads(eng, last)
                eng.wait_ge(S("q_done"), c + 1)
                eng.tensor_copy(e2[r, :, :], ps[r, 6, :].rearrange("p (s v) -> p s v", s=8)).then_inc(S("q_kept"), 1)
                eng.wait_ge(S("y_rest"), c + 1)
                eng.tensor_tensor(y, y, ps[:, 2, 0:256].rearrange("p (j t) -> p j t", j=HT), ALU.add).then_inc(S("y_made"), 1)
                if g < 2:
                    eng.wait_ge(S("state_add"), c + 1)
                    next_reads(eng, eng.tensor_tensor(state[:, :, :], state[:, :, :], ps[:, 3, 0:256].rearrange("p (j t) -> p j t", j=HT), ALU.add))
                    eng.tensor_tensor(state[:, :, :], state[:, :, :], w_end[:, :, c:c + 1].broadcast_to((P, HT, 64)), ALU.mult)\
                       .then_inc(S("state_made"), 1)
                    eng.wait_ge(S("state_made"), c + 2)
            if g == 2:
                own = const("own_batch", TS).unsqueeze(2).broadcast_to((TS, NB, 64))
                eng.wait_ge(S("q_kept"), 5)

                def spread(n_):
                    h, ho, j, s = heads()[n_]
                    if n_ >= 2:
                        eng.wait_ge(S("sample_add"), n_ - 1)
                    eng.tensor_tensor(qe[:, n_ % 2, :].rearrange("p (b v) -> p b v", b=NB), e2[0:TS, s, :].unsqueeze(1).broadcast_to((TS, NB, 64)),
                                      own, ALU.mult).then_inc(S("qe_made"), 1)

                spread(0)
                spread(1)
                for n_, (h, ho, j, s) in enumerate(heads()):
                    eng.wait_ge(S("sample_add"), n_ + 1)
                    if n_ + 2 < 8:
                        spread(n_ + 2)
                    v = swkv[ho:ho + 64, j, :, :]
                    bank = SAMPLE_BANKS[n_ % 4]
                    next_reads(eng, eng.tensor_tensor(v, v, ps[ho:ho + 64, bank, :].rearrange("p (b v) -> p b v", b=NB), ALU.add))
                    eng.tensor_tensor(v, v, w_end[ho:ho + 64, j, 4:12].unsqueeze(2).broadcast_to((64, NB, 64)), ALU.mult)\
                       .then_inc(S("sample_state"), 1)

        def wkv_group_pool(eng):
            own = const("own_batch", TS).unsqueeze(2).broadcast_to((TS, NB, 64))
            eng.wait_ge(S("sample_s"), 1)
            eng.wait_ge(S("tok_kept"), 9)
            for n_, (h, ho, j, s) in enumerate(heads()):
                if n_ >= 2:
                    eng.wait_ge(S("sample_add"), n_ - 1)
                eng.tensor_tensor(ve[:, n_ % 2, :].rearrange("p (b v) -> p b v", b=NB), v_tok[0:TS, h, :].unsqueeze(1).broadcast_to((TS, NB, 64)),
                                  own, ALU.mult).then_inc(S("ve_made"), 1)

        def per_group(g):
            return 7 + (8 if g < 2 else 0)


        def mix0_pool(eng):
            eng.wait_ge(S("small_loaded"), 16 * 8)
            for i in range(A_TILES):
                eng.wait_ge(S("ring_filled"), i + 1)
                v = p_ring[:, i % 4, :]
                eng.tensor_copy(shift_out[:, i, 0:1], v[:, 256:257])
                eng.tensor_copy(shift_out[:, i, 1:9], v[:, 257:329].rearrange("p (b s) -> p b s", b=NB)[:, :, NS]).then_inc(S("shift_kept"), 1)


        KV_RING = 4
        kv = take(5760, KV_RING, 2048)
        bias_p, bias_s = take(13952, 8, 384), take(17024, OLD_KEYS + 4 * TS)
        lru_w = take(18304, 2, HT, P)
        conv0, lru0 = take(19328, HT, NB, 3), take(19424, HT, NB)
        count_p, count_s = take(19456, 384), take(19840, OLD_KEYS + 4 * TS)
        XW = 3 + TP + NB * (3 + NS)
        xe = take(19456, HT, XW)
        lru_m = take(20844, HT, T)
        lru_t = take(19456, HT, T)
        q1, k1, v1, gy = (take(1280 * i, HT, T) for i in range(4))
        xc, lru_a, lru_i = h32[:, 0:4, :], h32[:, 4:8, :], hid[:, :, :]
        v1_tok = take(3840, 3, 512)
        score_s = take(18304, 2, OLD_KEYS + TS)
        pt_s = h32[:, :, :].rearrange("p a b -> p (a b)")[:, 0:2 * 7 * P].rearrange("p (a b c) -> p a b c", a=2, b=7)
        o_masked = take(20480, 512)
        qx = hid[:, :, :].rearrange("p a b -> p (a b)")[:, 0:1024].rearrange("p (r b j n) -> p r b j n", r=2, b=2, j=HT)
        score_p = take(20992, 2, 384)
        pt_p = (take(5376, 384), take(21760, 384))
        conv_out = state_flat[:, 0:108].rearrange("p (a b) -> p a b", a=HT)
        lru_out = state_flat[:, 108:144].rearrange("p (a b) -> p a b", a=HT)
        stat_p = state_flat[:, 144:156].rearrange("p (r w n) -> p r w n", r=2, w=3)
        stat_s = state_flat[:, 156:164].rearrange("p (r w) -> p r w", r=2)
        lam = state_flat[:, 164:192].rearrange("p (w j) -> p w j", w=7)

        KV_UNITS = [(what, b, half) for what, pair in (("k", 0), ("k", 1), ("v", 0), ("k", 2), ("v", 1), ("k", 3), ("v", 2), ("v", 3))
                    for b in (2 * pair, 2 * pair + 1) for half in (0, 1)]
        kv_at = {u: n for n, u in enumerate(KV_UNITS)}

        def load_kv(eng, n):
            what, b, half = KV_UNITS[n]
            if n >= KV_RING:
                eng.wait_ge(S("kv_used"), n - KV_RING + 1)
            n_floats = 2048 if half else 1024
            eng.dma_start(kv[:, n % KV_RING, 0:n_floats], ins[f"{what}_{('far', 'near')[half]}"][b]).then_inc(S(f"kv_loaded{n % KV_RING}"), 16)

        def kv_ready(eng, what, b, half):
            n = kv_at[what, b, half]
            eng.wait_ge(S(f"kv_loaded{n % KV_RING}"), 16 * (n // KV_RING + 1))
            return kv[:, n % KV_RING, 0:2048 if half else 1024].rearrange("p (a b) -> p a b", a=4 if what == "k" or half else 2)

        def xe_parts(j, lead):
            v = xe[:, j, :]
            s = v[:, 3 + TP:XW].rearrange("p (b s) -> p b s", b=NB)
            return v[:, 3 - lead:3 - lead + TP], s[:, :, 3 - lead:3 - lead + NS]

        def mix1_act(eng):
            split_hi(eng, AT_IN1)
            split_hi(eng, AT_IN1 + 1)
            eng.wait_ge(S("lam_abs"), 1)
            eng.activation(lam[:, 1, :], lam[:, 1, :], ACT.Exp, scale=-1.0).then_inc(S("lam_logs"), 1)
            eng.wait_ge(S("lam_u"), 1)
            eng.activation(lam[:, 3, :], lam[:, 2, :], ACT.Ln).then_inc(S("lam_logs"), 1)
            eng.wait_ge(S("down_added"), 2 * HT * NE)
            norm_act(eng, 2, True)
            eng.wait_ge(S("biases_made"), 1)
            eng.wait_ge(S("xe_lead"), 1)
            for i in range(2 * IN1_CHUNKS):
                eng.wait_ge(S("tile_done"), tile(AT_IN1, i))
                src, j = ps[:, i % 8, 0:T], i % HT
                if i < 4:
                    eng.activation(gy[:, j, :], src, ACT.Gelu_apprx_tanh).then_inc(S("in1_taken"), 1)
                elif i < 8:
                    a, b = xe_parts(j, 0)
                    pa, pb = prompt_sample(src)
                    eng.activation(a, pa, ACT.Copy)
                    eng.activation(b, pb, ACT.Copy).then_inc(S("in1_taken"), 1)
                elif i < 12:
                    eng.activation(q1[:, j, :], src, ACT.Copy, scale=0.125).then_inc(S("in1_taken"), 1)
                else:
                    eng.activation((k1 if i < 16 else v1)[:, j, :], src, ACT.Copy).then_inc(S("in1_taken"), 1)
                if i % 2 and i // 2 + 2 < IN1_CHUNKS:
                    split_hi(eng, AT_IN1 + i // 2 + 2)
            for j in range(HT):
                eng.wait_ge(S("lru_gate"), j + 1)
                eng.activation(lru_a[:, j, :], ps[:, j, 0:T], ACT.Sigmoid, bias=par("rgate_b", j)).then_inc(S("lru_sig"), 1)
            for j in range(HT):
                eng.wait_ge(S("lru_gate"), HT + j + 1)
                eng.activation(lru_i[:, j, :], ps[:, 4 + j, 0:T], ACT.Sigmoid, bias=par("igate_b", j)).then_inc(S("lru_sig"), 1)
            eng.wait_ge(S("log_a"), 1)
            eng.activation(lru_m, lru_a, ACT.Tanh, scale=-1.0).then_inc(S("lru_exps"), 1)
            eng.activation(lru_a, lru_a, ACT.Exp).then_inc(S("lru_exps"), 1)
            eng.wait_ge(S("lru_square"), 1)
            eng.activation(lru_m, lru_m, ACT.Sqrt).then_inc(S("lru_mult"), 1)
            eng.wait_ge(S("yc_made"), 1)
            eng.activation(h_hi[:, 0:4, :], gy, ACT.Copy).then_inc(S("y_hi"), 1)
            eng.wait_ge(S("y_lo"), 3)
            for i in range(3):
                n = P if i < 2 else TS
                eng.wait_ge(S("v1_turned"), i + 1)
                eng.activation(v1_tok[0:n, i, :], ps[0:n, 5 + i, :], ACT.Copy).then_inc(S("v1_tok_made"), 1)

            def prompt_exp(h):
                r = h % 2
                eng.wait_ge(S("p_max"), h + 1)
                eng.activation(score_p[:, r, 0:P], score_p[:, r, 0:P], ACT.Exp, bias=stat_p[:, r, 0, 0:1], accum_out=stat_p[:, r, 1, 0:1])
                eng.activation(score_p[:, r, P:384], score_p[:, r, P:384], ACT.Exp, bias=stat_p[:, r, 0, 1:2], accum_out=stat_p[:, r, 1, 1:2])\
                   .then_inc(S("p_exp"), 1)

            def prompt_turned(h):
                eng.wait_ge(S("p_turned"), h + 1)
                eng.activation(pt_p[h % 2], ps[:, 2 + h % 2, 0:384], ACT.Copy).then_inc(S("p_tok_made"), 1)

            for h in range(9):
                if h < 8:
                    prompt_exp(h)
                if h >= 1:
                    prompt_turned(h - 1)

            def sample_exp(p):
                r = p % 2
                eng.wait_ge(S("s_max"), p + 1)
                eng.activation(score_s[:, r, :], score_s[:, r, :], ACT.Exp, bias=stat_s[:, r, 1:2], accum_out=stat_s[:, r, 2:3])\
                   .then_inc(S("s_exp"), 1)

            def sample_turned(p):
                r = p % 2
                for n, (a, b, rows) in enumerate(((0, 2, P), (2, 6, P), (6, 7, 64))):
                    eng.wait_ge(S("s_turned"), 3 * p + n + 1)
                    eng.activation(pt_s[0:rows, r, a:b, :].rearrange("p a b -> p (a b)"), ps[0:rows, 6 + n % 2, 0:P * (b - a)], ACT.Copy)\
                       .then_inc(S("s_tok_made"), 1)

            for p in range(5):
                if p < 4:
                    sample_exp(p)
                if p >= 1:
                    sample_turned(p - 1)
            eng.wait_ge(S("attn_out"), 2 + 4)
            eng.activation(h_hi[:, 4:8, :], q1, ACT.Copy).then_inc(S("y_hi"), 1)

        def mix1_dve(eng):
            split_lo(eng, AT_IN1)
            split_lo(eng, AT_IN1 + 1)
            at = PCOL["lambda"][0]
            l = params[:, at:at + HT]
            eng.wait_ge(S("states_stored"), 32)
            next_reads(eng, eng.tensor_scalar(lam[:, 0, :], l, -1.0, None, ALU.mult))
            eng.tensor_tensor(lam[:, 1, :], lam[:, 0, :], l, ALU.max).then_inc(S("lam_abs"), 1)
            eng.wait_ge(S("lam_logs"), 1)
            eng.tensor_scalar(lam[:, 2, :], lam[:, 1, :], 1.0, None, ALU.add).then_inc(S("lam_u"), 1)
            eng.wait_ge(S("lam_u"), 1)
            next_reads(eng, eng.tensor_scalar(lam[:, 4, :], lam[:, 2, :], 1.0, None, ALU.subtract))
            next_reads(eng, eng.tensor_tensor(lam[:, 4, :], lam[:, 1, :], lam[:, 4, :], ALU.subtract))
            next_reads(eng, eng.reciprocal(lam[:, 5, :], lam[:, 2, :]))
            next_reads(eng, eng.tensor_tensor(lam[:, 4, :], lam[:, 4, :], lam[:, 5, :], ALU.mult))
            eng.wait_ge(S("lam_logs"), 2)
            next_reads(eng, eng.tensor_tensor(lam[:, 4, :], lam[:, 4, :], lam[:, 3, :], ALU.add))
            next_reads(eng, eng.tensor_scalar(lam[:, 0, :], lam[:, 0, :], 0.0, None, ALU.max))
            next_reads(eng, eng.tensor_tensor(lam[:, 4, :], lam[:, 4, :], lam[:, 0, :], ALU.add))
            next_reads(eng, eng.tensor_scalar(lam[:, 6, :], lam[:, 4, :], -8.0, None, ALU.mult))
            norm_dve(eng, 2, "norm_mix1", True)
            eng.wait_ge(S("biases_made"), 1)
            eng.wait_ge(S("lru_loaded"), 48)
            eng.memset(xe[:, :, 0:3], 0.0)
            for j in range(HT):
                last = eng.tensor_copy(xe[:, j, 3 + TP:XW].rearrange("p (b s) -> p b s", b=NB)[:, :, 0:3], conv0[:, j, :, :])
            last.then_inc(S("xe_lead"), 1)
            eng.wait_ge(S("norm_lo"), 6)
            split_lo(eng, AT_IN1 + 2)
            split_lo(eng, AT_IN1 + 3)
            split_lo(eng, AT_IN1 + 4)
            for j in range(HT):
                eng.wait_ge(S("in1_taken"), 4 + j + 1)
                eng.wait_ge(S("xe_lead"), 1)
                to = prompt_sample(xc[:, j, :])
                for tap in range(4):
                    src = xe_parts(j, 3 - tap)
                    for n in range(2):
                        if tap == 0:
                            last = eng.tensor_scalar(to[n], src[n], par("conv_w", j), par("conv_b", j), ALU.mult, ALU.add)
                        else:
                            last = eng.scalar_tensor_tensor(to[n], src[n], par("conv_w", HT * tap + j), to[n], ALU.mult, ALU.add)
                    next_reads(eng, last)
                if j % 2:
                    split_lo(eng, AT_IN1 + 5 + j // 2)
            eng.tensor_copy(conv_out[:, :, 0:3], xe[:, :, TP:TP + 3])
            for j in range(HT):
                last = eng.tensor_copy(conv_out[:, j, 3:27].rearrange("p (b s) -> p b s", b=NB),
                                       xe[:, j, 3 + TP:XW].rearrange("p (b s) -> p b s", b=NB)[:, :, NS:NS + 3])
            last.then_inc(S("xc_made"), 1)
            for c in range(7, IN1_CHUNKS):
                split_lo(eng, AT_IN1 + c)
            eng.wait_ge(S("lru_sig"), HT)
            for j in range(HT):
                last = eng.tensor_scalar(lru_a[:, j, :], lru_a[:, j, :], lam[:, 6, j:j + 1], None, ALU.mult)
            last.then_inc(S("log_a"), 1)
            eng.wait_ge(S("lru_sig"), 2 * HT)
            next_reads(eng, eng.tensor_tensor(lru_i, lru_i, xc, ALU.mult))
            eng.wait_ge(S("lru_exps"), 2)
            next_reads(eng, eng.tensor_tensor(lru_t, lru_a, lru_a, ALU.mult))
            eng.scalar_tensor_tensor(flat(lru_m), flat(lru_t), 1.0, flat(lru_m), ALU.add, ALU.mult).then_inc(S("lru_square"), 1)
            eng.wait_ge(S("lru_mult"), 1)
            next_reads(eng, eng.memset(lru_m[:, :, 0:1], 1.0))
            next_reads(eng, eng.tensor_tensor(lru_m, lru_m, lru_i, ALU.mult))
            starts = lambda v: v[:, :, TP:T].rearrange("p j (b s) -> p j b s", b=NB)[:, :, :, 0]
            next_reads(eng, eng.tensor_tensor(lru0, lru0, starts(lru_a), ALU.mult))
            next_reads(eng, eng.tensor_tensor(starts(lru_m), starts(lru_m), lru0, ALU.add))
            next_reads(eng, eng.memset(starts(lru_a), 0.0))
            for j in range(HT):
                last = eng.tensor_tensor_scan(lru_i[:, j, :], lru_a[:, j, :], lru_m[:, j, :], 0.0, ALU.mult, ALU.add)
            next_reads(eng, last)
            eng.tensor_copy(lru_out[:, :, 0:1], lru_i[:, :, TP - 1:TP])
            eng.tensor_copy(lru_out[:, :, 1:9], lru_i[:, :, TP:T].rearrange("p j (b s) -> p j b s", b=NB)[:, :, :, NS - 1])\
               .then_inc(S("lru_kept"), 1)
            eng.tensor_tensor(gy, gy, lru_i, ALU.mult).then_inc(S("yc_made"), 1)
            eng.wait_ge(S("y_hi"), 3)
            eng.tensor_tensor(h_lo[:, 0:4, :], gy, h_hi[:, 0:4, :], ALU.subtract).then_inc(S("y_lo"), 1)
            eng.wait_ge(S("y_lo"), 3)
            eng.memset(v1_tok[64:128, 2, :], 0.0)
            for r in range(2):
                last = eng.memset(pt_s[64:128, r, 6, :], 0.0)
            last.then_inc(S("pads_zeroed"), 1)

            def prompt_max(h):
                r = h % 2
                eng.wait_ge(S("p_scores"), h + 1)
                if h >= 2:
                    eng.wait_ge(S("p_turned"), h - 1)
                next_reads(eng, eng.tensor_tensor(score_p[:, r, :], ps[:, r, 0:384], bias_p[:, h, :], ALU.add))
                eng.tensor_reduce(stat_p[:, r, 2, 0:1], score_p[:, r, 0:P], AX, ALU.max)
                next_reads(eng, eng.tensor_reduce(stat_p[:, r, 2, 1:2], score_p[:, r, P:384], AX, ALU.max))
                eng.tensor_scalar(stat_p[:, r, 0, :], stat_p[:, r, 2, :], -1.0, None, ALU.mult).then_inc(S("p_max"), 1)

            def prompt_norm(h):
                r = h % 2
                eng.wait_ge(S("p_exp"), h + 1)
                next_reads(eng, eng.reciprocal(stat_p[:, r, 2, :], stat_p[:, r, 1, :]))
                eng.tensor_scalar(score_p[:, r, 0:P], score_p[:, r, 0:P], stat_p[:, r, 2, 0:1], None, ALU.mult)
                eng.tensor_scalar(score_p[:, r, P:384], score_p[:, r, P:384], stat_p[:, r, 2, 1:2], None, ALU.mult)\
                   .then_inc(S("p_normed"), 1)

            for h in range(9):
                if h < 8:
                    prompt_max(h)
                if h >= 1:
                    prompt_norm(h - 1)
            for j in range(0, HT, 2):
                eng.wait_ge(S("p_out"), 2 * j + 4)
                eng.tensor_copy(q1[:, j:j + 2, 0:TP], ps[:, 4 + j // 2, :].rearrange("p (j t) -> p j t", j=2)).then_inc(S("attn_out"), 1)

            def sample_queries(p):
                r = p % 2
                if p >= 2:
                    eng.wait_ge(S("s_scores"), p - 1)
                for bb in range(2):
                    a = TP + NS * (2 * p + bb)
                    last = eng.tensor_tensor(qx[:, r, bb, :, :].rearrange("p j (h q) -> p j h q", h=8),
                                             q1[:, :, a:a + NS].unsqueeze(2).broadcast_to((P, HT, 8, NS)),
                                             const("head_rows").rearrange("p (j h) -> p j h", j=HT).unsqueeze(3).broadcast_to((P, HT, 8, NS)),
                                             ALU.mult)
                last.then_inc(S("qx_made"), 1)

            def sample_max(p):
                r = p % 2
                eng.wait_ge(S("s_scores"), p + 1)
                if p >= 2:
                    eng.wait_ge(S("s_turned"), 3 * (p - 1))
                eng.tensor_tensor(score_s[:, r, 0:FAR], ps[:, 0, 0:FAR], bias_s[:, 0:FAR], ALU.add)
                eng.tensor_tensor(score_s[:, r, FAR:OLD_KEYS], ps[:, 1, :], bias_s[:, FAR:OLD_KEYS], ALU.add)
                last = eng.tensor_tensor(score_s[:, r, OLD_KEYS:OLD_KEYS + TS], ps[:, 2, 0:TS],
                                         bias_s[:, OLD_KEYS + TS * p:OLD_KEYS + TS * p + TS], ALU.add)
                last.then_inc(S("s_biased"), 1)
                eng.wait_ge(S("s_biased"), p + 1)
                next_reads(eng, eng.tensor_reduce(stat_s[:, r, 0:1], score_s[:, r, :], AX, ALU.max))
                eng.tensor_scalar(stat_s[:, r, 1:2], stat_s[:, r, 0:1], -1.0, None, ALU.mult).then_inc(S("s_max"), 1)

            def sample_out(p):
                r = p % 2
                eng.wait_ge(S("s_exp"), p + 1)
                next_reads(eng, eng.reciprocal(stat_s[:, r, 3:4], stat_s[:, r, 2:3]))
                eng.wait_ge(S("s_values"), p + 1)
                eng.scalar_tensor_tensor(o_masked.rearrange("p (h e) -> p h e", h=8), ps[:, 3 + r, :].rearrange("p (h e) -> p h e", h=8),
                                         stat_s[:, r, 3:4], const("own_head").unsqueeze(2).broadcast_to((P, 8, 64)), ALU.mult, ALU.mult)\
                   .then_inc(S("s_masked"), 1)
                eng.wait_ge(S("s_out"), p + 1)
                eng.tensor_copy(q1[:, :, TP + 16 * p:TP + 16 * p + 16], ps[:, 5, 0:64].rearrange("p (j n) -> p j n", j=HT))\
                   .then_inc(S("attn_out"), 1)

            sample_queries(0)
            sample_queries(1)
            for p in range(5):
                if p < 4:
                    sample_max(p)
                    if p + 2 < 4:
                        sample_queries(p + 2)
                if p >= 1:
                    sample_out(p - 1)
            eng.wait_ge(S("y_hi"), 4)
            eng.tensor_tensor(h_lo[:, 4:8, :], q1, h_hi[:, 4:8, :], ALU.subtract).then_inc(S("y_lo"), 1)

        def mix1_pe(eng):
            norm_pe(eng, 2)
            eng.wait_ge(S("norm_lo"), 6)
            project_pe(eng, "in1", AT_IN1, IN1_CHUNKS)
            eng.wait_ge(S("in1_taken"), 2 * IN1_CHUNKS)
            eng.wait_ge(S("xc_made"), 1)
            for n in range(2):
                for j in range(HT):
                    eng.matmul(ps[:, HT * n + j, 0:T], lru_w[:, n, j, :], xc[:, j, :], start=True, stop=True).then_inc(S("lru_gate"), 1)
            eng.wait_ge(S("lru_sig"), 2 * HT)
            for i, (a, b) in enumerate(((0, 128), (128, 256), (256, 320))):
                for j in range(HT):
                    mm = eng.transpose(ps[0:b - a, 5 + i, P * j:P * j + P], v1[:, j, a:b], ident)
                mm.then_inc(S("v1_turned"), 1)

            def prompt_scores(h):
                o, j = 64 * (h % 2), h // 2
                if h >= 2:
                    eng.wait_ge(S("p_max"), h - 1)
                eng.matmul(ps[:, h % 2, 0:P], q1[o:o + 64, j, 0:P], k1[o:o + 64, j, 0:P], start=True, stop=True)
                eng.matmul(ps[:, h % 2, P:384], q1[o:o + 64, j, P:TP], k1[o:o + 64, j, 0:TP], start=True, stop=True).then_inc(S("p_scores"), 1)

            def prompt_turn(h):
                eng.wait_ge(S("p_normed"), h + 1)
                if h >= 2:
                    eng.wait_ge(S("p_tok_made"), h - 1)
                for i in range(3):
                    mm = eng.transpose(ps[:, 2 + h % 2, P * i:P * i + P], score_p[:, h % 2, P * i:P * i + P], ident)
                mm.then_inc(S("p_turned"), 1)

            def prompt_values(h):
                o, j = 64 * (h % 2), h // 2
                if h == 0:
                    eng.wait_ge(S("v1_tok_made"), 3)
                eng.wait_ge(S("p_tok_made"), h + 1)
                out, pt = ps[o:o + 64, 4 + j // 2, TP * (j % 2):TP * (j % 2) + TP], pt_p[h % 2]
                eng.matmul(out[:, 0:P], v1_tok[:, 0, 64 * h:64 * h + 64], pt[:, 0:P], start=True, stop=True)
                eng.matmul(out[:, P:TP], v1_tok[:, 0, 64 * h:64 * h + 64], pt[:, P:TP], start=True, stop=False)
                eng.matmul(out[:, P:TP], v1_tok[:, 1, 64 * h:64 * h + 64], pt[:, TP:384], start=False, stop=True).then_inc(S("p_out"), 1)

            for h in range(10):
                if h < 8:
                    prompt_scores(h)
                if 1 <= h < 9:
                    prompt_turn(h - 1)
                if h >= 2:
                    prompt_values(h - 2)

            def sample_scores(p):
                r = p % 2
                eng.wait_ge(S("qx_made"), p + 1)
                if p:
                    eng.wait_ge(S("s_biased"), p)
                for bb in range(2):
                    o = 64 * bb
                    for half in range(2):
                        keys = kv_ready(eng, "k", 2 * p + bb, half)
                        for j in range(HT):
                            mm = eng.matmul(ps[o:o + 64, half, 0:NEAR if half else FAR], qx[:, r, bb, j, :], keys[:, j, :], start=(j == 0), stop=(j == HT - 1))
                        mm.then_inc(S("kv_used"), 1)
                    for j in range(HT):
                        mm = eng.matmul(ps[o:o + 64, 2, 0:TS], qx[:, r, bb, j, :], k1[:, j, TP:T], start=(j == 0), stop=(j == HT - 1))
                mm.then_inc(S("s_scores"), 1)

            def sample_values(p):
                r = p % 2
                eng.wait_ge(S("s_exp"), p + 1)
                for n, (a, b, rows) in enumerate(((0, 2, P), (2, 6, P), (6, 7, 64))):
                    if 3 * p + n >= 2:
                        eng.wait_ge(S("s_tok_made"), 3 * p + (0, 0, 1)[n])
                    for i in range(a, b):
                        mm = eng.transpose(ps[0:rows, 6 + n % 2, P * (i - a):P * (i - a) + P], score_s[:, r, P * i:P * i + rows], ident)
                    mm.then_inc(S("s_turned"), 1)
                eng.wait_ge(S("s_tok_made"), 3 * p + 3)
                eng.wait_ge(S("pads_zeroed"), 1)
                if p >= 2:
                    eng.wait_ge(S("s_masked"), p - 1)
                for bb in range(2):
                    o = 64 * bb
                    for half in range(2):
                        values = kv_ready(eng, "v", 2 * p + bb, half)
                        for i in range(4 if half else 2):
                            mm = eng.matmul(ps[o:o + 64, 3 + r, :], pt_s[:, r, 2 * half + i, o:o + 64], values[:, i, :],
                                            start=(half == 0 and i == 0), stop=False)
                        mm.then_inc(S("kv_used"), 1)
                    mm = eng.matmul(ps[o:o + 64, 3 + r, :], pt_s[:, r, 6, o:o + 64], v1_tok[:, 2, :], start=False, stop=True)
                mm.then_inc(S("s_values"), 1)
                eng.wait_ge(S("s_masked"), p + 1)
                if p:
                    eng.wait_ge(S("attn_out"), 2 + p)
                for j in range(HT):
                    mm = eng.matmul(ps[:, 5, 16 * j:16 * j + 16], o_masked[:, P * j:P * j + P], const("same_query"), start=True, stop=True)
                mm.then_inc(S("s_out"), 1)

            eng.wait_ge(S("attn_out"), 2)
            for p in range(5):
                if p < 4:
                    sample_scores(p)
                if p >= 1:
                    sample_values(p - 1)
            eng.wait_ge(S("y_lo"), 3)
            eng.wait_ge(S("y_lo"), 4)
            project_pe(eng, "out1", AT_OUT1, OUT_CHUNKS)

        def mix1_pool(eng):
            eng.wait_ge(S("bias_loaded"), 64)
            for h in range(8):
                eng.tensor_tensor(bias_p[:, h, :], bias_p[:, h, :], count_p, ALU.add)
            eng.tensor_tensor(bias_s, bias_s, count_s, ALU.add).then_inc(S("biases_made"), 1)

        @block.sync
        def _(eng):
            eng.dma_start(xt[:, :, :], ins["x"]).then_inc(S("x_loaded"), 16)
            for to, name in ((consts[:, :], "consts"), (params[:, :], "params"), (router[:, :, :, :], "router"),
                             (shift0, "shift0"), (lora, "lora"), (sw, "sgu_w"), (sw8, "sgu_w8")):
                eng.dma_start(to, ins[name]).then_inc(S("small_loaded"), 16)
            eng.dma_start(sbias, ins["sgu_bias"].broadcast_to((P, HT, T))).then_inc(S("small_loaded"), 16)
            for c in range(RAW_RING):
                load_chunk(eng, c)
            eng.dma_start(swkv, ins["wkv0"]).then_inc(S("wkv0_loaded"), 16)
            for c in range(RAW_RING, AT_MOE0 + 6):
                load_chunk(eng, c)
            eng.wait_ge(S("out0_taken"), 1)
            eng.wait_ge(S("states_stored"), 32)
            for to, name in ((bias_p, "bias_prompt"), (bias_s, "bias_sample"), (count_p, "count_prompt"), (count_s, "count_sample")):
                eng.dma_start(to, ins[name]).then_inc(S("bias_loaded"), 16)
            for to, name in ((lru_w, "lru_gates"), (conv0, "conv0"), (lru0, "lru0")):
                eng.dma_start(to, ins[name]).then_inc(S("lru_loaded"), 16)
            for n in range(KV_RING):
                load_kv(eng, n)
            with eng.Fori(0, NE - 1) as it:
                for c in range(6, 12):
                    load_chunk(eng, AT_MOE0 + c, it)
            for c in range(AT_IN1, AT_OUT1 + RAW_RING):
                load_chunk(eng, c)
            for n in range(KV_RING, len(KV_UNITS)):
                load_kv(eng, n)
            for c in range(AT_OUT1 + RAW_RING, AT_MOE1 + 6):
                load_chunk(eng, c)
            with eng.Fori(0, NE - 1) as it:
                for c in range(6, 12):
                    load_chunk(eng, AT_MOE1 + c, it)
            for q in range(2):
                eng.wait_ge(S("norm_h"), 4 * KT + 4 * q + 4)
                eng.dma_start(outs["y"][:, 4 * q:4 * q + 4, :], h32[:, 4 * q:4 * q + 4, :]).then_inc(S("y_stored"), 16)
            eng.wait_ge(S("y_stored"), 32)

        @block.scalar
        def _(eng):
            mix0_act(eng)
            out_proj_act(eng, AT_OUT0)
            eng.wait_ge(S("out0_taken"), KT)
            moe_act(eng, 0, AT_MOE0)
            mix1_act(eng)
            out_proj_act(eng, AT_OUT1)
            eng.wait_ge(S("out1_taken"), KT)
            eng.wait_ge(S("rows_stored"), 64)
            moe_act(eng, 1, AT_MOE1)
            eng.wait_ge(S("down_added"), 4 * HT * NE)
            norm_act(eng, 4, False)

        @block.vector
        def _(eng):
            mix0_dve(eng)
            out_proj_dve(eng, "out0", AT_OUT0)
            moe_dve(eng, 0, AT_MOE0)
            mix1_dve(eng)
            out_proj_dve(eng, "out1", AT_OUT1)
            moe_dve(eng, 1, AT_MOE1)
            norm_dve(eng, 4, "norm_final", False)

        @block.tensor
        def _(eng):
            mix0_pe(eng)
            project_pe(eng, "out0", AT_OUT0, OUT_CHUNKS)
            moe_pe(eng, 0, AT_MOE0)
            mix1_pe(eng)
            moe_pe(eng, 1, AT_MOE1)
            norm_pe(eng, 4)

        @block.gpsimd
        def _(eng):
            mix0_pool(eng)
            eng.wait_ge(S("vn_made"), 1)
            eng.dma_start(outs["chunk_v"], gv[:, :, TP:T]).then_inc(S("chunk_v_stored"), 16)
            eng.wait_ge(S("shift_kept"), A_TILES)
            eng.dma_start(outs["shift"], shift_out).then_inc(S("shift_stored"), 16)
            wkv_group_pool(eng)
            eng.wait_ge(S("state_made"), 5)
            eng.dma_start(outs["wkv_p"], state[:, :, :]).then_inc(S("states_stored"), 16)
            eng.wait_ge(S("sample_state"), 8)
            eng.dma_start(outs["wkv_s"], swkv).then_inc(S("states_stored"), 16)
            mix1_pool(eng)
            eng.wait_ge(S("in1_taken"), 2 * IN1_CHUNKS)
            eng.dma_start(outs["key"], k1).then_inc(S("rows_stored"), 16)
            eng.dma_start(outs["value"], v1).then_inc(S("rows_stored"), 16)
            eng.wait_ge(S("xc_made"), 1)
            eng.dma_start(outs["conv"], conv_out).then_inc(S("rows_stored"), 16)
            eng.wait_ge(S("lru_kept"), 1)
            eng.dma_start(outs["lru"], lru_out).then_inc(S("rows_stored"), 16)
            eng.wait_ge(S("rows_stored"), 64)
            for name, n in (("chunk_v_stored", 16), ("shift_stored", 16), ("states_stored", 32)):
                eng.wait_ge(S(name), n)


def lay_consts():
    import numpy as np

    c = np.zeros((P, NCONST), np.float32)

    def put(name, a):
        at, n = CCOL[name]
        c[:a.shape[0], at:at + n] = a

    i, j = np.arange(64)[:, None], np.arange(64)[None, :]
    twice = lambda a: np.concatenate([a, a], 0).astype(np.float32)
    block = lambda n: (i // n) == (j // n)
    put("ident", np.eye(P))
    put("ones", np.ones((P, P)))
    put("head_ones", np.kron(np.eye(2), np.ones((64, 64))))
    t = np.arange(T)
    starts = np.where(t < TP, t % C == 0, (t - TP) % NS == 0)
    put("reset", np.broadcast_to(1.0 - starts, (P, T)))
    put("mask_prompt", twice(np.concatenate([i < j, i <= j], 1)))
    put("mask_sample", twice(np.concatenate([(i < j) & block(8), (i <= j) & block(8)], 1)))
    put("diag8", twice((i < j) & block(8)))
    put("low8", twice((i > j) & block(8)))
    put("low16", twice((i > j) & block(16) & ~block(8)))
    put("low32", twice((i > j) & block(32) & ~block(16)))
    put("low64", twice((i > j) & ~block(32)))
    put("eye64", twice(i == j))
    put("own_batch", (np.arange(TS)[:, None] // NS == np.arange(NB)[None]).astype(np.float32))
    ii, jj = np.arange(P)[:, None], np.arange(P)[None]
    put("tri", (ii <= jj).astype(np.float32))
    put("first", np.broadcast_to(np.concatenate([4.0 - np.arange(4), 16.0 - np.arange(16)]), (P, 20)))
    r = np.arange(P)
    put("same_query", ((r // 64)[:, None] == np.arange(16)[None] // 8) & ((r % 8)[:, None] == np.arange(16)[None] % 8))
    put("own_head", ((r % 64) // 8)[:, None] == np.arange(8)[None])
    put("head_rows", ((r // 64)[:, None] + 2 * (np.arange(32) // 8)[None]) == (np.arange(32) % 8)[None])
    return c


def multiplicity(dist):
    import numpy as np

    n = sum(((dist >= 0) & (dist <= w) & (dist % d == 0)).astype(np.int64) for w, d in ((128, 1), (512, 4), (2048, 16)))
    return np.where(n > 0, np.log(np.maximum(n, 1)), NEG).astype(np.float32)


def bucket(dist):
    import numpy as np

    scaled = np.log(np.maximum(dist, 1) / 16) / np.log(2048 / 16)
    large = np.minimum(16 + (scaled * 16).astype(np.int32), 31)
    return np.where(dist < 16, dist, large).astype(np.int32)


def lay_out(inputs):
    import numpy as np

    g = {k: np.asarray(v) for k, v in inputs.items()}
    col = lambda v: v.reshape(-1, P).T
    stack = lambda w: w.reshape(-1, P, w.shape[1]).transpose(1, 0, 2)
    a = {}
    x = np.concatenate([g["x_prompt"].reshape(TP, D), g["x_sample"].reshape(TS, D)], 0)
    a["x"] = x.T.reshape(KT, P, T).transpose(1, 0, 2)
    stream = np.empty((STREAM, P, CHUNK_ELEMS), np.float32)

    def place(at, w, tiles):
        k, m = w.shape[0] // P, w.shape[1] // P
        stream[at:at + m // tiles] = w.reshape(k, P, m // tiles, tiles, P).transpose(2, 1, 3, 0, 4).reshape(-1, P, CHUNK_ELEMS)

    place(AT_IN0, g["w_in_even"][0], 2)
    place(AT_OUT0, g["w_out_even"][0], 2)
    place(AT_IN1, g["w_in_odd"][0], 2)
    place(AT_OUT1, g["w_out_odd"][0], 2)
    for layer, at in enumerate((AT_MOE0, AT_MOE1)):
        for e in range(NE):
            b = at + EXPERT_CHUNKS * e - (2 if e else 0)
            place(b, g["exp_w_gate"][layer, e], 2)
            place(b + (4 if e else 2), g["exp_w_up"][layer, e], 2)
            place(at + MOE_CHUNKS - 2 if e == NE - 1 else at + EXPERT_CHUNKS * (e + 1), g["exp_w_down"][layer, e], 4)
    a["stream"] = stream
    p = np.zeros((P, NPARAM), np.float32)

    def put(name, v):
        at, n = PCOL[name]
        p[:v.shape[0], at:at + n] = v

    for l in range(2):
        put(f"norm_mix{l}", col(g["norm_mix"][l]))
        put(f"norm_ffn{l}", col(g["norm_ffn"][l]))
        put(f"router_b{l}", np.concatenate([g["router_group_b"][l], g["router_expert_b"][l]])[:, None])
    put("norm_final", col(g["norm_final"]))
    for name, key in (("shift_mu", "shift_mu"), ("decay_w0", "decay_w0"), ("iclr_a0", "iclr_a0"), ("key_k", "key_k"),
                      ("key_a", "key_a"), ("bonus", "bonus_r_k"), ("lnx_g", "lnx_g"), ("lnx_b", "lnx_b"),
                      ("sgu_g", "sgu_norm_g"), ("sgu_b", "sgu_norm_b"), ("conv_b", "conv_b"), ("rgate_b", "rgate_b"),
                      ("igate_b", "igate_b"), ("lambda", "lru_lambda")):
        put(name, col(g[key][0].reshape(-1)))
    put("conv_w", np.concatenate([col(g["conv_w"][0, i]) for i in range(4)], 1))
    a["params"] = p
    a["consts"] = lay_consts()
    a["router"] = np.stack([stack(np.concatenate([g["router_group_w"][l], g["router_expert_w"][l]], 1)) for l in range(2)], 1)
    a["shift0"] = g["state_shift"][0].T.reshape(A_TILES, P, NB).transpose(1, 0, 2)
    a["lora"] = np.stack([np.concatenate([g["decay_up"][0], g["iclr_up"][0]], 0), g["gate_up"][0]], 1)
    a["wkv0"] = g["state_wkv"][0].reshape(NB, HT, 2, 64, 64).transpose(2, 4, 1, 0, 3).reshape(P, HT, NB, 64)
    a["sgu_w"] = g["sgu_w"][0].transpose(2, 0, 1)
    a["sgu_w8"] = np.tile(g["sgu_w"][0][:, :NS, :NS].transpose(2, 0, 1), (NB, 1, NB))
    a["sgu_bias"] = np.concatenate([np.tile(g["sgu_b"][0], (1, 2)), np.tile(g["sgu_b"][0][:, :NS], (1, NB))], 1)[None]
    a["conv0"] = g["state_conv"][0].transpose(2, 0, 1).reshape(HT, P, NB, 3).transpose(1, 0, 2, 3)
    a["lru0"] = g["state_rglru"][0].T.reshape(HT, P, NB).transpose(1, 0, 2)
    gate = np.zeros((P, 2, HT, P), np.float32)
    for n, key in enumerate(("rgate_w", "igate_w")):
        for h in range(8):
            o = 64 * (h % 2)
            gate[o:o + 64, n, h // 2, o:o + 64] = g[key][0, h]
    a["lru_gates"] = gate
    q, k = np.arange(TP)[:, None], np.arange(TP)[None]
    rel = g["rel_bias"]
    full = rel[bucket(np.maximum(q - k, 0))]
    full = full.reshape(2, P, TP, 8).transpose(1, 3, 0, 2)
    a["bias_prompt"] = np.concatenate([full[:, :, 0, :P], full[:, :, 1]], 2)
    m = multiplicity(q - k).reshape(2, P, TP).transpose(1, 0, 2)
    a["count_prompt"] = np.concatenate([m[:, 0, :P], m[:, 1]], 1)
    s = np.tile(np.arange(NS), 16)[:, None]
    head = ((r := np.arange(P)) % 64 // 8)[:, None]
    far = np.arange(PAST - NEAR).reshape(-1, 16)[:, :8].reshape(-1)
    old = np.concatenate([far, np.arange(PAST - NEAR, PAST)])
    dist = np.concatenate([PAST + s - old[None], np.tile(s - np.arange(TS)[None] % NS, (1, 4))], 1)
    a["bias_sample"] = rel[bucket(np.maximum(dist, 0)), head]
    own = np.concatenate([np.arange(TS)[None] // NS == 2 * p + (r // 64)[:, None] for p in range(4)], 1)
    a["count_sample"] = multiplicity(np.where(np.concatenate([np.ones((P, OLD_KEYS), bool), own], 1), dist, -1))
    for name, rows in (("far", far), ("near", old[FAR:])):
        n = len(rows)
        a[f"k_{name}"] = g["cache_k"][0][:, rows].reshape(NB, n, HT, 2, 64).transpose(0, 3, 4, 2, 1).reshape(NB, P, HT * n)
        a[f"v_{name}"] = g["cache_v"][0][:, rows].reshape(NB, n // P, P, 512).transpose(0, 2, 1, 3).reshape(NB, P, n // P * 512)
    return {n: np.ascontiguousarray(v) for n, v in a.items()}


OUTS = {"y": (P, KT, T), "shift": (P, A_TILES, 9), "wkv_p": (P, HT, 64), "wkv_s": (P, HT, NB, 64), "chunk_v": (P, HT, TS),
        "conv": (P, HT, 27), "lru": (P, HT, 9), "key": (P, HT, T), "value": (P, HT, T)}


def gather(o):
    rows = lambda v: v.transpose(2, 1, 0).reshape(v.shape[2], -1)
    y, k, v = rows(o["y"]), rows(o["key"]), rows(o["value"])
    shift, lru = rows(o["shift"]), rows(o["lru"])
    conv = rows(o["conv"])
    wkv_p = o["wkv_p"].reshape(2, 64, HT, 64).transpose(2, 0, 3, 1).reshape(1, 1, 8, 64, 64)
    wkv_s = o["wkv_s"].reshape(2, 64, HT, NB, 64).transpose(3, 2, 0, 4, 1).reshape(1, NB, 8, 64, 64)
    return (y[None, :TP], y[TP:].reshape(NB, NS, D), wkv_p, shift[None, :1], conv[None, None, :3], lru[None, :1],
            k[:TP].reshape(1, 1, TP, 8, 64), v[:TP].reshape(1, 1, TP, 8, 64),
            wkv_s, shift[None, 1:], rows(o["chunk_v"]).reshape(1, NB, NS, 512), conv[3:].reshape(1, NB, 3, 512),
            lru[None, 1:], k[TP:].reshape(1, NB, NS, 8, 64), v[TP:].reshape(1, NB, NS, 8, 64))


def kernel(**inputs):
    import numpy as np
    import concourse.bacc as bacc
    from concourse.bass_utils import run_bass_kernel_spmd

    nc = bacc.Bacc("TRN2", target_bir_lowering=False, num_devices=1)
    arrays = {f"in_{n}": v for n, v in lay_out(inputs).items()}
    ins = {n[3:]: nc.dram_tensor(n, v.shape, F32, kind="ExternalInput").ap() for n, v in arrays.items()}
    outs = {n: nc.dram_tensor(f"out_{n}", s, F32, kind="ExternalOutput").ap() for n, s in OUTS.items()}
    decoder_layers(nc, ins, outs)
    r = run_bass_kernel_spmd(nc, [arrays], core_ids=[0])
    return tuple(np.ascontiguousarray(v) for v in gather({n: r.results[0][f"out_{n}"] for n in OUTS}))
```
